# Optimizing a Trainium2 kernel written in Bass

```python
import math
import jax, jax.numpy as jnp
from jax import lax
import numpy as np

D_MODEL = 1024
BATCH = 1
SEQ = 512
DEPTH = 2

N_MIXERS = 2
N_LAYERS_A = (DEPTH + 1) // 2
N_LAYERS_B = DEPTH // 2

MEM_LEN = 256
MEM_HEADS = 4
MEM_HEAD_DIM = 64
MEM_WIDTH = MEM_HEADS * MEM_HEAD_DIM
TOK_WIDTH = D_MODEL - MEM_WIDTH

RNN_WIDTH = TOK_WIDTH
RNN_BLOCKS = 8
RNN_BLOCK_DIM = RNN_WIDTH // RNN_BLOCKS
CONV_WIDTH = 4
LRU_C = 8.0

DIFF_HEADS = 6
DIFF_QK_DIM = 64
DIFF_V_DIM = 2 * DIFF_QK_DIM
DIFF_QK_WIDTH = DIFF_HEADS * 2 * DIFF_QK_DIM
DIFF_V_WIDTH = DIFF_HEADS * DIFF_V_DIM
Q_BLOCK = 128

REL_BUCKETS = 32
REL_MAX_EXACT = 16
REL_MAX_DIST = 128

N_GROUPS = 4
EXPERTS_PER_GROUP = 4
N_EXPERTS = N_GROUPS * EXPERTS_PER_GROUP
TOP_K_INNER = 2
D_EXPERT = D_MODEL // 4

IN_A = 2 * RNN_WIDTH + MEM_WIDTH
IN_B = 2 * DIFF_QK_WIDTH + DIFF_V_WIDTH + MEM_WIDTH
EPS = 1e-6

kernel_name = "hybrid_rglru_diffattn_hiermoe"

def rmsnorm(x, g):
    x32 = x.astype(jnp.float32)
    y = x32 * lax.rsqrt(jnp.mean(x32 * x32, axis=-1, keepdims=True) + EPS) * g.astype(jnp.float32)
    return y.astype(x.dtype)

def t5_bucket(q_pos, k_pos):
    n = jnp.maximum(q_pos[:, None] - k_pos[None, :], 0)
    nf = jnp.maximum(n, 1).astype(jnp.float32)
    large = REL_MAX_EXACT + (jnp.log(nf / REL_MAX_EXACT) / math.log(REL_MAX_DIST / REL_MAX_EXACT)
                             * (REL_BUCKETS - REL_MAX_EXACT)).astype(jnp.int32)
    large = jnp.minimum(large, REL_BUCKETS - 1)
    return jnp.where(n < REL_MAX_EXACT, n, large)

def _lin_combine(c1, c2):
    a1, b1 = c1
    a2, b2 = c2
    return a1 * a2, a2 * b1 + b2

def rglru_mixer(u_x, u_gate, conv_w, conv_b, wa, ba, wx, bx, lam):
    B, S, C = u_x.shape
    xc = lax.conv_general_dilated(
        u_x, conv_w[:, None, :], window_strides=(1,), padding=[(CONV_WIDTH - 1, 0)],
        dimension_numbers=('NWC', 'WIO', 'NWC'), feature_group_count=C) + conv_b
    xb = xc.reshape(B, S, RNN_BLOCKS, RNN_BLOCK_DIM)
    r = jax.nn.sigmoid((jnp.einsum('bsgi,gij->bsgj', xb, wa).reshape(B, S, C) + ba).astype(jnp.float32))
    ig = jax.nn.sigmoid((jnp.einsum('bsgi,gij->bsgj', xb, wx).reshape(B, S, C) + bx).astype(jnp.float32))
    log_a = -LRU_C * r * jax.nn.softplus(-lam.astype(jnp.float32))
    a = jnp.exp(log_a)
    b = jnp.sqrt(-jnp.expm1(2.0 * log_a)) * (ig * xc.astype(jnp.float32))
    _, h = lax.associative_scan(_lin_combine, (a, b), axis=1)
    return (h * jax.nn.gelu(u_gate.astype(jnp.float32))).astype(u_x.dtype)

def diff_attention(q, k, v, lq1, lk1, lq2, lk2, subln_g, rel_bias, lambda_init):
    B, S, _ = q.shape
    qh = q.reshape(B, S, DIFF_HEADS, 2, DIFF_QK_DIM).transpose(3, 0, 2, 1, 4)
    kh = k.reshape(B, S, DIFF_HEADS, 2, DIFF_QK_DIM).transpose(3, 0, 2, 1, 4)
    vh = v.reshape(B, S, DIFF_HEADS, DIFF_V_DIM).transpose(0, 2, 1, 3)
    f32 = jnp.float32
    lam = (jnp.exp(jnp.sum(lq1.astype(f32) * lk1.astype(f32)))
           - jnp.exp(jnp.sum(lq2.astype(f32) * lk2.astype(f32))) + lambda_init)
    scale = DIFF_QK_DIM ** -0.5
    outs = []
    for blk in range(S // Q_BLOCK):
        start = blk * Q_BLOCK
        end = start + Q_BLOCK
        qb = qh[:, :, :, start:end]
        kb = kh[:, :, :, :end]
        s = jnp.einsum('nbhqd,nbhkd->nbhqk', qb, kb).astype(f32) * scale
        q_pos = jnp.arange(start, end)
        k_pos = jnp.arange(end)
        bias = rel_bias[t5_bucket(q_pos, k_pos)].astype(f32).transpose(2, 0, 1)
        s = jnp.where(k_pos[None, :] <= q_pos[:, None], s + bias, -jnp.inf)
        p = jax.nn.softmax(s, axis=-1)
        o = jnp.einsum('bhqk,bhkd->bhqd', p[0] - lam * p[1], vh[:, :, :end].astype(f32))
        outs.append(o)
    o = jnp.concatenate(outs, axis=2)
    o = rmsnorm(o, subln_g) * (1.0 - lambda_init)
    return o.transpose(0, 2, 1, 3).reshape(B, S, DIFF_V_WIDTH).astype(q.dtype)

def memory_attention(q_mem, mem_k, mem_v):
    B, S, _ = q_mem.shape
    qh = q_mem.reshape(B, S, MEM_HEADS, MEM_HEAD_DIM)
    s = jnp.einsum('bshd,bmhd->bhsm', qh, mem_k).astype(jnp.float32) * (MEM_HEAD_DIM ** -0.5)
    p = jax.nn.softmax(s, axis=-1)
    o = jnp.einsum('bhsm,bmhd->bshd', p, mem_v.astype(jnp.float32))
    return o.reshape(B, S, MEM_WIDTH).astype(q_mem.dtype)

def hier_moe(h, w_group, w_router, w1, w3, w2):
    B, S, D = h.shape
    t = h.reshape(B * S, D)
    g_logits = (t @ w_group).astype(jnp.float32)
    g_prob = jax.nn.softmax(g_logits, axis=-1)
    g_idx = jnp.argmax(g_logits, axis=-1)
    g_w = jnp.take_along_axis(g_prob, g_idx[:, None], axis=1)
    e_logits = (t @ w_router).astype(jnp.float32).reshape(-1, N_GROUPS, EXPERTS_PER_GROUP)
    e_in = jnp.take_along_axis(e_logits, g_idx[:, None, None], axis=1)[:, 0]
    top_v, top_i = lax.top_k(e_in, TOP_K_INNER)
    w = jax.nn.softmax(top_v, axis=-1) * g_w
    eid = g_idx[:, None] * EXPERTS_PER_GROUP + top_i
    gates = jnp.sum(jax.nn.one_hot(eid, N_EXPERTS, dtype=jnp.float32) * w[..., None], axis=1)
    a = jnp.einsum('td,edf->tef', t, w1)
    u = jnp.einsum('td,edf->tef', t, w3)
    hid = jax.nn.silu(a) * u * gates[:, :, None].astype(t.dtype)
    y = jnp.einsum('tef,efd->td', hid, w2)
    return y.reshape(B, S, D)

def setup_inputs(seed: int = 0) -> dict:
    key = jax.random.key(seed)
    ks = jax.random.split(key, 32)
    nrm = jax.random.normal
    f32 = jnp.float32
    u = jax.random.uniform(ks[12], (N_LAYERS_A, RNN_WIDTH), f32, minval=0.9, maxval=0.999)
    a0 = u ** (1.0 / LRU_C)
    lru_lambda = jnp.log(a0) - jnp.log1p(-a0)
    return {
        "x": nrm(ks[0], (BATCH, SEQ, D_MODEL), f32),
        "mem": nrm(ks[1], (BATCH, MEM_LEN, D_MODEL), f32),
        "norm_mix_g": 1.0 + 0.05 * nrm(ks[2], (DEPTH, D_MODEL), f32),
        "w_in_a": nrm(ks[3], (N_LAYERS_A, D_MODEL, IN_A), f32) * D_MODEL ** -0.5,
        "w_in_b": nrm(ks[4], (N_LAYERS_B, D_MODEL, IN_B), f32) * D_MODEL ** -0.5,
        "w_out": nrm(ks[5], (DEPTH, D_MODEL, D_MODEL), f32) * D_MODEL ** -0.5,
        "conv_w": nrm(ks[6], (N_LAYERS_A, CONV_WIDTH, RNN_WIDTH), f32) * CONV_WIDTH ** -0.5,
        "conv_b": 0.01 * nrm(ks[7], (N_LAYERS_A, RNN_WIDTH), f32),
        "gate_a_w": nrm(ks[8], (N_LAYERS_A, RNN_BLOCKS, RNN_BLOCK_DIM, RNN_BLOCK_DIM), f32) * RNN_BLOCK_DIM ** -0.5,
        "gate_a_b": 0.01 * nrm(ks[9], (N_LAYERS_A, RNN_WIDTH), f32),
        "gate_x_w": nrm(ks[10], (N_LAYERS_A, RNN_BLOCKS, RNN_BLOCK_DIM, RNN_BLOCK_DIM), f32) * RNN_BLOCK_DIM ** -0.5,
        "gate_x_b": 0.01 * nrm(ks[11], (N_LAYERS_A, RNN_WIDTH), f32),
        "lru_lambda": lru_lambda,
        "diff_lq1": 0.1 * nrm(ks[13], (N_LAYERS_B, DIFF_QK_DIM), f32),
        "diff_lk1": 0.1 * nrm(ks[14], (N_LAYERS_B, DIFF_QK_DIM), f32),
        "diff_lq2": 0.1 * nrm(ks[15], (N_LAYERS_B, DIFF_QK_DIM), f32),
        "diff_lk2": 0.1 * nrm(ks[16], (N_LAYERS_B, DIFF_QK_DIM), f32),
        "diff_subln_g": 1.0 + 0.05 * nrm(ks[17], (N_LAYERS_B, DIFF_V_DIM), f32),
        "rel_bias": 0.5 * nrm(ks[18], (REL_BUCKETS, DIFF_HEADS), f32),
        "mem_norm_g": 1.0 + 0.05 * nrm(ks[19], (D_MODEL,), f32),
        "w_mem_kv": nrm(ks[20], (DEPTH, D_MODEL, 2 * MEM_WIDTH), f32) * D_MODEL ** -0.5,
        "norm_ffn_g": 1.0 + 0.05 * nrm(ks[21], (DEPTH, D_MODEL), f32),
        "w_group": nrm(ks[22], (DEPTH, D_MODEL, N_GROUPS), f32) * D_MODEL ** -0.5,
        "w_router": nrm(ks[23], (DEPTH, D_MODEL, N_EXPERTS), f32) * D_MODEL ** -0.5,
        "w_exp1": nrm(ks[24], (DEPTH, N_EXPERTS, D_MODEL, D_EXPERT), f32) * D_MODEL ** -0.5,
        "w_exp3": nrm(ks[25], (DEPTH, N_EXPERTS, D_MODEL, D_EXPERT), f32) * D_MODEL ** -0.5,
        "w_exp2": nrm(ks[26], (DEPTH, N_EXPERTS, D_EXPERT, D_MODEL), f32) * D_EXPERT ** -0.5,
        "final_norm_g": 1.0 + 0.05 * nrm(ks[27], (D_MODEL,), f32),
    }

def reference(x, mem, norm_mix_g, w_in_a, w_in_b, w_out, conv_w, conv_b, gate_a_w, gate_a_b,
              gate_x_w, gate_x_b, lru_lambda, diff_lq1, diff_lk1, diff_lq2, diff_lk2, diff_subln_g,
              rel_bias, mem_norm_g, w_mem_kv, norm_ffn_g, w_group, w_router, w_exp1, w_exp3,
              w_exp2, final_norm_g):
    B = x.shape[0]
    mem_n = rmsnorm(mem, mem_norm_g)
    h = x
    for i in range(DEPTH):
        j = i // N_MIXERS
        hn = rmsnorm(h, norm_mix_g[i])
        kv = (mem_n @ w_mem_kv[i]).reshape(B, MEM_LEN, 2, MEM_HEADS, MEM_HEAD_DIM)
        if i % N_MIXERS == 0:
            proj = hn @ w_in_a[j]
            u_x, u_g, q_mem = jnp.split(proj, [RNN_WIDTH, 2 * RNN_WIDTH], axis=-1)
            tok = rglru_mixer(u_x, u_g, conv_w[j], conv_b[j], gate_a_w[j], gate_a_b[j],
                              gate_x_w[j], gate_x_b[j], lru_lambda[j])
        else:
            proj = hn @ w_in_b[j]
            q, k, v, q_mem = jnp.split(
                proj, [DIFF_QK_WIDTH, 2 * DIFF_QK_WIDTH, 2 * DIFF_QK_WIDTH + DIFF_V_WIDTH], axis=-1)
            lambda_init = 0.8 - 0.6 * math.exp(-0.3 * i)
            tok = diff_attention(q, k, v, diff_lq1[j], diff_lk1[j], diff_lq2[j], diff_lk2[j],
                                 diff_subln_g[j], rel_bias, lambda_init)
        mo = memory_attention(q_mem, kv[:, :, 0], kv[:, :, 1])
        h = h + jnp.concatenate([tok, mo], axis=-1) @ w_out[i]
        h = h + hier_moe(rmsnorm(h, norm_ffn_g[i]), w_group[i], w_router[i],
                         w_exp1[i], w_exp3[i], w_exp2[i])
    return rmsnorm(h, final_norm_g)


_drawn_inputs = setup_inputs


def setup_inputs(seed=0):
    import zlib

    import numpy as np

    out = dict(_drawn_inputs(seed))
    spreads = {}
    factors = {'gate_a_b': 19.515, 'gate_x_b': 11.602, 'mem_norm_g': 2.817}
    for name, (base, spread) in spreads.items():
        noise = np.random.default_rng([zlib.crc32(name.encode()), seed]).standard_normal(out[name].shape)
        drawn = base * np.exp(spread * noise) if base else spread * noise
        out[name] = __import__('jax').numpy.asarray(drawn.astype(out[name].dtype))
    for name, factor in factors.items():
        out[name] = (out[name] * factor).astype(out[name].dtype)
    return out
```

```python
import math
from contextlib import ExitStack

import concourse.bass as bass
from concourse import mybir

F32 = mybir.dt.float32
F16 = mybir.dt.float16
I32 = mybir.dt.int32
ALU = mybir.AluOpType
ACT = mybir.ActivationFunctionType
AXX = mybir.AxisListType.X

P = 128
D = 1024
T = 512
NT = T // P
KC = D // P
MEM = 256
MT = MEM // P
DH = 64
RB, RW = 8, 96
CONV = 4
HEADS = 6
NG, EPG = 4, 4
NE = NG * EPG
DE = 256
EPS = 1e-6
REL = 32
NEAR = 2 * P
REVLEN = 384
UNIT = KC * 256
RING = 6
MORE = 2 * T // P - 1
UPW = KC * 2 * DE
EXPW = UPW + 2 * D
LAMBDA_INIT = 0.8 - 0.6 * math.exp(-0.3)
GELU_C = math.sqrt(2.0 / math.pi)
NEG = -1.0e30

KV0, INA, QMA, OUTA = 0, 2, 10, 11
KV1 = OUTA + 5
INB = KV1 + 2
QMB = INB + 9
OUTB = QMB + 1
UNITS = OUTB + 4


def vec_columns():
    at, out = 0, {}
    for name, n in (("mix0", KC), ("mix1", KC), ("ffn0", KC), ("ffn1", KC), ("mem", KC),
                    ("subln", 1), ("conv_w", RB * CONV), ("conv_b", RB), ("gate_a_b", RB),
                    ("gate_x_b", RB), ("lam", RB)):
        out[name] = (at, at + n)
        at += n
    return out, at


VEC, NVEC = vec_columns()


def build(nc, x, mem, units, experts, gate_w, vecs, router, diff_l, rel_bias, final_g, onehot, out):
    ctx = ExitStack()
    with ctx:
        def sb(name, shape, dt=F32):
            return ctx.enter_context(nc.sbuf_tensor(name, shape, dt))

        def sem(name):
            return ctx.enter_context(nc.semaphore(name))

        h = sb("h", [P, NT, D])
        xs_all = sb("xs_all", [P, 10 * T])
        xs = xs_all[:, 0:NT * D].rearrange("p (t d) -> p t d", t=NT)
        cat = xs_all[:, :].rearrange("p (c t) -> p c t", t=T)
        hnT = sb("hnT", [P, KC, T])
        memT = sb("memT", [P, KC, MEM])
        ring = sb("ring", [P, RING, UNIT])
        expw = sb("expw", [P, 2, EXPW])
        w_up = [expw[:, s, 0:UPW] for s in range(2)]
        w_down = [expw[:, s, UPW:EXPW] for s in range(2)]
        wgr = sb("wgr", [P, 2, KC, NG + NE])
        arena = sb("arena", [P, 9 * D])
        kvq = sb("kvq", [P, 2 * D])
        kTm = kvq[:, 0:512].rearrange("p (c m) -> p c m", c=2)
        vm = kvq[:, 512:1024].rearrange("p (c m) -> p c m", c=MT)
        qmT = kvq[:, 1024:2048].rearrange("p (c t) -> p c t", c=2)
        ident = sb("ident", [P, P])
        iota = sb("iota", [P, P])
        before = sb("before", [P, P])
        ones = sb("ones", [P, P])
        vec = sb("vec", [P, NVEC])
        small = sb("small", [P, 820])

        def v(name, lo=0, hi=None):
            a, b = VEC[name]
            return vec[:, a + lo:(b if hi is None else a + hi)]

        taken = [0]

        def sm(*shape, dt=None):
            n = 1
            for s in shape:
                n *= s
            a = taken[0]
            taken[0] += n
            assert taken[0] <= 820
            t = small[:, a:a + n]
            if dt is not None:
                t = t.bitcast(dt)
            if len(shape) == 2:
                t = t.rearrange("p (a b) -> p a b", a=shape[0])
            if len(shape) == 3:
                t = t.rearrange("p (a b c) -> p a b c", a=shape[0], b=shape[1])
            return t

        ssq, msq, rstd, mhalf = sm(NT), sm(NT), sm(NT), sm(8)
        mx, nmx, rsum, rec = sm(2, 2), sm(2, 2), sm(2, 2), sm(2, 2)
        lprod, lsum, lexp, neglam = sm(2, DH), sm(2), sm(2), sm(1)
        ossq, orstd, gsub = sm(HEADS), sm(HEADS), sm(1)
        c31 = sm(HEADS)
        iota4, iota16, row16, jcol = sm(4), sm(NE), sm(NE), sm(NE, 3)
        wv1, wv2 = sm(NT), sm(NT)
        r1i, r2i = sm(NT, dt=I32), sm(NT, dt=I32)
        idxi = sm(NE, dt=I32)
        vcount, vsteer = sm(1, dt=I32), sm(1, dt=I32)
        vidx, vc = sm(NE, 3), sm(1)
        rk = sm(NT, NE)
        ntot = sm(NE)
        ovi = sm(1, dt=I32)
        hba, hbx, spl, sp8 = sm(RB), sm(RB), sm(RB), sm(RB)
        tokid = sb("tokid", [P, NT], F16)

        upad = arena[0:RW, 0:2 * 515].rearrange("p (s n) -> p s n", s=2)
        def ab(i, n=1):
            a = 1040 + 512 * i
            return arena[0:RW, a:a + 512 * n]
        xc = [ab(0), ab(1)]
        ta, tx, sq, dd, ra, hh, gg, gq = (ab(i) for i in range(2, 10))
        gw = arena[0:RW, 1040 + 5120:1040 + 5120 + 2 * RB * RW].rearrange("p (s g j) -> p s g j", s=2, g=RB)
        qT = arena[:, 0:3072].rearrange("p (c t) -> p c t", c=HEADS)
        kT = arena[:, 3072:6144].rearrange("p (c t) -> p c t", c=HEADS)
        vB = arena[:, 6144:9216].rearrange("p (t c) -> p t c", t=NT)
        bias = memT[:, :, :].rearrange("p k m -> p (k m)")[:, 0:HEADS * NEAR].rearrange("p (h n) -> p h n", h=HEADS)
        hflat = hnT[:, :, :].rearrange("p k t -> p (k t)")
        E = [hflat[:, s * 1024:(s + 1) * 1024].rearrange("p (n k) -> p n k", n=2) for s in range(2)]
        PTs = [hflat[:, 2048 + s * 512:2560 + s * 512].rearrange("p (c q) -> p c q", c=4) for s in range(2)]
        Osb = hflat[:, 3072:3840].rearrange("p (h d) -> p h d", h=HEADS)
        gfin = hflat[:, 0:D]
        xg = [arena[:, s * D:(s + 1) * D] for s in range(2)]
        xgT = [arena[:, (2 + s) * D:(3 + s) * D].rearrange("p (k t) -> p k t", k=KC) for s in range(2)]
        ysb = [arena[:, (4 + s) * D:(5 + s) * D] for s in range(2)]
        hid = [arena[:, 6144 + s * 256:6400 + s * 256] for s in range(2)]
        tnh = [arena[:, 6656 + s * 256:6912 + s * 256] for s in range(2)]
        hidT = [arena[:, 7168 + s * 256:7424 + s * 256].rearrange("p (f t) -> p f t", f=2) for s in range(2)]
        onesl = [arena[:, 7680 + s * 256:7936 + s * 256].bitcast(F16).rearrange("p (c t) -> p c t", c=NT) for s in range(2)]
        rsc = arena[:, 8192:9216]
        comb = [[arena[:, (2 * s + r) * D:(2 * s + r + 1) * D] for r in range(2)] for s in range(2)]
        lall = arena[:, 6144:6400]
        relsb = arena[0:REL, 6400:6406]
        hotsb = arena[0:REL, 6408:6792]
        relrep = arena[0:REL, 6792:7560].rearrange("p (h m) -> p h m", h=HEADS)
        relrows = arena[:, 7560:8328].rearrange("p (s m) -> p s m", s=2)
        On = xs_all[:, 8 * T:8 * T + HEADS * P].rearrange("p (h d) -> p h d", h=HEADS)

        scr = [0]

        def rt(*shape):
            n = 1
            for k in shape:
                n *= k
            a = scr[0]
            scr[0] += n
            assert scr[0] <= D
            t = rsc[:, a:a + n]
            if len(shape) == 2:
                t = t.rearrange("p (a b) -> p a b", a=shape[0])
            if len(shape) == 3:
                t = t.rearrange("p (a b c) -> p a b c", a=shape[0], b=shape[1])
            return t

        lg = rt(NT, NG + NE)
        r_gmax, r_gi, r_gsum, r_gw, r_m1, r_m2, r_ji, r_den = (rt(NT) for _ in range(8))
        rdiff = rt(NT)
        r_eqg, ohg, rg_e, e_in, r_eqe, oh1, oh2 = (rt(NT, 4) for _ in range(7))
        r_prod = rt(NT, NG, EPG)
        ohe1, ohe2, sel, r_rankv, r_slot, r_cnt = (rt(NT, NE) for _ in range(6))
        r_off, r_base = rt(NT, NE), rt(NE)
        r_over, r_cum = rt(NE, 3), rt(NE, 3)
        r_r1, r_r2 = rt(NT), rt(NT)
        v_m, v_eoh, v_jv, v_rr, v_rk, v_t16, v_es = rt(NE, 3), rt(NE), rt(1), rt(NT, NE), rt(NT), rt(NE), rt(1)

        ps = ctx.enter_context(nc.psum_tensor("ps", [P, 8, 512], F32))

        def bank(i):
            return ps[:, i, :]

        xs_d = nc.dram_tensor("xs_rows", [T, D], F32).ap()
        y_d = nc.dram_tensor("expert_rows", [(NE + MORE) * P, D], F32).ap()
        rel_d = nc.dram_tensor("bias_rows", [HEADS, P, REVLEN], F32).ap()

        h_in, mem_in, small_in, gate_in, fin_in = (sem(n) for n in ("h_in", "mem_in", "small_in", "gate_in", "fin_in"))
        pool_const, dve_const = sem("pool_const"), sem("dve_const")
        dve_link, act_link = sem("dve_link"), sem("act_link")
        ring_full = [sem(f"ring_full{i}") for i in range(RING)]
        unit_used = sem("unit_used")
        up_full = [sem("up_full0"), sem("up_full1")]
        down_full = [sem("down_full0"), sem("down_full1")]
        n_sq, n_ms, n_rs, n_xs, n_tr, n_ev = (
            sem(n) for n in ("norm_squared", "norm_mean", "norm_rstd", "norm_rows", "norm_turned", "norm_stored"))
        job_mm, job_ev = sem("job_mm"), sem("job_ev")
        a_ux, a_ug, a_gates = sem("a_ux"), sem("a_ug"), sem("a_gates")
        a_uev, a_gsq, a_T, a_sqrt, a_tg = (sem(n) for n in ("a_uev", "a_gsq", "a_T", "a_sqrt", "a_tg"))
        a_xc, a_q, a_g3, a_cat = (sem(n) for n in ("a_xc", "a_q", "a_g3", "a_cat"))
        a_vec, a_exp = sem("a_vec"), sem("a_exp")
        d_s, d_pt, d_o, d_ot = (sem(n) for n in ("d_s", "d_pt", "d_o", "d_ot"))
        d_nmx, d_p, d_ms, d_on = (sem(n) for n in ("d_nmx", "d_p", "d_ms", "d_on"))
        d_exp, d_ptev, d_oev, d_otev = (sem(n) for n in ("d_exp", "d_ptev", "d_oev", "d_otev"))
        d_rs, b_mm, b_ev, b_in, b_mask = (sem(n) for n in ("d_rs", "b_mm", "b_ev", "b_in", "b_mask"))
        b_out = [sem("b_out0"), sem("b_out1")]
        l_sum, l_exp, b_rep, b_load = sem("l_sum"), sem("l_exp"), sem("b_rep"), sem("b_load")
        m_s, m_pt, m_o, m_nmx, m_p, m_exp, m_ptev, m_oev = (
            sem(n) for n in ("m_s", "m_pt", "m_o", "m_nmx", "m_p", "m_exp", "m_ptev", "m_oev"))
        o_mm, o_ev = sem("o_mm"), sem("o_ev")
        xs_out, r_lg, r_lgev, r_exp, r_pexp, r_sel, r_rank, r_hot, r_idx, r_idxi, r_done = (
            sem(n) for n in ("xs_out", "r_lg", "r_lgev", "r_exp", "r_pexp", "r_sel", "r_rank", "r_hot", "r_idx", "r_idxi", "r_done"))
        x_full, y_out, c_full = ([sem(f"{n}{s}") for s in range(2)] for n in ("x_full", "y_out", "c_full"))
        x_tr, x_ev, e_up, e_tanh, e_hid, e_ht, e_htev, e_down, e_yev, e_gate = (
            sem(n) for n in ("x_tr", "x_ev", "e_up", "e_tanh", "e_hid", "e_ht", "e_htev", "e_down", "e_yev", "e_gate"))
        sp_turn, pool_turn = sem("sp_turn"), sem("pool_turn")
        v_over, v_done, c_done = sem("v_over"), sem("v_done"), sem("c_done")
        (v_hot, v_idx, v_idxi, v_xfull, v_tr, v_ev, v_up, v_tanh, v_hid, v_ht, v_htev, v_down,
         v_yev, v_out, v_wfull, v_link, v_free) = (
            [sem(f"{n}{i}") for i in range(2)]
            for n in ("v_hot", "v_idx", "v_idxi", "v_xfull", "v_tr", "v_ev", "v_up", "v_tanh", "v_hid",
                      "v_ht", "v_htev", "v_down", "v_yev", "v_out", "v_wfull", "v_link", "v_free"))
        vec_in, pool_zero, zero_out = sem("vec_in"), sem("pool_zero"), sem("zero_out")
        fin_row, fin_out = sem("fin_row"), sem("fin_out")

        STEPS = [(b, hd) for b in range(NT) for hd in range(HEADS)]
        MSTEPS = [(t, hp) for t in range(NT) for hp in range(2)]
        MS = len(MSTEPS)
        NORM_TILES = [MT, NT, NT, NT, NT, NT]
        NORM_BASE = [sum(NORM_TILES[:n]) for n in range(6)]

        block = ctx.enter_context(nc.Block())

        @block.sync
        def _(sp):
            sp.dma_start(xs[:, 0:MT, :], mem.rearrange("(t p) d -> p t d", p=P)).then_inc(mem_in, 16)
            sp.dma_start(vec[:, :], vecs).then_inc(vec_in, 16)
            sp.dma_start(h[:, :, :], x.rearrange("(t p) d -> p t d", p=P)).then_inc(h_in, 16)

            def load_unit(n):
                if n >= RING:
                    sp.wait_ge(unit_used, n - RING + 1)
                sp.dma_start(ring[:, n % RING, :], units[n, :, :]).then_inc(ring_full[n % RING], 16)

            def load_up(L, e, s, reused=True):
                if reused:
                    sp.wait_ge(e_up, e - 1 + NE * L)
                src = experts[L, e, :, 0:UPW] if isinstance(e, int) else \
                    experts[L, bass.ds(e, 1), :, 0:UPW].rearrange("o p n -> p (o n)")
                sp.dma_start(w_up[s], src).then_inc(up_full[s], 16)

            def load_down(L, e, s, reused=True):
                if reused:
                    sp.wait_ge(e_down, e - 1 + NE * L)
                src = experts[L, e, :, UPW:EXPW] if isinstance(e, int) else \
                    experts[L, bass.ds(e, 1), :, UPW:EXPW].rearrange("o p n -> p (o n)")
                sp.dma_start(w_down[s], src).then_inc(down_full[s], 16)

            def first_experts(L):
                for e in range(2):
                    load_up(L, e, e, False)
                    load_down(L, e, e, False)

            for n in range(0, 10):
                load_unit(n)
            first_experts(0)
            for n in range(10, KV1 + 2):
                load_unit(n)

            for L in range(2):
                for t in range(NT):
                    sp.wait_ge(n_xs, t + 1 + NORM_BASE[2 + 2 * L])
                    sp.dma_start(xs_d[t * P:(t + 1) * P, :], xs[:, t, :]).then_inc(xs_out, 16)
                load_up(L, 2, 0)
                with sp.Fori(1, NE // 2 - 1) as i:
                    load_up(L, 2 * i + 1, 1)
                    load_down(L, 2 * i, 0)
                    load_up(L, 2 * i + 2, 0)
                    load_down(L, 2 * i + 1, 1)
                load_up(L, NE - 1, 1)
                load_down(L, NE - 2, 0)
                load_down(L, NE - 1, 1)
                if L == 0:
                    for n in range(INB, INB + RING - 2):
                        load_unit(n)
                sp.wait_ge(v_over, 1 + L)
                V = sp.value_load(vcount[0:1, 0:1], min_val=0, max_val=MORE)
                with sp.If(V > 0):
                    sp.sem_inc(v_free[L], 1)
                    with sp.Fori(0, V) as i:
                        sp.wait_ge(v_hot[L], i + 1)
                        sp.sem_inc(sp_turn, 1)
                        ev = sp.value_load(vsteer[0:1, 0:1], min_val=0, max_val=NE - 1)
                        sp.wait_ge(e_down, NE + NE * L)
                        sp.dma_start(w_up[0], experts[L, bass.ds(ev, 1), :, 0:UPW]
                                     .rearrange("o p n -> p (o n)")).then_inc(v_wfull[L], 16)
                        sp.dma_start(w_down[0], experts[L, bass.ds(ev, 1), :, UPW:EXPW]
                                     .rearrange("o p n -> p (o n)")).then_inc(v_wfull[L], 16)
                        sp.wait_ge(v_yev[L], i + 1)
                        sp.dma_start(y_d[bass.ds(i * P + NE * P, P), :], ysb[0]).then_inc(v_out[L], 16)
                        sp.wait_ge(v_out[L], 16 * i + 16)
                        sp.sem_inc(v_free[L], 1)
                sp.sem_inc(v_done, 1)
                if L == 0:
                    sp.wait_ge(e_down, NE)
                    first_experts(1)
                    for n in range(INB + RING - 2, UNITS):
                        load_unit(n)
            for t in range(NT):
                sp.wait_ge(fin_row, t + 1)
                sp.dma_start(out[t * P:(t + 1) * P, :], xs[:, t, :]).then_inc(fin_out, 16)
            sp.wait_ge(fin_out, 16 * NT)

        @block.gpsimd
        def _(pool):
            pool.memset(ones[:, :], 1.0).then_inc(pool_const, 1)
            pool.memset(ident[:, :], 0.0).then_inc(pool_const, 1)
            pool.memset(mhalf, -0.5).then_inc(pool_const, 1)
            pool.wait_ge(pool_const, 3)
            pool.affine_select(out=ident[:, :], in_=ident[:, :], compare_op=ALU.not_equal, fill=1.0, base=0,
                               pattern=[[-1, P]], channel_multiplier=1).then_inc(pool_const, 1)
            pool.affine_select(out=before[:, :], in_=ones[:, :], compare_op=ALU.is_gt, fill=0.0, base=0,
                               pattern=[[1, P]], channel_multiplier=-1).then_inc(pool_const, 1)
            pool.iota(iota[:, :], pattern=[[1, P]], base=0, channel_multiplier=0,
                      allow_small_or_imprecise_dtypes=True).then_inc(pool_const, 1)
            pool.iota(tokid[:, :], pattern=[[P, NT]], base=0, channel_multiplier=1,
                      allow_small_or_imprecise_dtypes=True).then_inc(pool_const, 1)
            pool.iota(iota4, pattern=[[1, 4]], base=-16, channel_multiplier=0,
                      allow_small_or_imprecise_dtypes=True).then_inc(pool_const, 1)
            pool.iota(iota16, pattern=[[1, NE]], base=0, channel_multiplier=0,
                      allow_small_or_imprecise_dtypes=True).then_inc(pool_const, 1)
            pool.iota(row16, pattern=[[P, NE]], base=0, channel_multiplier=0,
                      allow_small_or_imprecise_dtypes=True).then_inc(pool_const, 1)
            pool.iota(jcol, pattern=[[0, NE], [P, 3]], base=P, channel_multiplier=0,
                      allow_small_or_imprecise_dtypes=True).then_inc(pool_const, 1)
            pool.dma_start(gw, gate_w.rearrange("s p n -> p s n").rearrange("p s (g j) -> p s g j", g=RB)).then_inc(gate_in, 16)
            pool.dma_start(wgr[:, :, :, :], router.rearrange("l p k e -> p l k e")).then_inc(small_in, 16)
            pool.dma_start(c31, rel_bias[REL - 1:REL, :].to_broadcast([P, HEADS])).then_inc(small_in, 16)

            pool.memset(rsc, 0.0).then_inc(pool_zero, 1)
            pool.wait_ge(pool_zero, 1)
            for j in range(MORE):
                pool.dma_start(y_d[(NE + j) * P:(NE + j + 1) * P, :], rsc).then_inc(zero_out, 16)

            def powers(n):
                for t in range(NORM_TILES[n]):
                    pool.wait_ge(n_ms, t + 1 + NORM_BASE[n])
                    pool.tensor_tensor(rstd[:, t:t + 1], msq[:, t:t + 1], mhalf[:, 0:1], ALU.pow).then_inc(n_rs, 1)

            def gather_experts(L):
                pool.wait_ge(xs_out, 16 * NT + 16 * NT * L)
                for e in range(NE):
                    pool.wait_ge(r_idxi, (1 if e < 2 else 2) + 2 * L)
                    if e >= 2:
                        pool.wait_ge(x_tr, e - 1 + NE * L)
                    pool.indirect_dma_start(xg[e % 2], None, xs_d, bass.IndirectOffsetOnAxis(ap=idxi[:, e:e + 1], axis=0)
                                            ).then_inc(x_full[e % 2], 16)

            def gather_overflow(L):
                pool.wait_ge(v_over, 1 + L)
                V = pool.value_load(vcount[0:1, 0:1], min_val=0, max_val=MORE)
                with pool.If(V > 0):
                    pool.wait_ge(x_tr, NE + NE * L)
                    with pool.Fori(0, V) as i:
                        pool.wait_ge(v_idxi[L], i + 1)
                        pool.sem_inc(pool_turn, 1)
                        pool.indirect_dma_start(xg[0], None, xs_d, bass.IndirectOffsetOnAxis(ap=ovi, axis=0)
                                                ).then_inc(v_xfull[L], 16)

            def gather_results(L):
                pool.wait_ge(y_out[0], 16 * NE // 2 + 8 * NE * L)
                pool.wait_ge(y_out[1], 16 * NE // 2 + 8 * NE * L)
                pool.wait_ge(r_done, 1 + L)
                pool.wait_ge(v_done, 1 + L)
                for t in range(NT):
                    if t >= 2:
                        pool.wait_ge(c_done, t - 1 + NT * L)
                    for r, ri in enumerate((r1i, r2i)):
                        pool.indirect_dma_start(comb[t % 2][r], None, y_d, bass.IndirectOffsetOnAxis(ap=ri[:, t:t + 1], axis=0)
                                                ).then_inc(c_full[t % 2], 16)

            powers(0)
            powers(1)
            powers(2)
            gather_experts(0)
            gather_overflow(0)
            gather_results(0)
            powers(3)
            pool.wait_ge(b_in, 16)
            pool.affine_select(out=bias, in_=bias, compare_op=ALU.is_ge, fill=NEG, base=P,
                               pattern=[[0, HEADS], [-1, NEAR]], channel_multiplier=1).then_inc(b_mask, 1)
            for b in range(NT):
                pool.wait_ge(d_ms, b + 1)
                pool.tensor_tensor(orstd, ossq, mhalf[:, 0:HEADS], ALU.pow).then_inc(d_rs, 1)
            powers(4)
            gather_experts(1)
            gather_overflow(1)
            gather_results(1)
            powers(5)

        @block.scalar
        def _(act):
            links = [0]

            def link(ins):
                links[0] += 1
                ins.then_inc(act_link, 1)
                act.wait_ge(act_link, links[0])

            def norm_squares(n, ready, into):
                for t in range(NORM_TILES[n]):
                    ready(t)
                    act.activation(into(t), (xs if n == 0 else h)[:, t, :], ACT.Square,
                                   accum_out=ssq[:, t:t + 1]).then_inc(n_sq, 1)

            jobs = [0]

            def stored(pairs):
                for dst, src in pairs:
                    n = jobs[0]
                    act.wait_ge(job_mm, n + 1)
                    act.activation(dst, src, ACT.Copy).then_inc(job_ev, 1)
                    jobs[0] += 1

            def kv_jobs():
                stored([(kTm[:, c, :], bank(6 + c)[:, 0:MEM]) for c in range(2)]
                       + [(vm[:, c, :], bank(6 + c)[:, 0:MEM]) for c in range(2)])

            def q_jobs():
                stored([(qmT[:, c, :], bank(6 + c)) for c in range(2)])

            def b_jobs():
                for c in range(HEADS // 2):
                    for dst in (qT, kT):
                        for j in range(2):
                            yield dst[:, 2 * c + j, :], slice(0, T)
                for c in range(3):
                    for t in range(NT):
                        yield vB[:, t, c * 256:(c + 1) * 256], slice(0, 256)
                for c in range(2):
                    yield qmT[:, c, :], slice(0, T)

            def recurrence():
                act.wait_ge(a_vec, 1)
                act.activation(spl[0:RW, :], spl[0:RW, :], ACT.Exp, scale=-1.0).then_inc(a_exp, 1)

                def first(c):
                    act.wait_ge(a_ux, c + 1)
                    if c >= 2:
                        act.wait_ge(a_xc, c - 1)
                    act.activation(upad[:, c % 2, 3:515], bank(c % 2)[0:RW, :], ACT.Copy).then_inc(a_uev, 1)

                def second(c):
                    act.wait_ge(a_gates, c + 1)
                    if c >= 1:
                        act.wait_ge(a_cat, c)
                    link(act.activation(ta, bank(4)[0:RW, :], ACT.Tanh, bias=hba[0:RW, c:c + 1], scale=0.5))
                    act.activation(tx, bank(5)[0:RW, :], ACT.Tanh, bias=hbx[0:RW, c:c + 1], scale=0.5)
                    act.activation(ta, ta, ACT.Tanh, bias=spl[0:RW, c:c + 1], scale=spl[0:RW, c:c + 1]).then_inc(a_T, 1)
                    act.wait_ge(a_ug, c + 1)
                    act.activation(gq, bank(2 + c % 2)[0:RW, :], ACT.Square).then_inc(a_gsq, 1)
                    act.wait_ge(a_g3, c + 1)
                    act.activation(gg, gq, ACT.Tanh, scale=GELU_C).then_inc(a_tg, 1)
                    act.wait_ge(a_q, c + 1)
                    act.activation(sq, dd, ACT.Sqrt, scale=-1.0).then_inc(a_sqrt, 1)

                act.wait_ge(a_vec, 2)
                for c in range(RB):
                    first(c)
                    if c >= 1:
                        second(c - 1)
                second(RB - 1)

            def memory_attention(L):
                def softmax(i):
                    s = i % 2
                    act.wait_ge(m_nmx, i + 1 + MS * L)
                    if i >= 2:
                        act.wait_ge(m_pt, i - 1 + MS * L)
                    for n in range(2):
                        last = act.activation(E[s][:, n, 0:MEM], bank(2 * s + n)[:, 0:MEM], ACT.Exp,
                                              bias=nmx[:, s, n:n + 1], scale=DH ** -0.5, accum_out=rsum[:, s, n:n + 1])
                    last.then_inc(m_exp, 1)

                def turned(i):
                    s = i % 2
                    act.wait_ge(m_pt, i + 1 + MS * L)
                    if i >= 2:
                        act.wait_ge(m_o, i - 1 + MS * L)
                    act.activation(PTs[s], bank(4 + s).rearrange("p (c q) -> p c q", c=4), ACT.Copy).then_inc(m_ptev, 1)

                def result(i):
                    t, hp = MSTEPS[i]
                    act.wait_ge(m_o, i + 1 + MS * L)
                    act.activation(cat[:, (RB if L == 0 else HEADS) + hp, t * P:(t + 1) * P], bank(6 + i % 2)[:, 0:P], ACT.Copy
                                   ).then_inc(m_oev, 1)

                n = len(MSTEPS)
                for i in range(n + 2):
                    if i < n:
                        softmax(i)
                    if 1 <= i <= n:
                        turned(i - 1)
                    if i >= 2:
                        result(i - 2)

            def diff_attention():
                def softmax(i):
                    b, hd = STEPS[i]
                    s, nk = i % 2, (b + 1) * P
                    act.wait_ge(d_nmx, i + 1)
                    for n in range(2):
                        last = act.activation(E[s][:, n, 0:nk], E[s][:, n, 0:nk], ACT.Exp, bias=nmx[:, s, n:n + 1],
                                              accum_out=rsum[:, s, n:n + 1])
                    last.then_inc(d_exp, 1)

                def turned(i):
                    b, hd = STEPS[i]
                    s = i % 2
                    act.wait_ge(d_pt, i + 1)
                    if i >= 2:
                        act.wait_ge(d_o, i - 1)
                    act.activation(PTs[s][:, 0:b + 1, :], bank(4).rearrange("p (c q) -> p c q", c=4)[:, 0:b + 1, :],
                                   ACT.Copy).then_inc(d_ptev, 1)

                def result(i):
                    b, hd = STEPS[i]
                    act.wait_ge(d_o, i + 1)
                    if hd == 0 and b >= 1:
                        act.wait_ge(d_on, b)
                    act.activation(Osb[:, hd, :], bank(5)[:, 0:P], ACT.Copy).then_inc(d_oev, 1)

                def block_out(b):
                    for j, (a, n) in enumerate(((0, 4), (4, 2))):
                        act.wait_ge(d_ot, 2 * b + j + 1)
                        act.activation(cat[:, a:a + n, b * P:(b + 1) * P],
                                       bank(6 + j)[:, 0:n * P].rearrange("p (c q) -> p c q", c=n), ACT.Copy,
                                       scale=gsub[:, 0:1]).then_inc(d_otev, 1)

                n = len(STEPS)
                for i in range(n + 2):
                    if i < n:
                        softmax(i)
                    if 1 <= i <= n:
                        turned(i - 1)
                    if i >= 2:
                        result(i - 2)
                        if (i - 2) % HEADS == 3 and i - 2 > HEADS:
                            block_out((i - 2) // HEADS - 1)
                block_out(NT - 1)

            def routing(L):
                act.wait_ge(r_lg, 1 + L)
                act.wait_ge(zero_out, 16 * MORE)
                act.activation(lg, bank(4)[:, 0:NT * (NG + NE)].rearrange("p (t e) -> p t e", t=NT), ACT.Copy).then_inc(r_lgev, 1)
                act.wait_ge(r_exp, 1 + 2 * L)
                act.activation(rg_e, rg_e, ACT.Exp).then_inc(r_pexp, 1)
                act.wait_ge(r_exp, 2 + 2 * L)
                act.activation(rdiff, rdiff, ACT.Exp).then_inc(r_pexp, 1)

            def experts_act(L):
                def first(e, s):
                    act.wait_ge(e_up, e + 1 + NE * L)
                    act.activation(tnh[s], bank(4 + s)[:, 0:DE], ACT.Tanh, scale=0.5).then_inc(e_tanh, 1)

                def turned(e, s):
                    act.wait_ge(e_ht, e + 1 + NE * L)
                    act.activation(hidT[s], bank(2)[:, 0:2 * P].rearrange("p (f t) -> p f t", f=2), ACT.Copy
                                   ).then_inc(e_htev, 1)

                def result(e, s, uses):
                    act.wait_ge(e_down, e + 1 + NE * L)
                    if uses is not None:
                        act.wait_ge(y_out[s], uses + 8 * NE * L)
                    act.activation(ysb[s].rearrange("p (b n) -> p b n", b=2), ps[:, 6:8, :], ACT.Copy).then_inc(e_yev, 1)
                    act.wait_ge(e_yev, e + 1 + NE * L)
                    if isinstance(e, int):
                        act.dma_start(y_d[e * P:(e + 1) * P, :], ysb[s]).then_inc(y_out[s], 16)
                    else:
                        act.dma_start(y_d[bass.ds(e * P, P), :], ysb[s]).then_inc(y_out[s], 16)

                first(0, 0)
                turned(0, 0)
                first(1, 1)
                result(0, 0, None)
                turned(1, 1)
                first(2, 0)
                result(1, 1, None)
                turned(2, 0)
                with act.Fori(1, NE // 2 - 1) as i:
                    first(2 * i + 1, 1)
                    result(2 * i, 0, 16 * i)
                    turned(2 * i + 1, 1)
                    first(2 * i + 2, 0)
                    result(2 * i + 1, 1, 16 * i)
                    turned(2 * i + 2, 0)
                first(NE - 1, 1)
                result(NE - 2, 0, 16 * (NE // 2 - 1))
                turned(NE - 1, 1)
                result(NE - 1, 1, 16 * (NE // 2 - 1))

            def overflow(L):
                act.wait_ge(v_over, 1 + L)
                V = act.value_load(vcount[0:1, 0:1], min_val=0, max_val=MORE)
                with act.If(V > 0):
                    act.wait_ge(y_out[0], 16 * NE // 2 + 8 * NE * L)
                    with act.Fori(0, V) as i:
                        act.wait_ge(v_up[L], i + 1)
                        act.activation(tnh[0], bank(4)[:, 0:DE], ACT.Tanh, scale=0.5).then_inc(v_tanh[L], 1)
                        act.wait_ge(v_ht[L], i + 1)
                        act.activation(hidT[0], bank(2)[:, 0:2 * P].rearrange("p (f t) -> p f t", f=2), ACT.Copy
                                       ).then_inc(v_htev[L], 1)
                        act.wait_ge(v_down[L], i + 1)
                        act.activation(ysb[0].rearrange("p (b n) -> p b n", b=2), ps[:, 6:8, :], ACT.Copy
                                       ).then_inc(v_yev[L], 1)

            norm_squares(0, lambda t: act.wait_ge(mem_in, 16), lambda t: hflat[:, t * D:(t + 1) * D])
            act.wait_ge(h_in, 16)
            norm_squares(1, lambda t: act.wait_ge(n_tr, MT), lambda t: xs[:, t, :])
            kv_jobs()
            recurrence()
            q_jobs()
            memory_attention(0)
            norm_squares(2, lambda t: act.wait_ge(o_ev, t + 1), lambda t: xs[:, t, :])
            routing(0)
            kv_jobs()
            experts_act(0)
            overflow(0)
            norm_squares(3, lambda t: act.wait_ge(c_done, t + 1), lambda t: xs[:, t, :])
            act.dma_start(lall, diff_l.to_broadcast([P, 4 * DH])).then_inc(b_load, 16)
            act.dma_start(relsb, rel_bias).then_inc(b_load, 16)
            act.dma_start(hotsb, onehot).then_inc(b_load, 16)
            act.wait_ge(l_sum, 1)
            act.activation(lexp, lsum, ACT.Exp).then_inc(l_exp, 1)
            for hd in range(HEADS):
                act.wait_ge(b_mm, hd + 1)
                if hd >= 2:
                    act.wait_ge(b_out[hd % 2], 16 * (hd // 2))
                act.activation(relrows[:, hd % 2, :], bank(hd % 2)[:, 0:REVLEN], ACT.Copy).then_inc(b_ev, 1)
                act.wait_ge(b_ev, hd + 1)
                act.dma_start(rel_d[hd, :, :], relrows[:, hd % 2, :]).then_inc(b_out[hd % 2], 16)
            for o in b_out:
                act.wait_ge(o, 16 * HEADS // 2)
            skew = rel_d.rearrange("h p m -> h (p m)")[:, P - 1:P - 1 + (REVLEN - 1) * P] \
                .rearrange("h (q c) -> q h c", c=REVLEN - 1)[:, :, 0:NEAR]
            act.dma_start(bias, skew).then_inc(b_in, 16)
            stored([(dst, bank(4 + j % 4)[:, cols]) for j, (dst, cols) in enumerate(b_jobs())])
            diff_attention()
            memory_attention(1)
            norm_squares(4, lambda t: act.wait_ge(o_ev, t + 1 + NT), lambda t: xs[:, t, :])
            routing(1)
            experts_act(1)
            overflow(1)
            act.dma_start(gfin, final_g.to_broadcast([P, D])).then_inc(fin_in, 16)
            norm_squares(5, lambda t: act.wait_ge(c_done, t + 1 + NT), lambda t: xs[:, t, :])

        @block.vector
        def _(dve):
            links = [0]

            def link(ins):
                links[0] += 1
                ins.then_inc(dve_link, 1)
                dve.wait_ge(dve_link, links[0])

            def norm(n, src, turned, g):
                nt = NORM_TILES[n]
                for t in range(nt + 1):
                    if t < nt:
                        dve.wait_ge(n_sq, t + 1 + NORM_BASE[n])
                        dve.tensor_scalar(msq[:, t:t + 1], ssq[:, t:t + 1], 1.0 / D, EPS, ALU.mult, ALU.add
                                          ).then_inc(n_ms, 1)
                        dve.wait_ge(n_rs, t + 1 + NORM_BASE[n])
                        dve.tensor_scalar(xs[:, t, :], src[:, t, :], rstd[:, t:t + 1], None, ALU.mult
                                          ).then_inc(n_xs, 1)
                    if t >= 1:
                        b = 2 * ((t - 1) % 2)
                        dve.wait_ge(n_tr, t + NORM_BASE[n])
                        dve.tensor_tensor(turned[:, :, (t - 1) * P:t * P],
                                          ps[:, b:b + 2, :].rearrange("p b (k t) -> p (b k) t", k=KC // 2),
                                          v(g).unsqueeze(2).to_broadcast([P, KC, P]), ALU.mult).then_inc(n_ev, 1)

            def channel_vectors():
                lam, s, z, z2 = v("lam")[0:RW, :], hba[0:RW, :], hbx[0:RW, :], sp8[0:RW, :]
                sp = spl[0:RW, :]
                link(dve.tensor_scalar(z, lam, -1.0, None, ALU.mult))
                dve.tensor_tensor(sp, lam, z, ALU.max).then_inc(a_vec, 1)
                dve.wait_ge(a_exp, 1)
                link(dve.tensor_scalar(z, sp, 2.0, None, ALU.add))
                link(dve.reciprocal(z, z))
                link(dve.tensor_tensor(z, z, sp, ALU.mult))
                link(dve.tensor_tensor(z2, z, z, ALU.mult))
                link(dve.tensor_scalar(s, z2, 1.0 / 19, None, ALU.mult))
                for k in range(17, 1, -2):
                    link(dve.scalar_tensor_tensor(s, s, 1.0 / k, z2, ALU.add, ALU.mult))
                link(dve.tensor_scalar(s, s, 1.0, 4.0, ALU.add, ALU.mult))
                link(dve.tensor_tensor(s, s, z, ALU.mult))
                link(dve.tensor_scalar(z, lam, -1.0, 0.0, ALU.mult, ALU.max))
                link(dve.scalar_tensor_tensor(sp, z, 2.0, s, ALU.mult, ALU.add))
                link(dve.tensor_scalar(hba[0:RW, :], v("gate_a_b")[0:RW, :], 0.5, None, ALU.mult))
                dve.tensor_scalar(hbx[0:RW, :], v("gate_x_b")[0:RW, :], 0.5, None, ALU.mult).then_inc(a_vec, 1)

            def recurrence():
                def conv(c):
                    u, o = upad[:, c % 2, :], xc[c % 2]
                    w = v("conv_w", c * CONV, (c + 1) * CONV)[0:RW, :]
                    dve.wait_ge(a_uev, c + 1)
                    if c >= 2:
                        dve.wait_ge(a_gates, c - 1)
                        dve.wait_ge(a_cat, c - 1)
                    link(dve.tensor_scalar(o, u[:, 0:T], w[:, 0:1], v("conv_b", c, c + 1)[0:RW, :], ALU.mult, ALU.add))
                    for j in range(1, CONV):
                        ins = dve.scalar_tensor_tensor(o, u[:, j:j + T], w[:, j:j + 1], o, ALU.mult, ALU.add)
                        if j < CONV - 1:
                            link(ins)
                    ins.then_inc(a_xc, 1)

                def mix(c):
                    ug = bank(2 + c % 2)[0:RW, :]
                    dve.wait_ge(a_T, c + 1)
                    dve.wait_ge(a_gsq, c + 1)
                    link(dve.tensor_scalar(gq, gq, 0.044715, 1.0, ALU.mult, ALU.add))
                    dve.tensor_tensor(gq, gq, ug, ALU.mult).then_inc(a_g3, 1)
                    link(dve.tensor_scalar(ra, ta, 1.0, None, ALU.add))
                    link(dve.reciprocal(ra, ra))
                    link(dve.scalar_tensor_tensor(dd, ta, 2.0, ra, ALU.mult, ALU.mult))
                    link(dve.tensor_scalar(ra, dd, -1.0, 1.0, ALU.mult, ALU.add))
                    dve.scalar_tensor_tensor(dd, dd, -2.0, dd, ALU.add, ALU.mult).then_inc(a_q, 1)
                    dve.scalar_tensor_tensor(tx, tx, 1.0, xc[c % 2], ALU.add, ALU.mult)
                    dve.wait_ge(a_tg, c + 1)
                    link(dve.scalar_tensor_tensor(gg, gg, 1.0, ug, ALU.add, ALU.mult))
                    dve.wait_ge(a_sqrt, c + 1)
                    link(dve.scalar_tensor_tensor(tx, tx, 0.5, sq, ALU.mult, ALU.mult))
                    link(dve.tensor_tensor_scan(hh, ra, tx, 0.0, ALU.mult, ALU.add))
                    dve.scalar_tensor_tensor(cat[0:RW, c, :], hh, 0.5, gg, ALU.mult, ALU.mult).then_inc(a_cat, 1)

                for c in range(RB):
                    conv(c)
                    if c >= 1:
                        mix(c - 1)
                mix(RB - 1)

            def memory_attention(L):
                n = len(MSTEPS)
                for i in range(n + 1):
                    if i < n:
                        s = i % 2
                        dve.wait_ge(m_s, i + 1 + MS * L)
                        link(dve.tensor_reduce(mx[:, s, :], ps[:, 2 * s:2 * s + 2, 0:MEM], AXX, ALU.max))
                        dve.tensor_scalar(nmx[:, s, :], mx[:, s, :], -DH ** -0.5, None, ALU.mult).then_inc(m_nmx, 1)
                    if i >= 1:
                        s = (i - 1) % 2
                        dve.wait_ge(m_exp, i + MS * L)
                        link(dve.reciprocal(rec[:, s, :], rsum[:, s, :]))
                        dve.tensor_tensor(E[s][:, :, 0:MEM], E[s][:, :, 0:MEM],
                                          rec[:, s, :].unsqueeze(2).to_broadcast([P, 2, MEM]), ALU.mult).then_inc(m_p, 1)

            def output(L):
                for t in range(NT):
                    dve.wait_ge(o_mm, t + 1 + NT * L)
                    ht = h[:, t, :].rearrange("p (b n) -> p b n", b=2)
                    dve.tensor_tensor(ht, ps[:, 2 * t:2 * t + 2, :], ht, ALU.add).then_inc(o_ev, 1)

            def routing(L):
                def bc(a, axis, shape):
                    return a.unsqueeze(axis).to_broadcast(shape)

                def first_max(src, n_max, eq, ji, oh):
                    link(dve.tensor_reduce(n_max, src, AXX, ALU.max))
                    link(dve.tensor_tensor(eq, src, bc(n_max, 2, [P, NT, 4]), ALU.is_equal))
                    link(dve.tensor_tensor(eq, eq, bc(iota4, 1, [P, NT, 4]), ALU.mult))
                    link(dve.tensor_reduce(ji, eq, AXX, ALU.min))
                    link(dve.tensor_tensor(oh, bc(iota4, 1, [P, NT, 4]), bc(ji, 2, [P, NT, 4]), ALU.is_equal))

                dve.wait_ge(r_lgev, 1 + L)
                g, el = lg[:, :, 0:NG], lg[:, :, NG:NG + NE]
                first_max(g, r_gmax, r_eqg, r_gi, ohg)
                dve.tensor_tensor(rg_e, g, bc(r_gmax, 2, [P, NT, NG]), ALU.subtract).then_inc(r_exp, 1)
                for t in range(NT):
                    last = dve.tensor_tensor(r_prod[:, t, :, :], el[:, t, :].rearrange("p (g j) -> p g j", g=NG),
                                             bc(ohg[:, t, :], 2, [P, NG, EPG]), ALU.mult)
                link(last)
                link(dve.tensor_reduce(e_in, r_prod.rearrange("p t g j -> p t j g"), AXX, ALU.add))
                first_max(e_in, r_m1, r_eqe, r_ji, oh1)
                link(dve.scalar_tensor_tensor(e_in, oh1, NEG, e_in, ALU.mult, ALU.add))
                first_max(e_in, r_m2, r_eqe, r_ji, oh2)
                dve.tensor_tensor(rdiff, r_m2, r_m1, ALU.subtract).then_inc(r_exp, 1)
                for t in range(NT):
                    for o, oh in ((ohe1, oh1), (ohe2, oh2)):
                        last = dve.tensor_tensor(o[:, t, :].rearrange("p (g j) -> p g j", g=NG),
                                                 bc(ohg[:, t, :], 2, [P, NG, EPG]), bc(oh[:, t, :], 1, [P, NG, EPG]), ALU.mult)
                link(last)
                dve.tensor_tensor(sel, ohe1, ohe2, ALU.add).then_inc(r_sel, 1)
                dve.wait_ge(r_pexp, 1 + 2 * L)
                link(dve.tensor_reduce(r_gsum, rg_e, AXX, ALU.add))
                link(dve.reciprocal(r_gw, r_gsum))
                dve.wait_ge(r_pexp, 2 + 2 * L)
                link(dve.tensor_scalar(r_den, rdiff, 1.0, None, ALU.add))
                link(dve.reciprocal(r_den, r_den))
                link(dve.tensor_tensor(wv1, r_den, r_gw, ALU.mult))
                link(dve.tensor_tensor(wv2, rdiff, wv1, ALU.mult))
                dve.wait_ge(r_rank, 1 + L)
                link(dve.tensor_copy(r_cnt, bank(5)[:, 64:128].rearrange("p (t e) -> p t e", t=NT)))
                link(dve.tensor_scalar(r_off[:, 0, :], r_cnt[:, 0, :], 0.0, None, ALU.mult))
                for t in range(1, NT):
                    link(dve.tensor_tensor(r_off[:, t, :], r_off[:, t - 1, :], r_cnt[:, t - 1, :], ALU.add))
                link(dve.tensor_tensor(ntot, r_off[:, NT - 1, :], r_cnt[:, NT - 1, :], ALU.add))
                link(dve.tensor_tensor(r_rankv, bank(5)[:, 0:64].rearrange("p (t e) -> p t e", t=NT), r_off, ALU.add))
                link(dve.scalar_tensor_tensor(rk, r_rankv, 1.0, sel, ALU.add, ALU.mult))
                link(dve.tensor_scalar(rk, rk, -1.0, None, ALU.add))

                def hot(e):
                    if e >= 2:
                        dve.wait_ge(r_idx, e - 1 + NE * L)
                    dve.tensor_tensor(onesl[e % 2], bc(iota[:, :], 1, [P, NT, P]), bc(rk[:, :, e], 2, [P, NT, P]), ALU.is_equal
                                      ).then_inc(r_hot, 1)

                hot(0)
                hot(1)
                dve.wait_ge(r_idx, 2 + NE * L)
                dve.tensor_copy(idxi[:, 0:2], bank(3)[:, 0:2]).then_inc(r_idxi, 1)
                for e in range(2, NE):
                    hot(e)
                dve.wait_ge(r_idx, NE + NE * L)
                dve.tensor_copy(idxi[:, 2:NE], bank(3)[:, 2:NE]).then_inc(r_idxi, 1)
                for j in range(1, NT):
                    last = dve.tensor_scalar(r_over[:, :, j - 1], ntot, float(j * P), None, ALU.is_gt)
                link(last)
                flat = r_over.rearrange("p e j -> p (e j)")
                cum = r_cum.rearrange("p e j -> p (e j)")
                link(dve.tensor_tensor_scan(cum, ones[:, 0:NE * 3], flat, 0.0, ALU.mult, ALU.add))
                link(dve.tensor_tensor(vidx, r_cum, r_over, ALU.mult))
                link(dve.memset(vc, 0.0))
                dve.tensor_copy(vcount, cum[:, NE * 3 - 1:NE * 3]).then_inc(v_over, 1)
                link(dve.tensor_tensor(r_base, r_cum[:, :, 0], r_over[:, :, 0], ALU.subtract))
                link(dve.tensor_scalar(r_base, r_base, float(P), float((NE - 1) * P), ALU.mult, ALU.add))
                link(dve.tensor_tensor(r_base, r_base, row16, ALU.subtract))
                link(dve.tensor_scalar(r_slot, r_rankv, float(P), None, ALU.is_ge))
                link(dve.tensor_tensor(r_slot, r_slot, bc(r_base, 1, [P, NT, NE]), ALU.mult))
                link(dve.tensor_tensor(r_slot, r_slot, r_rankv, ALU.add))
                link(dve.tensor_tensor(r_slot, r_slot, bc(row16, 1, [P, NT, NE]), ALU.add))
                link(dve.tensor_tensor(ohe1, ohe1, r_slot, ALU.mult))
                link(dve.tensor_tensor(ohe2, ohe2, r_slot, ALU.mult))
                link(dve.tensor_reduce(r_r1, ohe1, AXX, ALU.add))
                link(dve.tensor_reduce(r_r2, ohe2, AXX, ALU.add))
                link(dve.tensor_copy(r1i, r_r1))
                dve.tensor_copy(r2i, r_r2).then_inc(r_done, 1)

            def turned_rows(L, s):
                return dve.tensor_tensor(xgT[s], ps[:, 0:2, :].rearrange("p b (k t) -> p (b k) t", k=KC // 2),
                                         v(f"ffn{L}").unsqueeze(2).to_broadcast([P, KC, P]), ALU.mult)

            def gated(s):
                return dve.scalar_tensor_tensor(tnh[s], tnh[s], 1.0, bank(4 + s)[:, 0:DE], ALU.add, ALU.mult)

            def hidden(s):
                return dve.scalar_tensor_tensor(hid[s], tnh[s], 0.5, bank(4 + s)[:, DE:2 * DE], ALU.mult, ALU.mult)

            def experts_dve(L):
                def rows(e, s, reused=True):
                    dve.wait_ge(x_tr, e + 1 + NE * L)
                    if reused:
                        dve.wait_ge(e_up, e - 1 + NE * L)
                    turned_rows(L, s).then_inc(x_ev, 1)

                def hidden_of(e, s, reused=True):
                    dve.wait_ge(e_tanh, e + 1 + NE * L)
                    gated(s).then_inc(e_gate, 1)
                    if reused:
                        dve.wait_ge(e_ht, e - 1 + NE * L)
                    dve.wait_ge(e_gate, e + 1 + NE * L)
                    hidden(s).then_inc(e_hid, 1)

                rows(0, 0, False)
                hidden_of(0, 0, False)
                rows(1, 1, False)
                hidden_of(1, 1, False)
                rows(2, 0)
                with dve.Fori(1, NE // 2 - 1) as i:
                    hidden_of(2 * i, 0)
                    rows(2 * i + 1, 1)
                    hidden_of(2 * i + 1, 1)
                    rows(2 * i + 2, 0)
                hidden_of(NE - 2, 0)
                rows(NE - 1, 1)
                hidden_of(NE - 1, 1)

            def overflow(L):
                dve.wait_ge(v_over, 1 + L)
                V = dve.value_load(vcount[0:1, 0:1], min_val=0, max_val=MORE)
                steps = 12
                with dve.If(V > 0):
                    with dve.Fori(0, V) as i:
                        at = [0]

                        def vlink(ins):
                            at[0] += 1
                            ins.then_inc(v_link[L], 1)
                            dve.wait_ge(v_link[L], i * steps + at[0])

                        dve.wait_ge(v_free[L], i + 1)
                        vlink(dve.tensor_scalar(vc, vc, 1.0, None, ALU.add))
                        vlink(dve.tensor_scalar(v_m, vidx, vc, None, ALU.is_equal))
                        vlink(dve.tensor_reduce(v_eoh, v_m, AXX, ALU.add))
                        vlink(dve.tensor_tensor(v_m, v_m, jcol, ALU.mult))
                        vlink(dve.tensor_reduce(v_jv, v_m.rearrange("p e j -> p (e j)"), AXX, ALU.add))
                        vlink(dve.tensor_tensor(v_rr, rk, v_eoh.unsqueeze(1).to_broadcast([P, NT, NE]), ALU.mult))
                        vlink(dve.tensor_reduce(v_rk, v_rr, AXX, ALU.add))
                        vlink(dve.tensor_scalar(v_rk, v_rk, v_jv, None, ALU.subtract))
                        vlink(dve.tensor_tensor(v_t16, v_eoh, iota16, ALU.mult))
                        vlink(dve.tensor_reduce(v_es, v_t16, AXX, ALU.add))
                        vlink(dve.tensor_copy(vsteer, v_es))
                        dve.tensor_tensor(onesl[0], iota[:, :].unsqueeze(1).to_broadcast([P, NT, P]),
                                          v_rk.unsqueeze(2).to_broadcast([P, NT, P]), ALU.is_equal).then_inc(v_hot[L], 1)
                        dve.wait_ge(v_idx[L], i + 1)
                        dve.tensor_copy(ovi, bank(3)[:, 0:1]).then_inc(v_idxi[L], 1)
                        dve.wait_ge(v_tr[L], i + 1)
                        turned_rows(L, 0).then_inc(v_ev[L], 1)
                        dve.wait_ge(v_tanh[L], i + 1)
                        vlink(gated(0))
                        assert at[0] == steps
                        hidden(0).then_inc(v_hid[L], 1)

            def combine(L):
                for t in range(NT):
                    dve.wait_ge(c_full[t % 2], 32 * (t // 2 + 1) + 32 * (NT // 2) * L)
                    link(dve.scalar_tensor_tensor(h[:, t, :], comb[t % 2][0], wv1[:, t:t + 1], h[:, t, :], ALU.mult, ALU.add))
                    dve.scalar_tensor_tensor(h[:, t, :], comb[t % 2][1], wv2[:, t:t + 1], h[:, t, :], ALU.mult, ALU.add
                                             ).then_inc(c_done, 1)

            def lambda_and_bias():
                dve.wait_ge(b_load, 48)
                lv = lall.rearrange("p (a b d) -> p a b d", a=2, b=2)
                link(dve.tensor_tensor(lprod, lv[:, :, 0, :], lv[:, :, 1, :], ALU.mult))
                dve.tensor_reduce(lsum, lprod, AXX, ALU.add).then_inc(l_sum, 1)
                dve.tensor_copy(relrep, relsb.unsqueeze(2).to_broadcast([REL, HEADS, P])).then_inc(b_rep, 1)
                dve.wait_ge(l_exp, 1)
                link(dve.tensor_tensor(neglam, lexp[:, 1:2], lexp[:, 0:1], ALU.subtract))
                link(dve.tensor_scalar(neglam, neglam, -LAMBDA_INIT, None, ALU.add))
                link(dve.tensor_scalar(gsub, v("subln"), 1.0 - LAMBDA_INIT, None, ALU.mult))

            def diff_attention():
                def scores(i):
                    b, hd = STEPS[i]
                    s, nk = i % 2, (b + 1) * P
                    near = min(nk, NEAR)
                    far = nk - near
                    S = ps[:, 2 * s:2 * s + 2, :]
                    dve.wait_ge(d_s, i + 1)
                    if i >= 2:
                        dve.wait_ge(d_pt, i - 1)
                    last = dve.scalar_tensor_tensor(E[s][:, :, far:nk], S[:, :, far:nk], DH ** -0.5,
                                                    bias[:, hd, NEAR - near:NEAR].unsqueeze(1).to_broadcast([P, 2, near]),
                                                    ALU.mult, ALU.add)
                    if far:
                        last = dve.tensor_scalar(E[s][:, :, 0:far], S[:, :, 0:far], DH ** -0.5, c31[:, hd:hd + 1],
                                                 ALU.mult, ALU.add)
                    link(last)
                    link(dve.tensor_reduce(mx[:, s, :], E[s][:, :, 0:nk], AXX, ALU.max))
                    dve.tensor_scalar(nmx[:, s, :], mx[:, s, :], -1.0, None, ALU.mult).then_inc(d_nmx, 1)

                def weights(i):
                    b, hd = STEPS[i]
                    s, nk = i % 2, (b + 1) * P
                    dve.wait_ge(d_exp, i + 1)
                    link(dve.reciprocal(rec[:, s, :], rsum[:, s, :]))
                    link(dve.tensor_tensor(rec[:, s, 1:2], rec[:, s, 1:2], neglam, ALU.mult))
                    link(dve.tensor_scalar(E[s][:, 0, 0:nk], E[s][:, 0, 0:nk], rec[:, s, 0:1], None, ALU.mult))
                    dve.scalar_tensor_tensor(E[s][:, 0, 0:nk], E[s][:, 1, 0:nk], rec[:, s, 1:2], E[s][:, 0, 0:nk],
                                             ALU.mult, ALU.add).then_inc(d_p, 1)

                def subnorm(b):
                    dve.wait_ge(d_oev, HEADS * (b + 1))
                    if b >= 1:
                        dve.wait_ge(d_ot, 2 * b)
                    link(dve.tensor_tensor(On, Osb, Osb, ALU.mult))
                    link(dve.tensor_reduce(ossq, On, AXX, ALU.add))
                    dve.tensor_scalar(ossq, ossq, 1.0 / P, EPS, ALU.mult, ALU.add).then_inc(d_ms, 1)
                    dve.wait_ge(d_rs, b + 1)
                    dve.tensor_tensor(On, Osb, orstd.unsqueeze(2).to_broadcast([P, HEADS, P]), ALU.mult).then_inc(d_on, 1)

                n = len(STEPS)
                dve.wait_ge(b_mask, 1)
                for i in range(n + 1):
                    if i < n:
                        scores(i)
                    if i >= 1:
                        weights(i - 1)
                    if i % HEADS == 2 and i > HEADS:
                        subnorm(i // HEADS - 1)
                subnorm(NT - 1)

            dve.wait_ge(vec_in, 16)
            dve.wait_ge(small_in, 32)
            dve.memset(upad[:, :, 0:3], 0.0).then_inc(dve_const, 1)
            norm(0, xs, memT, "mem")
            channel_vectors()
            norm(1, h, hnT, "mix0")
            recurrence()
            memory_attention(0)
            output(0)
            norm(2, h, hnT, "ffn0")
            routing(0)
            experts_dve(0)
            overflow(0)
            combine(0)
            norm(3, h, hnT, "mix1")
            lambda_and_bias()
            diff_attention()
            memory_attention(1)
            output(1)
            norm(4, h, hnT, "ffn1")
            routing(1)
            experts_dve(1)
            overflow(1)
            combine(1)
            dve.wait_ge(fin_in, 16)
            for t in range(NT):
                dve.wait_ge(n_sq, t + 1 + NORM_BASE[5])
                dve.tensor_scalar(msq[:, t:t + 1], ssq[:, t:t + 1], 1.0 / D, EPS, ALU.mult, ALU.add).then_inc(n_ms, 1)
                dve.wait_ge(n_rs, t + 1 + NORM_BASE[5])
                dve.scalar_tensor_tensor(xs[:, t, :], h[:, t, :], rstd[:, t:t + 1], gfin, ALU.mult, ALU.mult
                                         ).then_inc(fin_row, 1)

        @block.tensor
        def _(pe):
            mm = nc.tensor.matmul

            def unit(n):
                pe.wait_ge(ring_full[n % RING], 16 * (n // RING + 1))
                return ring[:, n % RING, :]

            def chain(dst, pairs):
                pairs = list(pairs)
                for k, (lhsT, rhs) in enumerate(pairs):
                    ins = mm(dst, lhsT, rhs, start=(k == 0), stop=(k == len(pairs) - 1))
                return ins

            def turn_rows(n, L=None):
                for t in range(NORM_TILES[n]):
                    b = 2 * (t % 2)
                    pe.wait_ge(n_xs, t + 1 + NORM_BASE[n])
                    if t >= 2:
                        pe.wait_ge(n_ev, t - 1 + NORM_BASE[n])
                    elif t == 1 and L is not None:
                        pe.wait_ge(o_ev, 2 + NT * L)
                    for k in range(KC):
                        ins = nc.tensor.transpose(ps[:, b + k // 4, (k % 4) * P:(k % 4 + 1) * P],
                                                  xs[:, t, k * P:(k + 1) * P], ident[:, :])
                    ins.then_inc(n_tr, 1)

            jobs = [0]

            def job(dst, banks, pairs):
                n = jobs[0]
                if n >= banks:
                    pe.wait_ge(job_ev, n - banks + 1)
                jobs[0] += 1
                ins = chain(dst, pairs)
                ins.then_inc(job_mm, 1)

            def used(n):
                pe.wait_ge(job_mm, jobs[0])
                pe.sem_inc(unit_used, 1)

            def kv(n0):
                w = unit(n0).rearrange("p (k n) -> p k n", k=KC)
                for c in range(2):
                    job(bank(6 + c)[:, 0:MEM], 2, ((w[:, k, c * P:(c + 1) * P], memT[:, k, :]) for k in range(KC)))
                w2 = unit(n0 + 1).rearrange("p (k n) -> p k n", k=KC)
                for c in range(MT):
                    job(bank(6 + c)[:, 0:256], 2, ((memT[:, k, c * P:(c + 1) * P], w2[:, k, :]) for k in range(KC)))
                used(n0)
                used(n0 + 1)

            def recurrence():
                def project(c):
                    for j, (done, b) in enumerate(((a_ux, 0), (a_ug, 2))):
                        n = INA + 2 * (c // 2) + j
                        w = unit(n)[:, 0:KC * 2 * RW].rearrange("p (k n) -> p k n", k=KC)
                        if c >= 2:
                            pe.wait_ge((a_uev, a_cat)[j], c - 1)
                        ins = chain(bank(b + c % 2)[0:RW, :],
                                    ((w[:, k, (c % 2) * RW:(c % 2 + 1) * RW], hnT[:, k, :]) for k in range(KC)))
                        ins.then_inc(done, 1)
                        if c % 2 == 1:
                            pe.wait_ge(done, c + 1)
                            pe.sem_inc(unit_used, 1)

                def gates(c):
                    pe.wait_ge(a_xc, c + 1)
                    if c >= 1:
                        pe.wait_ge(a_T, c)
                    else:
                        pe.wait_ge(gate_in, 16)
                    mm(bank(4)[0:RW, :], gw[:, 0, c, :], xc[c % 2], start=True, stop=True)
                    mm(bank(5)[0:RW, :], gw[:, 1, c, :], xc[c % 2], start=True, stop=True).then_inc(a_gates, 1)

                for c in range(RB):
                    project(c)
                    if c >= 1:
                        gates(c - 1)
                gates(RB - 1)

            def q_memory(n):
                w = unit(n).rearrange("p (k n) -> p k n", k=KC)
                for c in range(2):
                    job(bank(6 + c), 2, ((w[:, k, c * P:(c + 1) * P], hnT[:, k, :]) for k in range(KC)))
                used(n)

            def memory_attention(L):
                def scores(i):
                    t, hp = MSTEPS[i]
                    if i >= 2:
                        pe.wait_ge(m_exp, i - 1 + MS * L)
                    for n in range(2):
                        r = slice(n * DH, (n + 1) * DH)
                        ins = mm(bank(2 * (i % 2) + n)[:, 0:MEM], qmT[r, hp, t * P:(t + 1) * P], kTm[r, hp, :],
                                 start=True, stop=True)
                    ins.then_inc(m_s, 1)

                def turn(i):
                    s = i % 2
                    pe.wait_ge(m_p, i + 1 + MS * L)
                    if i >= 2:
                        pe.wait_ge(m_ptev, i - 1 + MS * L)
                    for n in range(2):
                        for c in range(MT):
                            j = n * MT + c
                            ins = nc.tensor.transpose(bank(4 + s)[:, j * P:(j + 1) * P], E[s][:, n, c * P:(c + 1) * P], ident[:, :])
                    ins.then_inc(m_pt, 1)

                def values(i):
                    t, hp = MSTEPS[i]
                    s = i % 2
                    pe.wait_ge(m_ptev, i + 1 + MS * L)
                    if i >= 2:
                        pe.wait_ge(m_oev, i - 1 + MS * L)
                    for n in range(2):
                        hd = 2 * hp + n
                        ins = chain(bank(6 + s)[n * DH:(n + 1) * DH, 0:P],
                                    ((vm[:, c, hd * DH:(hd + 1) * DH], PTs[s][:, n * MT + c, :]) for c in range(MT)))
                    ins.then_inc(m_o, 1)

                n = len(MSTEPS)
                pe.wait_ge(job_ev, jobs[0])
                if L == 0:
                    pe.wait_ge(a_cat, RB)
                else:
                    pe.wait_ge(d_otev, 2 * NT)
                for i in range(n + 2):
                    if i < n:
                        scores(i)
                    if 1 <= i <= n:
                        turn(i - 1)
                    if i >= 2:
                        values(i - 2)

            def output(L):
                pe.wait_ge(m_oev, MS + MS * L)
                pe.wait_ge(a_cat, RB)
                if L == 1:
                    pe.wait_ge(d_otev, 2 * NT)
                n0, chunks = ((OUTA, [RW] * RB + [P] * 2), (OUTB, [P] * 8))[L]
                for j, rows in enumerate(chunks):
                    w = unit(n0 + j // 2)[0:rows, (j % 2) * D:(j % 2 + 1) * D]
                    last = j == len(chunks) - 1
                    for t in range(NT):
                        for b in range(2):
                            ins = mm(bank(2 * t + b), cat[0:rows, j, t * P:(t + 1) * P], w[:, b * 512:(b + 1) * 512],
                                     start=(j == 0), stop=last)
                        if last:
                            ins.then_inc(o_mm, 1)
                    if j % 2 == 1 and not last:
                        ins.then_inc(unit_used, 1)
                pe.wait_ge(o_mm, NT + NT * L)
                pe.sem_inc(unit_used, 1)

            def routing(L):
                pe.wait_ge(n_ev, NT + NORM_BASE[2 + 2 * L])
                for t in range(NT):
                    ins = chain(bank(4)[:, t * (NG + NE):(t + 1) * (NG + NE)],
                                ((hnT[:, k, t * P:(t + 1) * P], wgr[:, L, k, :]) for k in range(KC)))
                ins.then_inc(r_lg, 1)
                if L == 0:
                    kv(KV1)
                pe.wait_ge(r_sel, 1 + L)
                mm(bank(5)[:, 0:64], before[:, :], sel.rearrange("p t e -> p (t e)"), start=True, stop=True)
                mm(bank(5)[:, 64:128], ones[:, :], sel.rearrange("p t e -> p (t e)"), start=True, stop=True).then_inc(r_rank, 1)
                for e in range(NE):
                    pe.wait_ge(r_hot, e + 1 + NE * L)
                    chain(bank(3)[:, e:e + 1], ((onesl[e % 2][:, c, :], tokid[:, c:c + 1]) for c in range(NT))).then_inc(r_idx, 1)

            def turn_tile(s):
                for k in range(KC):
                    ins = nc.tensor.transpose(ps[:, k // 4, (k % 4) * P:(k % 4 + 1) * P], xg[s][:, k * P:(k + 1) * P], ident[:, :])
                return ins

            def up_tile(s):
                w = w_up[s].rearrange("p (k n) -> p k n", k=KC)
                return chain(bank(4 + s), ((xgT[s][:, k, :], w[:, k, :]) for k in range(KC)))

            def turn_hidden(s):
                for f in range(2):
                    ins = nc.tensor.transpose(bank(2)[:, f * P:(f + 1) * P], hid[s][:, f * P:(f + 1) * P], ident[:, :])
                return ins

            def down_tile(s):
                w = w_down[s].rearrange("p (f n) -> p f n", f=2)
                for b in range(2):
                    ins = chain(bank(6 + b), ((hidT[s][:, f, :], w[:, f, b * 512:(b + 1) * 512]) for f in range(2)))
                return ins

            def experts_pe(L):
                def turn(e, s, use, reused=True):
                    pe.wait_ge(x_full[s], 16 * use + 8 * NE * L)
                    if reused:
                        pe.wait_ge(x_ev, e + NE * L)
                    turn_tile(s).then_inc(x_tr, 1)

                def up(e, s, use, reused=True):
                    pe.wait_ge(up_full[s], 16 * use + 16 * (NE // 2) * L)
                    if reused:
                        pe.wait_ge(e_hid, e - 1 + NE * L)
                    pe.wait_ge(x_ev, e + 1 + NE * L)
                    up_tile(s).then_inc(e_up, 1)

                def down(e, s, use, reused=True):
                    pe.wait_ge(down_full[s], 16 * use + 16 * (NE // 2) * L)
                    if reused:
                        pe.wait_ge(e_yev, e + NE * L)
                    pe.wait_ge(e_htev, e + 1 + NE * L)
                    down_tile(s).then_inc(e_down, 1)

                def turn_h(e, s, reused=True):
                    if reused:
                        pe.wait_ge(e_htev, e + NE * L)
                    pe.wait_ge(e_hid, e + 1 + NE * L)
                    turn_hidden(s).then_inc(e_ht, 1)

                turn(0, 0, 1, False)
                up(0, 0, 1, False)
                turn(1, 1, 1)
                turn_h(0, 0, False)
                up(1, 1, 1, False)
                turn(2, 0, 2)
                down(0, 0, 1, False)
                turn_h(1, 1)
                with pe.Fori(1, NE // 2 - 1) as i:
                    up(2 * i, 0, i + 1)
                    turn(2 * i + 1, 1, i + 1)
                    down(2 * i - 1, 1, i)
                    turn_h(2 * i, 0)
                    up(2 * i + 1, 1, i + 1)
                    turn(2 * i + 2, 0, i + 2)
                    down(2 * i, 0, i + 1)
                    turn_h(2 * i + 1, 1)
                h8 = NE // 2
                up(NE - 2, 0, h8)
                turn(NE - 1, 1, h8)
                down(NE - 3, 1, h8 - 1)
                turn_h(NE - 2, 0)
                up(NE - 1, 1, h8)
                down(NE - 2, 0, h8)
                turn_h(NE - 1, 1)
                down(NE - 1, 1, h8)

            def overflow(L):
                pe.wait_ge(v_over, 1 + L)
                V = pe.value_load(vcount[0:1, 0:1], min_val=0, max_val=MORE)
                with pe.If(V > 0):
                    with pe.Fori(0, V) as i:
                        pe.wait_ge(v_hot[L], i + 1)
                        chain(bank(3)[:, 0:1], ((onesl[0][:, c, :], tokid[:, c:c + 1]) for c in range(NT))).then_inc(v_idx[L], 1)
                        pe.wait_ge(v_xfull[L], 16 * i + 16)
                        turn_tile(0).then_inc(v_tr[L], 1)
                        pe.wait_ge(v_wfull[L], 32 * i + 32)
                        pe.wait_ge(v_ev[L], i + 1)
                        up_tile(0).then_inc(v_up[L], 1)
                        pe.wait_ge(v_hid[L], i + 1)
                        turn_hidden(0).then_inc(v_ht[L], 1)
                        pe.wait_ge(v_htev[L], i + 1)
                        pe.wait_ge(e_yev, NE + NE * L)
                        down_tile(0).then_inc(v_down[L], 1)

            def relative_bias():
                pe.wait_ge(b_rep, 1)
                for hd in range(HEADS):
                    if hd >= 2:
                        pe.wait_ge(b_ev, hd - 1)
                    mm(bank(hd % 2)[:, 0:REVLEN], relrep[:, hd, :], hotsb, start=True, stop=True).then_inc(b_mm, 1)

            def project_b():
                j = [0]
                for c in range(HEADS // 2):
                    for o in range(2):
                        w = unit(INB + 2 * c + o).rearrange("p (k n) -> p k n", k=KC)
                        for m in range(2):
                            job(bank(4 + j[0] % 4), 4, ((w[:, k, m * P:(m + 1) * P], hnT[:, k, :]) for k in range(KC)))
                            j[0] += 1
                        used(INB + 2 * c + o)
                for c in range(3):
                    w = unit(INB + 6 + c).rearrange("p (k n) -> p k n", k=KC)
                    for t in range(NT):
                        job(bank(4 + j[0] % 4)[:, 0:256], 4, ((hnT[:, k, t * P:(t + 1) * P], w[:, k, :]) for k in range(KC)))
                        j[0] += 1
                    used(INB + 6 + c)
                w = unit(QMB).rearrange("p (k n) -> p k n", k=KC)
                for c in range(2):
                    job(bank(4 + j[0] % 4), 4, ((w[:, k, c * P:(c + 1) * P], hnT[:, k, :]) for k in range(KC)))
                    j[0] += 1
                used(QMB)

            def diff_attention():
                def scores(i):
                    b, hd = STEPS[i]
                    s, nk = i % 2, (b + 1) * P
                    if i >= 2:
                        pe.wait_ge(d_nmx, i - 1)
                    for n in range(2):
                        r = slice(n * DH, (n + 1) * DH)
                        ins = mm(bank(2 * s + n)[:, 0:nk], qT[r, hd, b * P:(b + 1) * P], kT[r, hd, 0:nk], start=True, stop=True)
                    ins.then_inc(d_s, 1)

                def turn(i):
                    b, hd = STEPS[i]
                    s = i % 2
                    pe.wait_ge(d_p, i + 1)
                    if i >= 1:
                        pe.wait_ge(d_ptev, i)
                    for c in range(b + 1):
                        ins = nc.tensor.transpose(bank(4)[:, c * P:(c + 1) * P], E[s][:, 0, c * P:(c + 1) * P], ident[:, :])
                    ins.then_inc(d_pt, 1)

                def values(i):
                    b, hd = STEPS[i]
                    pe.wait_ge(d_ptev, i + 1)
                    if i >= 1:
                        pe.wait_ge(d_oev, i)
                    chain(bank(5)[:, 0:P], ((PTs[i % 2][:, c, :], vB[:, c, hd * P:(hd + 1) * P]) for c in range(b + 1))
                          ).then_inc(d_o, 1)

                def turn_out(b):
                    pe.wait_ge(d_on, b + 1)
                    if b >= 1:
                        pe.wait_ge(d_otev, 2 * b)
                    for j, (a, n) in enumerate(((0, 4), (4, 2))):
                        for c in range(n):
                            ins = nc.tensor.transpose(bank(6 + j)[:, c * P:(c + 1) * P], On[:, a + c, :], ident[:, :])
                        ins.then_inc(d_ot, 1)

                n = len(STEPS)
                pe.wait_ge(job_ev, jobs[0])
                for i in range(n + 2):
                    if i < n:
                        scores(i)
                    if 1 <= i <= n:
                        turn(i - 1)
                    if i >= 2:
                        values(i - 2)
                    if i % HEADS == 4 and i > HEADS:
                        turn_out(i // HEADS - 1)
                turn_out(NT - 1)

            pe.wait_ge(pool_const, 11)
            turn_rows(0)
            pe.wait_ge(n_ev, MT)
            kv(KV0)
            turn_rows(1)
            pe.wait_ge(n_ev, NT + NORM_BASE[1])
            recurrence()
            q_memory(QMA)
            memory_attention(0)
            output(0)
            turn_rows(2, 0)
            routing(0)
            experts_pe(0)
            overflow(0)
            turn_rows(3)
            pe.wait_ge(n_ev, NT + NORM_BASE[3])
            relative_bias()
            project_b()
            diff_attention()
            memory_attention(1)
            output(1)
            turn_rows(4, 1)
            routing(1)
            experts_pe(1)
            overflow(1)


def reversed_buckets(np):
    n = np.maximum(255 - np.arange(REVLEN), 0)
    large = 16 + (np.log(np.maximum(n, 1) / 16) / math.log(8) * 16 + 1e-9).astype(np.int64)
    bucket = np.where(n < 16, n, np.minimum(large, REL - 1))
    hot = np.zeros((REL, REVLEN), np.float32)
    hot[bucket, np.arange(REVLEN)] = 1.0
    return hot


def kernel(**inputs):
    import numpy as np
    import concourse.bacc as bacc
    from concourse.bass_utils import run_bass_kernel_spmd as run

    a = {k: np.asarray(w) for k, w in inputs.items()}

    def by_partition(w):
        return w.reshape(w.shape[0] // P, P, -1).transpose(1, 0, 2).reshape(P, -1)

    units = np.zeros((UNITS, P, UNIT), np.float32)

    def put(n, block):
        units[n, :block.shape[0], :block.shape[1]] = block

    for L, n in ((0, KV0), (1, KV1)):
        for j in range(2):
            put(n + j, by_partition(a["w_mem_kv"][L][:, j * 256:(j + 1) * 256]))
    wa, wb = a["w_in_a"][0], a["w_in_b"][0]
    tok = RB * RW
    for g in range(RB // 2):
        for j in range(2):
            c = j * tok + g * 2 * RW
            put(INA + 2 * g + j, by_partition(wa[:, c:c + 2 * RW]))
    put(QMA, by_partition(wa[:, 2 * tok:2 * tok + 256]))
    for c in range(3):
        for o in range(2):
            put(INB + 2 * c + o, by_partition(wb[:, o * tok + c * 256:o * tok + (c + 1) * 256]))
        put(INB + 6 + c, by_partition(wb[:, 2 * tok + c * 256:2 * tok + (c + 1) * 256]))
    put(QMB, by_partition(wb[:, 3 * tok:3 * tok + 256]))
    oa, ob = a["w_out"]
    for c in range(RB):
        units[OUTA + c // 2, :RW, (c % 2) * D:(c % 2 + 1) * D] = oa[c * RW:(c + 1) * RW]
    put(OUTA + 4, by_partition(oa[tok:]))
    for c in range(4):
        put(OUTB + c, by_partition(ob[c * 256:(c + 1) * 256]))

    experts = np.empty((2, NE, P, EXPW), np.float32)
    up = np.concatenate([a["w_exp1"], a["w_exp3"]], axis=3).reshape(2, NE, KC, P, 2 * DE)
    experts[..., :UPW] = up.transpose(0, 1, 3, 2, 4).reshape(2, NE, P, UPW)
    experts[..., UPW:] = a["w_exp2"].reshape(2, NE, 2, P, D).transpose(0, 1, 3, 2, 4).reshape(2, NE, P, 2 * D)

    vecs = np.zeros((P, NVEC), np.float32)

    def vec(name, block):
        lo, hi = VEC[name]
        vecs[:block.shape[0], lo:hi] = block

    for name, g in (("mix0", a["norm_mix_g"][0]), ("mix1", a["norm_mix_g"][1]), ("ffn0", a["norm_ffn_g"][0]),
                    ("ffn1", a["norm_ffn_g"][1]), ("mem", a["mem_norm_g"])):
        vec(name, g.reshape(KC, P).T)
    vec("subln", a["diff_subln_g"][0].reshape(P, 1))
    vec("conv_w", a["conv_w"][0].reshape(CONV, RB, RW).transpose(2, 1, 0).reshape(RW, RB * CONV))
    for name, key in (("conv_b", "conv_b"), ("gate_a_b", "gate_a_b"), ("gate_x_b", "gate_x_b"), ("lam", "lru_lambda")):
        vec(name, a[key][0].reshape(RB, RW).T)

    router = np.concatenate([a["w_group"], a["w_router"]], axis=2).reshape(2, KC, P, NG + NE).transpose(0, 2, 1, 3)
    gate_w = np.stack([a["gate_a_w"][0], a["gate_x_w"][0]]).transpose(0, 2, 1, 3).reshape(2, RW, RB * RW)
    diff_l = np.concatenate([a[k][0] for k in ("diff_lq1", "diff_lk1", "diff_lq2", "diff_lk2")]).reshape(1, -1)

    arrays = {
        "x": a["x"][0], "mem": a["mem"][0], "units": units, "experts": experts, "gate_w": gate_w, "vecs": vecs,
        "router": router, "diff_l": diff_l, "rel_bias": a["rel_bias"], "final_g": a["final_norm_g"].reshape(1, D),
        "onehot": reversed_buckets(np),
    }
    arrays = {f"in_{k}": np.ascontiguousarray(w) for k, w in arrays.items()}
    nc = bacc.Bacc("TRN2", target_bir_lowering=False, num_devices=1)
    args = [nc.dram_tensor(k, w.shape, mybir.dt.from_np(w.dtype), kind="ExternalInput").ap() for k, w in arrays.items()]
    args.append(nc.dram_tensor("out_0", (T, D), F32, kind="ExternalOutput").ap())
    build(nc, *args)
    r = run(nc, [arrays], core_ids=[0])
    return r.results[0]["out_0"].reshape(1, T, D)
```

```python
import math
from contextlib import ExitStack

import concourse.bass as bass
from concourse import mybir

F32 = mybir.dt.float32
F32R = mybir.dt.float32r
F16 = mybir.dt.float16
I32 = mybir.dt.int32
ALU = mybir.AluOpType
ACT = mybir.ActivationFunctionType
AXX = mybir.AxisListType.X

P = 128
D = 1024
T = 512
NT = T // P
KC = D // P
MEM = 256
MT = MEM // P
DH = 64
RB, RW = 8, 96
CONV = 4
HEADS = 6
NG, EPG = 4, 4
NE = NG * EPG
DE = 256
EPS = 1e-6
REL = 32
NEAR = 2 * P
REVLEN = 384
UNIT = KC * 256
RING = 3
MORE = 2 * T // P - 1
UPW = KC * 2 * DE
EXPW = UPW + 2 * D
LAMBDA_INIT = 0.8 - 0.6 * math.exp(-0.3)
GELU_C = math.sqrt(2.0 / math.pi)
NEG = -1.0e30

KV0, INA, QMA, OUTA = 0, 2, 10, 11
KV1 = OUTA + 5
INB = KV1 + 2
QMB = INB + 9
OUTB = QMB + 1
UNITS = OUTB + 4


def split_before(n):
    return n - 2 if n < KV1 else n - 4


def vec_columns():
    at, out = 0, {}
    for name, n in (("mix0", KC), ("mix1", KC), ("ffn0", KC), ("ffn1", KC), ("mem", KC),
                    ("subln", 1), ("conv_w", RB * CONV), ("conv_b", RB), ("gate_a_b", RB),
                    ("gate_x_b", RB), ("lam", RB)):
        out[name] = (at, at + n)
        at += n
    return out, at


VEC, NVEC = vec_columns()


def build(nc, x, mem, units, experts, gate_w, vecs, router, diff_l, rel_bias, final_g, onehot, out):
    ctx = ExitStack()
    with ctx:
        def sb(name, shape, dt=F32):
            return ctx.enter_context(nc.sbuf_tensor(name, shape, dt))

        def both(name, shape):
            with nc.sbuf_tensor(name, shape, F32) as whole:
                pass
            return whole, sb(f"{name}_low", shape, F32R)

        def sem(name):
            return ctx.enter_context(nc.semaphore(name))

        h = sb("h", [P, NT, D])
        xs_all, cat_low = both("xs_all", [P, 10 * T])
        xs = xs_all[:, 0:NT * D].rearrange("p (t d) -> p t d", t=NT)
        cat = xs_all[:, :].rearrange("p (c t) -> p c t", t=T)
        cat_lo = cat_low[:, :].rearrange("p (c t) -> p c t", t=T)
        hnT, hn_lo = both("hnT", [P, KC, T])
        memT = sb("memT", [P, KC, MEM])
        ring, ring_lo = both("ring", [P, RING, UNIT])
        ring_hi = sb("ring_high", [P, RING, UNIT], F32R)
        expw, expw_part = both("expw", [P, 2, EXPW])
        hn_hi = expw_part[:, 1, 0:KC * T].rearrange("p (k t) -> p k t", k=KC)
        cat_hi = expw_part[:, 1, 0:10 * T].rearrange("p (c t) -> p c t", t=T)
        w_up = [expw[:, s, 0:UPW] for s in range(2)]
        w_down = [expw[:, s, UPW:EXPW] for s in range(2)]
        wgr = sb("wgr", [P, 2, KC, NG + NE])
        arena = sb("arena", [P, 9 * D])
        kvq = sb("kvq", [P, 2 * D])
        kTm = kvq[:, 0:512].rearrange("p (c m) -> p c m", c=2)
        vm = kvq[:, 512:1024].rearrange("p (c m) -> p c m", c=MT)
        qmT = kvq[:, 1024:2048].rearrange("p (c t) -> p c t", c=2)
        ident = sb("ident", [P, P])
        iota = sb("iota", [P, P])
        before = sb("before", [P, P])
        ones = sb("ones", [P, P])
        vec = sb("vec", [P, NVEC])
        small = sb("small", [P, 820])

        def v(name, lo=0, hi=None):
            a, b = VEC[name]
            return vec[:, a + lo:(b if hi is None else a + hi)]

        taken = [0]

        def sm(*shape, dt=None):
            n = 1
            for s in shape:
                n *= s
            a = taken[0]
            taken[0] += n
            assert taken[0] <= 820
            t = small[:, a:a + n]
            if dt is not None:
                t = t.bitcast(dt)
            if len(shape) == 2:
                t = t.rearrange("p (a b) -> p a b", a=shape[0])
            if len(shape) == 3:
                t = t.rearrange("p (a b c) -> p a b c", a=shape[0], b=shape[1])
            return t

        ssq, msq, rstd, mhalf = sm(NT), sm(NT), sm(NT), sm(8)
        mx, nmx, rsum, rec = sm(2, 2), sm(2, 2), sm(2, 2), sm(2, 2)
        lprod, lsum, lexp, neglam = sm(2, DH), sm(2), sm(2), sm(1)
        ossq, orstd, gsub = sm(HEADS), sm(HEADS), sm(1)
        c31 = sm(HEADS)
        iota4, iota16, row16, jcol = sm(4), sm(NE), sm(NE), sm(NE, 3)
        wv1, wv2 = sm(NT), sm(NT)
        r1i, r2i = sm(NT, dt=I32), sm(NT, dt=I32)
        idxi = sm(NE, dt=I32)
        vcount, vsteer = sm(1, dt=I32), sm(1, dt=I32)
        vidx, vc = sm(NE, 3), sm(1)
        rk = sm(NT, NE)
        ntot = sm(NE)
        ovi = sm(1, dt=I32)
        hba, hbx, spl, msp = sm(RB), sm(RB), sm(RB), sm(RB)
        tokid = sb("tokid", [P, NT], F16)

        upad = arena[0:RW, 0:2 * 515].rearrange("p (s n) -> p s n", s=2)
        def ab(i, n=1):
            a = 1040 + 512 * i
            return arena[0:RW, a:a + 512 * n]
        xc = [ab(0), ab(1)]
        ta, tx0, sq, dd, ra0, ra1, gg, gq = (ab(i) for i in range(2, 10))
        ra = [ra0, ra1]
        tx = [tx0, cat[0:RW, RB + 1, :]]
        gw = arena[0:RW, 1040 + 5120:1040 + 5120 + 2 * RB * RW].rearrange("p (s g j) -> p s g j", s=2, g=RB)
        qT = arena[:, 0:3072].rearrange("p (c t) -> p c t", c=HEADS)
        kT = arena[:, 3072:6144].rearrange("p (c t) -> p c t", c=HEADS)
        vB = arena[:, 6144:9216].rearrange("p (t c) -> p t c", t=NT)
        bias = memT[:, :, :].rearrange("p k m -> p (k m)")[:, 0:HEADS * NEAR].rearrange("p (h n) -> p h n", h=HEADS)
        hflat = hnT[:, :, :].rearrange("p k t -> p (k t)")
        E = [hflat[:, s * 1024:(s + 1) * 1024].rearrange("p (n k) -> p n k", n=2) for s in range(2)]
        PTs = [hflat[:, 2048 + s * 512:2560 + s * 512].rearrange("p (c q) -> p c q", c=4) for s in range(2)]
        Osb = hflat[:, 3072:3840].rearrange("p (h d) -> p h d", h=HEADS)
        gfin = hflat[:, 0:D]
        xg = [arena[:, s * D:(s + 1) * D] for s in range(2)]
        xgT = [arena[:, (2 + s) * D:(3 + s) * D].rearrange("p (k t) -> p k t", k=KC) for s in range(2)]
        ysb = [arena[:, (4 + s) * D:(5 + s) * D] for s in range(2)]
        hid = [arena[:, 6144 + s * 256:6400 + s * 256] for s in range(2)]
        tnh = [arena[:, 6656 + s * 256:6912 + s * 256] for s in range(2)]
        hidT = [arena[:, 7168 + s * 256:7424 + s * 256].rearrange("p (f t) -> p f t", f=2) for s in range(2)]
        onesl = [arena[:, 7680 + s * 256:7936 + s * 256].bitcast(F16).rearrange("p (c t) -> p c t", c=NT) for s in range(2)]
        rsc = arena[:, 8192:9216]
        comb = [[arena[:, (2 * s + r) * D:(2 * s + r + 1) * D] for r in range(2)] for s in range(2)]
        lall = arena[:, 6144:6400]
        relsb = arena[0:REL, 6400:6406]
        hotsb = arena[0:REL, 6408:6792]
        relrep = arena[0:REL, 6792:7560].rearrange("p (h m) -> p h m", h=HEADS)
        relrows = arena[:, 7560:8328].rearrange("p (s m) -> p s m", s=2)
        On = xs_all[:, 8 * T:8 * T + HEADS * P].rearrange("p (h d) -> p h d", h=HEADS)

        scr = [0]

        def rt(*shape):
            n = 1
            for k in shape:
                n *= k
            a = scr[0]
            scr[0] += n
            assert scr[0] <= D
            t = rsc[:, a:a + n]
            if len(shape) == 2:
                t = t.rearrange("p (a b) -> p a b", a=shape[0])
            if len(shape) == 3:
                t = t.rearrange("p (a b c) -> p a b c", a=shape[0], b=shape[1])
            return t

        lg = rt(NT, NG + NE)
        r_gmax, r_gi, r_gsum, r_gw, r_m1, r_m2, r_ji, r_den = (rt(NT) for _ in range(8))
        rdiff = rt(NT)
        r_eqg, ohg, rg_e, e_in, r_eqe, oh1, oh2 = (rt(NT, 4) for _ in range(7))
        r_prod = rt(NT, NG, EPG)
        ohe1, ohe2, sel, r_rankv, r_slot, r_cnt = (rt(NT, NE) for _ in range(6))
        r_off, r_base = rt(NT, NE), rt(NE)
        r_over, r_cum = rt(NE, 3), rt(NE, 3)
        r_r1, r_r2 = rt(NT), rt(NT)
        v_m, v_eoh, v_jv, v_rr, v_rk, v_t16, v_es = rt(NE, 3), rt(NE), rt(1), rt(NT, NE), rt(NT), rt(NE), rt(1)

        ps = ctx.enter_context(nc.psum_tensor("ps", [P, 8, 512], F32))

        def bank(i):
            return ps[:, i, :]

        def part(r, n):
            if INA <= n < QMA:
                return r[:, n % RING, :].rearrange("p (k n) -> p k n", n=P)[:, :, 0:RW]
            return r[:, n % RING, :]

        def gelu_bank(c):
            return bank((2, 3, 6)[c % 3])

        xs_d = nc.dram_tensor("xs_rows", [T, D], F32).ap()
        y_d = nc.dram_tensor("expert_rows", [(NE + MORE) * P, D], F32).ap()
        rel_d = nc.dram_tensor("bias_rows", [HEADS, P, REVLEN], F32).ap()

        h_in, mem_in, small_in, gate_in, fin_in = (sem(n) for n in ("h_in", "mem_in", "small_in", "gate_in", "fin_in"))
        pool_const, dve_const = sem("pool_const"), sem("dve_const")
        dve_link, act_link = sem("dve_link"), sem("act_link")
        ring_full = [sem(f"ring_full{i}") for i in range(RING)]
        unit_used, unit_hi, unit_lo = sem("unit_used"), sem("unit_hi"), sem("unit_lo")
        rows_hi, rows_lo, cat_high, cat_lows = sem("rows_hi"), sem("rows_lo"), sem("cat_high"), sem("cat_lows")
        up_full = [sem("up_full0"), sem("up_full1")]
        down_full = [sem("down_full0"), sem("down_full1")]
        n_sq, n_ms, n_rs, n_xs, n_tr, n_ev = (
            sem(n) for n in ("norm_squared", "norm_mean", "norm_rstd", "norm_rows", "norm_turned", "norm_stored"))
        job_mm, job_ev = sem("job_mm"), sem("job_ev")
        a_ux, a_ug, a_gates = sem("a_ux"), sem("a_ug"), sem("a_gates")
        a_uev, a_gsq, a_T, a_sqrt, a_tg = (sem(n) for n in ("a_uev", "a_gsq", "a_T", "a_sqrt", "a_tg"))
        a_xc, a_q, a_g3, a_cat = (sem(n) for n in ("a_xc", "a_q", "a_g3", "a_cat"))
        a_vec, a_exp = sem("a_vec"), sem("a_exp")
        d_s, d_pt, d_o, d_ot = (sem(n) for n in ("d_s", "d_pt", "d_o", "d_ot"))
        d_nmx, d_p, d_ms, d_on = (sem(n) for n in ("d_nmx", "d_p", "d_ms", "d_on"))
        d_exp, d_ptev, d_oev, d_otev = (sem(n) for n in ("d_exp", "d_ptev", "d_oev", "d_otev"))
        d_rs, b_mm, b_ev, b_in, b_mask = (sem(n) for n in ("d_rs", "b_mm", "b_ev", "b_in", "b_mask"))
        b_out = [sem("b_out0"), sem("b_out1")]
        l_sum, l_exp, b_rep, b_load = sem("l_sum"), sem("l_exp"), sem("b_rep"), sem("b_load")
        m_s, m_pt, m_o, m_nmx, m_p, m_exp, m_ptev, m_oev = (
            sem(n) for n in ("m_s", "m_pt", "m_o", "m_nmx", "m_p", "m_exp", "m_ptev", "m_oev"))
        o_mm, o_ev = sem("o_mm"), sem("o_ev")
        xs_out, r_lg, r_lgev, r_exp, r_pexp, r_sel, r_rank, r_hot, r_idx, r_idxi, r_done = (
            sem(n) for n in ("xs_out", "r_lg", "r_lgev", "r_exp", "r_pexp", "r_sel", "r_rank", "r_hot", "r_idx", "r_idxi", "r_done"))
        x_full, y_out, c_full = ([sem(f"{n}{s}") for s in range(2)] for n in ("x_full", "y_out", "c_full"))
        x_tr, x_ev, e_up, e_tanh, e_hid, e_ht, e_htev, e_down, e_yev, e_gate = (
            sem(n) for n in ("x_tr", "x_ev", "e_up", "e_tanh", "e_hid", "e_ht", "e_htev", "e_down", "e_yev", "e_gate"))
        sp_turn, pool_turn = sem("sp_turn"), sem("pool_turn")
        v_over, v_done, c_done = sem("v_over"), sem("v_done"), sem("c_done")
        (v_hot, v_idx, v_idxi, v_xfull, v_tr, v_ev, v_up, v_tanh, v_hid, v_ht, v_htev, v_down,
         v_yev, v_out, v_wfull, v_link, v_free) = (
            [sem(f"{n}{i}") for i in range(2)]
            for n in ("v_hot", "v_idx", "v_idxi", "v_xfull", "v_tr", "v_ev", "v_up", "v_tanh", "v_hid",
                      "v_ht", "v_htev", "v_down", "v_yev", "v_out", "v_wfull", "v_link", "v_free"))
        vec_in, pool_zero, zero_out = sem("vec_in"), sem("pool_zero"), sem("zero_out")
        fin_row, fin_out = sem("fin_row"), sem("fin_out")

        STEPS = [(b, hd) for b in range(NT) for hd in range(HEADS)]
        MSTEPS = [(t, hp) for t in range(NT) for hp in range(2)]
        MS = len(MSTEPS)
        CAT_PAIRS = [(RB + 2) // 2, (HEADS + 2) // 2]
        NORM_TILES = [MT, NT, NT, NT, NT, NT]
        NORM_BASE = [sum(NORM_TILES[:n]) for n in range(6)]

        block = ctx.enter_context(nc.Block())

        @block.sync
        def _(sp):
            sp.dma_start(vec[:, :], vecs).then_inc(vec_in, 16)
            sp.dma_start(xs[:, 0:MT, :], mem.rearrange("(t p) d -> p t d", p=P)).then_inc(mem_in, 16)
            sp.dma_start(h[:, :, :], x.rearrange("(t p) d -> p t d", p=P)).then_inc(h_in, 16)

            def load_unit(n):
                if n >= RING:
                    sp.wait_ge(unit_used, n - RING + 1)
                sp.dma_start(ring[:, n % RING, :], units[n, :, :]).then_inc(ring_full[n % RING], 16)

            def load_up(L, e, s, reused=True):
                if reused:
                    sp.wait_ge(e_up, e - 1 + NE * L)
                src = experts[L, e, :, 0:UPW] if isinstance(e, int) else \
                    experts[L, bass.ds(e, 1), :, 0:UPW].rearrange("o p n -> p (o n)")
                sp.dma_start(w_up[s], src).then_inc(up_full[s], 16)

            def load_down(L, e, s, reused=True):
                if reused:
                    sp.wait_ge(e_down, e - 1 + NE * L)
                src = experts[L, e, :, UPW:EXPW] if isinstance(e, int) else \
                    experts[L, bass.ds(e, 1), :, UPW:EXPW].rearrange("o p n -> p (o n)")
                sp.dma_start(w_down[s], src).then_inc(down_full[s], 16)

            def first_expert(L, e):
                load_up(L, e, e, False)
                load_down(L, e, e, False)

            for n in range(0, QMA):
                load_unit(n)
            first_expert(0, 0)
            for n in range(QMA, KV1 + 2):
                load_unit(n)

            for L in range(2):
                sp.wait_ge(o_mm, NT + NT * L)
                first_expert(L, 1)
                for t in range(NT):
                    sp.wait_ge(n_xs, t + 1 + NORM_BASE[2 + 2 * L])
                    sp.dma_start(xs_d[t * P:(t + 1) * P, :], xs[:, t, :]).then_inc(xs_out, 16)
                load_up(L, 2, 0)
                with sp.Fori(1, NE // 2 - 1) as i:
                    load_up(L, 2 * i + 1, 1)
                    load_down(L, 2 * i, 0)
                    load_up(L, 2 * i + 2, 0)
                    load_down(L, 2 * i + 1, 1)
                load_up(L, NE - 1, 1)
                load_down(L, NE - 2, 0)
                load_down(L, NE - 1, 1)
                if L == 0:
                    for n in range(INB, INB + RING):
                        load_unit(n)
                sp.wait_ge(v_over, 1 + L)
                V = sp.value_load(vcount[0:1, 0:1], min_val=0, max_val=MORE)
                with sp.If(V > 0):
                    sp.sem_inc(v_free[L], 1)
                    with sp.Fori(0, V) as i:
                        sp.wait_ge(v_hot[L], i + 1)
                        sp.sem_inc(sp_turn, 1)
                        ev = sp.value_load(vsteer[0:1, 0:1], min_val=0, max_val=NE - 1)
                        sp.wait_ge(e_down, NE + NE * L)
                        sp.dma_start(w_up[0], experts[L, bass.ds(ev, 1), :, 0:UPW]
                                     .rearrange("o p n -> p (o n)")).then_inc(v_wfull[L], 16)
                        sp.dma_start(w_down[0], experts[L, bass.ds(ev, 1), :, UPW:EXPW]
                                     .rearrange("o p n -> p (o n)")).then_inc(v_wfull[L], 16)
                        sp.wait_ge(v_yev[L], i + 1)
                        sp.dma_start(y_d[bass.ds(i * P + NE * P, P), :], ysb[0]).then_inc(v_out[L], 16)
                        sp.wait_ge(v_out[L], 16 * i + 16)
                        sp.sem_inc(v_free[L], 1)
                sp.sem_inc(v_done, 1)
                if L == 0:
                    sp.wait_ge(c_done, 3)
                    first_expert(1, 0)
                    for n in range(INB + RING, UNITS):
                        load_unit(n)
            for t in range(NT):
                sp.wait_ge(fin_row, t + 1)
                sp.dma_start(out[t * P:(t + 1) * P, :], xs[:, t, :]).then_inc(fin_out, 16)
            sp.wait_ge(fin_out, 16 * NT)

        @block.gpsimd
        def _(pool):
            pool.memset(ones[:, :], 1.0).then_inc(pool_const, 1)
            pool.memset(ident[:, :], 0.0).then_inc(pool_const, 1)
            pool.memset(mhalf, -0.5).then_inc(pool_const, 1)
            pool.wait_ge(pool_const, 3)
            pool.affine_select(out=ident[:, :], in_=ident[:, :], compare_op=ALU.not_equal, fill=1.0, base=0,
                               pattern=[[-1, P]], channel_multiplier=1).then_inc(pool_const, 1)
            pool.affine_select(out=before[:, :], in_=ones[:, :], compare_op=ALU.is_gt, fill=0.0, base=0,
                               pattern=[[1, P]], channel_multiplier=-1).then_inc(pool_const, 1)
            pool.iota(iota[:, :], pattern=[[1, P]], base=0, channel_multiplier=0,
                      allow_small_or_imprecise_dtypes=True).then_inc(pool_const, 1)
            pool.iota(tokid[:, :], pattern=[[P, NT]], base=0, channel_multiplier=1,
                      allow_small_or_imprecise_dtypes=True).then_inc(pool_const, 1)
            pool.iota(iota4, pattern=[[1, 4]], base=-16, channel_multiplier=0,
                      allow_small_or_imprecise_dtypes=True).then_inc(pool_const, 1)
            pool.iota(iota16, pattern=[[1, NE]], base=0, channel_multiplier=0,
                      allow_small_or_imprecise_dtypes=True).then_inc(pool_const, 1)
            pool.iota(row16, pattern=[[P, NE]], base=0, channel_multiplier=0,
                      allow_small_or_imprecise_dtypes=True).then_inc(pool_const, 1)
            pool.iota(jcol, pattern=[[0, NE], [P, 3]], base=P, channel_multiplier=0,
                      allow_small_or_imprecise_dtypes=True).then_inc(pool_const, 1)
            pool.dma_start(gw, gate_w.rearrange("p (s g j) -> p s g j", s=2, g=RB)).then_inc(gate_in, 16)
            pool.dma_start(wgr[:, :, :, :], router.rearrange("p (l k e) -> p l k e", l=2, k=KC)).then_inc(small_in, 16)
            pool.dma_start(c31, rel_bias[REL - 1:REL, :].to_broadcast([P, HEADS])).then_inc(small_in, 16)

            def low(n):
                pool.wait_ge(unit_hi, split_before(n) + 1)
                pool.tensor_tensor(part(ring_lo, n), part(ring, n), part(ring_hi, n).bitcast(F32), ALU.subtract).then_inc(unit_lo, 1)

            def powers(n):
                for t in range(NORM_TILES[n]):
                    pool.wait_ge(n_ms, t + 1 + NORM_BASE[n])
                    pool.tensor_tensor(rstd[:, t:t + 1], msq[:, t:t + 1], mhalf[:, 0:1], ALU.pow).then_inc(n_rs, 1)

            def gather_experts(L):
                pool.wait_ge(xs_out, 16 * NT + 16 * NT * L)
                for e in range(NE):
                    pool.wait_ge(r_idxi, e // 2 + 1 + NE // 2 * L)
                    if e >= 2:
                        pool.wait_ge(x_tr, e - 1 + NE * L)
                    pool.indirect_dma_start(xg[e % 2], None, xs_d, bass.IndirectOffsetOnAxis(ap=idxi[:, e:e + 1], axis=0)
                                            ).then_inc(x_full[e % 2], 16)

            def gather_overflow(L):
                pool.wait_ge(v_over, 1 + L)
                V = pool.value_load(vcount[0:1, 0:1], min_val=0, max_val=MORE)
                with pool.If(V > 0):
                    pool.wait_ge(x_tr, NE + NE * L)
                    with pool.Fori(0, V) as i:
                        pool.wait_ge(v_idxi[L], i + 1)
                        pool.sem_inc(pool_turn, 1)
                        pool.indirect_dma_start(xg[0], None, xs_d, bass.IndirectOffsetOnAxis(ap=ovi, axis=0)
                                                ).then_inc(v_xfull[L], 16)

            def gather_results(L):
                pool.wait_ge(y_out[0], 16 * NE // 2 + 8 * NE * L)
                pool.wait_ge(y_out[1], 16 * NE // 2 + 8 * NE * L)
                pool.wait_ge(r_done, 1 + L)
                pool.wait_ge(v_done, 1 + L)
                for t in range(NT):
                    if t >= 2:
                        pool.wait_ge(c_done, t - 1 + NT * L)
                    for r, ri in enumerate((r1i, r2i)):
                        pool.indirect_dma_start(comb[t % 2][r], None, y_d, bass.IndirectOffsetOnAxis(ap=ri[:, t:t + 1], axis=0)
                                                ).then_inc(c_full[t % 2], 16)

            def zero_rows():
                pool.memset(rsc, 0.0).then_inc(pool_zero, 1)
                pool.wait_ge(pool_zero, 1)
                for j in range(MORE):
                    pool.dma_start(y_d[(NE + j) * P:(NE + j + 1) * P, :], rsc).then_inc(zero_out, 16)

            powers(0)
            low(INA)
            powers(1)
            zero_rows()
            for n in range(INA + 1, KV1):
                low(n)
            powers(2)
            gather_experts(0)
            gather_overflow(0)
            gather_results(0)
            powers(3)
            pool.wait_ge(b_in, 16)
            pool.affine_select(out=bias, in_=bias, compare_op=ALU.is_ge, fill=NEG, base=P,
                               pattern=[[0, HEADS], [-1, NEAR]], channel_multiplier=1).then_inc(b_mask, 1)
            for n in range(INB + RING, OUTB + RING):
                low(n)
            for b in range(NT):
                pool.wait_ge(d_ms, b + 1)
                pool.tensor_tensor(orstd, ossq, mhalf[:, 0:HEADS], ALU.pow).then_inc(d_rs, 1)
            low(OUTB + 3)
            powers(4)
            gather_experts(1)
            gather_overflow(1)
            gather_results(1)
            powers(5)

        @block.scalar
        def _(act):
            links = [0]

            def link(ins):
                links[0] += 1
                ins.then_inc(act_link, 1)
                act.wait_ge(act_link, links[0])

            def norm_squares(n, ready, into):
                for t in range(NORM_TILES[n]):
                    ready(t)
                    act.activation(into(t), (xs if n == 0 else h)[:, t, :], ACT.Square,
                                   accum_out=ssq[:, t:t + 1]).then_inc(n_sq, 1)

            jobs = [0]

            def stored(pairs):
                for dst, src in pairs:
                    n = jobs[0]
                    act.wait_ge(job_mm, n + 1)
                    act.activation(dst, src, ACT.Copy).then_inc(job_ev, 1)
                    jobs[0] += 1

            def high(n):
                act.wait_ge(ring_full[n % RING], 16 * (n // RING + 1))
                act.activation(part(ring_hi, n), part(ring, n), ACT.Copy).then_inc(unit_hi, 1)

            def high_rows(n):
                for t in range(NT):
                    act.wait_ge(n_ev, t + 1 + NORM_BASE[n])
                    act.activation(hn_hi[:, :, t * P:(t + 1) * P], hnT[:, :, t * P:(t + 1) * P], ACT.Copy).then_inc(rows_hi, 1)

            def high_cat(L, j):
                rows = RW if L == 0 and j < RB // 2 else P
                act.activation(cat_hi[0:rows, 2 * j:2 * j + 2, :], cat[0:rows, 2 * j:2 * j + 2, :], ACT.Copy).then_inc(cat_high, 1)

            def kv_jobs():
                stored([(kTm[:, c, :], bank(6 + c)[:, 0:MEM]) for c in range(2)]
                       + [(vm[:, c, :], bank(6 + c)[:, 0:MEM]) for c in range(2)])

            def q_jobs():
                stored([(qmT[:, c, :], bank(6 + c)) for c in range(2)])

            def b_jobs():
                for c in range(HEADS // 2):
                    for dst in (qT, kT):
                        for j in range(2):
                            yield dst[:, 2 * c + j, :], slice(0, T)
                for c in range(3):
                    for t in range(NT):
                        yield vB[:, t, c * 256:(c + 1) * 256], slice(0, 256)
                for c in range(2):
                    yield qmT[:, c, :], slice(0, T)

            def recurrence():
                def first(c):
                    act.wait_ge(a_ux, c + 1)
                    if c >= 2:
                        act.wait_ge(a_xc, c - 1)
                    act.activation(upad[:, c % 2, 3:515], bank(c % 2)[0:RW, :], ACT.Copy).then_inc(a_uev, 1)

                def second(c):
                    act.wait_ge(a_gates, c + 1)
                    if c >= 1:
                        act.wait_ge(a_q, c)
                    if c >= 2:
                        act.wait_ge(a_cat, c - 1)
                    link(act.activation(ta, bank(4)[0:RW, :], ACT.Tanh, bias=hba[0:RW, c:c + 1], scale=0.5))
                    act.activation(tx[c % 2], bank(5)[0:RW, :], ACT.Tanh, bias=hbx[0:RW, c:c + 1], scale=0.5)
                    act.activation(ra[c % 2], ta, ACT.Exp, bias=msp[0:RW, c:c + 1], scale=msp[0:RW, c:c + 1])
                    act.activation(ta, ta, ACT.Tanh, bias=spl[0:RW, c:c + 1], scale=spl[0:RW, c:c + 1]).then_inc(a_T, 1)
                    act.wait_ge(a_ug, c + 1)
                    if c >= 1:
                        act.wait_ge(a_tg, c)
                    act.activation(gq, gelu_bank(c)[0:RW, :], ACT.Square).then_inc(a_gsq, 1)
                    act.wait_ge(a_g3, c + 1)
                    act.activation(gg, gq, ACT.Tanh, scale=GELU_C).then_inc(a_tg, 1)
                    act.wait_ge(a_q, c + 1)
                    act.activation(sq, dd, ACT.Sqrt).then_inc(a_sqrt, 1)

                act.wait_ge(a_vec, 2)
                for c in range(RB):
                    first(c)
                    if c >= 1:
                        second(c - 1)
                    high(INA + c + RING)
                second(RB - 1)

            def memory_attention(L):
                def softmax(i):
                    s = i % 2
                    act.wait_ge(m_nmx, i + 1 + MS * L)
                    if i >= 2:
                        act.wait_ge(m_pt, i - 1 + MS * L)
                    for n in range(2):
                        last = act.activation(E[s][:, n, 0:MEM], bank(2 * s + n)[:, 0:MEM], ACT.Exp,
                                              bias=nmx[:, s, n:n + 1], scale=DH ** -0.5, accum_out=rsum[:, s, n:n + 1])
                    last.then_inc(m_exp, 1)

                def turned(i):
                    s = i % 2
                    act.wait_ge(m_pt, i + 1 + MS * L)
                    if i >= 2:
                        act.wait_ge(m_o, i - 1 + MS * L)
                    act.activation(PTs[s], bank(4 + s).rearrange("p (c q) -> p c q", c=4), ACT.Copy).then_inc(m_ptev, 1)

                def result(i):
                    t, hp = MSTEPS[i]
                    act.wait_ge(m_o, i + 1 + MS * L)
                    act.activation(cat[:, (RB if L == 0 else HEADS) + hp, t * P:(t + 1) * P], bank(6 + i % 2)[:, 0:P], ACT.Copy
                                   ).then_inc(m_oev, 1)

                n = len(MSTEPS)
                done = CAT_PAIRS[L] - 1
                if L == 0:
                    act.wait_ge(a_cat, RB)
                else:
                    act.wait_ge(d_otev, 2 * NT)
                for i in range(n + 2):
                    if i < n:
                        softmax(i)
                    if i < done:
                        high_cat(L, i)
                    if 1 <= i <= n:
                        turned(i - 1)
                    if i >= 2:
                        result(i - 2)
                act.wait_ge(m_oev, MS + MS * L)
                high_cat(L, done)

            def diff_attention():
                def softmax(i):
                    b, hd = STEPS[i]
                    s, nk = i % 2, (b + 1) * P
                    act.wait_ge(d_nmx, i + 1)
                    for n in range(2):
                        last = act.activation(E[s][:, n, 0:nk], E[s][:, n, 0:nk], ACT.Exp, bias=nmx[:, s, n:n + 1],
                                              accum_out=rsum[:, s, n:n + 1])
                    last.then_inc(d_exp, 1)

                def turned(i):
                    b, hd = STEPS[i]
                    s = i % 2
                    act.wait_ge(d_pt, i + 1)
                    if i >= 2:
                        act.wait_ge(d_o, i - 1)
                    act.activation(PTs[s][:, 0:b + 1, :], bank(4).rearrange("p (c q) -> p c q", c=4)[:, 0:b + 1, :],
                                   ACT.Copy).then_inc(d_ptev, 1)

                def result(i):
                    b, hd = STEPS[i]
                    act.wait_ge(d_o, i + 1)
                    if hd == 0 and b >= 1:
                        act.wait_ge(d_on, b)
                    act.activation(Osb[:, hd, :], bank(5)[:, 0:P], ACT.Copy).then_inc(d_oev, 1)

                def block_out(b):
                    for j, (a, n) in enumerate(((0, 4), (4, 2))):
                        act.wait_ge(d_ot, 2 * b + j + 1)
                        act.activation(cat[:, a:a + n, b * P:(b + 1) * P],
                                       bank(6 + j)[:, 0:n * P].rearrange("p (c q) -> p c q", c=n), ACT.Copy,
                                       scale=gsub[:, 0:1]).then_inc(d_otev, 1)

                n = len(STEPS)
                for i in range(n + 2):
                    if i < n:
                        softmax(i)
                    if 1 <= i <= n:
                        turned(i - 1)
                    if i >= 2:
                        result(i - 2)
                        if (i - 2) % HEADS == 3 and i - 2 > HEADS:
                            block_out((i - 2) // HEADS - 1)
                block_out(NT - 1)

            def routing(L):
                act.wait_ge(r_lg, 1 + L)
                act.wait_ge(zero_out, 16 * MORE)
                act.activation(lg, bank(4)[:, 0:NT * (NG + NE)].rearrange("p (t e) -> p t e", t=NT), ACT.Copy).then_inc(r_lgev, 1)
                act.wait_ge(r_exp, 1 + 2 * L)
                act.activation(rg_e, rg_e, ACT.Exp).then_inc(r_pexp, 1)
                act.wait_ge(r_exp, 2 + 2 * L)
                act.activation(rdiff, rdiff, ACT.Exp).then_inc(r_pexp, 1)

            def experts_act(L):
                def first(e, s):
                    act.wait_ge(e_up, e + 1 + NE * L)
                    act.activation(tnh[s], bank(4 + s)[:, 0:DE], ACT.Tanh, scale=0.5).then_inc(e_tanh, 1)

                def turned(e, s):
                    act.wait_ge(e_ht, e + 1 + NE * L)
                    act.activation(hidT[s], bank(2)[:, 0:2 * P].rearrange("p (f t) -> p f t", f=2), ACT.Copy
                                   ).then_inc(e_htev, 1)

                def result(e, s, uses):
                    act.wait_ge(e_down, e + 1 + NE * L)
                    if uses is not None:
                        act.wait_ge(y_out[s], uses + 8 * NE * L)
                    act.activation(ysb[s].rearrange("p (b n) -> p b n", b=2), ps[:, 6:8, :], ACT.Copy).then_inc(e_yev, 1)
                    act.wait_ge(e_yev, e + 1 + NE * L)
                    if isinstance(e, int):
                        act.dma_start(y_d[e * P:(e + 1) * P, :], ysb[s]).then_inc(y_out[s], 16)
                    else:
                        act.dma_start(y_d[bass.ds(e * P, P), :], ysb[s]).then_inc(y_out[s], 16)

                first(0, 0)
                turned(0, 0)
                first(1, 1)
                result(0, 0, None)
                turned(1, 1)
                first(2, 0)
                result(1, 1, None)
                turned(2, 0)
                with act.Fori(1, NE // 2 - 1) as i:
                    first(2 * i + 1, 1)
                    result(2 * i, 0, 16 * i)
                    turned(2 * i + 1, 1)
                    first(2 * i + 2, 0)
                    result(2 * i + 1, 1, 16 * i)
                    turned(2 * i + 2, 0)
                first(NE - 1, 1)
                result(NE - 2, 0, 16 * (NE // 2 - 1))
                turned(NE - 1, 1)
                result(NE - 1, 1, 16 * (NE // 2 - 1))

            def overflow(L):
                act.wait_ge(v_over, 1 + L)
                V = act.value_load(vcount[0:1, 0:1], min_val=0, max_val=MORE)
                with act.If(V > 0):
                    act.wait_ge(y_out[0], 16 * NE // 2 + 8 * NE * L)
                    with act.Fori(0, V) as i:
                        act.wait_ge(v_up[L], i + 1)
                        act.activation(tnh[0], bank(4)[:, 0:DE], ACT.Tanh, scale=0.5).then_inc(v_tanh[L], 1)
                        act.wait_ge(v_ht[L], i + 1)
                        act.activation(hidT[0], bank(2)[:, 0:2 * P].rearrange("p (f t) -> p f t", f=2), ACT.Copy
                                       ).then_inc(v_htev[L], 1)
                        act.wait_ge(v_down[L], i + 1)
                        act.activation(ysb[0].rearrange("p (b n) -> p b n", b=2), ps[:, 6:8, :], ACT.Copy
                                       ).then_inc(v_yev[L], 1)

            act.wait_ge(a_vec, 1)
            act.activation(spl[0:RW, :], spl[0:RW, :], ACT.Exp, scale=-1.0).then_inc(a_exp, 1)
            norm_squares(0, lambda t: act.wait_ge(mem_in, 16), lambda t: hflat[:, t * D:(t + 1) * D])
            high(INA)
            act.wait_ge(h_in, 16)
            norm_squares(1, lambda t: act.wait_ge(n_tr, MT), lambda t: xs[:, t, :])
            kv_jobs()
            high_rows(1)
            high(INA + 1)
            high(INA + 2)
            recurrence()
            q_jobs()
            high(OUTA + 2)
            memory_attention(0)
            high(OUTA + 3)
            high(OUTA + 4)
            norm_squares(2, lambda t: act.wait_ge(o_ev, t + 1), lambda t: xs[:, t, :])
            routing(0)
            kv_jobs()
            experts_act(0)
            overflow(0)
            for n in range(RING):
                high(INB + n)
            norm_squares(3, lambda t: act.wait_ge(c_done, t + 1), lambda t: xs[:, t, :])
            high_rows(3)
            act.dma_start(lall, diff_l.to_broadcast([P, 4 * DH])).then_inc(b_load, 16)
            act.dma_start(relsb, rel_bias).then_inc(b_load, 16)
            act.dma_start(hotsb, onehot).then_inc(b_load, 16)
            act.wait_ge(l_sum, 1)
            act.activation(lexp, lsum, ACT.Exp).then_inc(l_exp, 1)
            for hd in range(HEADS):
                act.wait_ge(b_mm, hd + 1)
                if hd >= 2:
                    act.wait_ge(b_out[hd % 2], 16 * (hd // 2))
                act.activation(relrows[:, hd % 2, :], bank(hd % 2)[:, 0:REVLEN], ACT.Copy).then_inc(b_ev, 1)
                act.wait_ge(b_ev, hd + 1)
                act.dma_start(rel_d[hd, :, :], relrows[:, hd % 2, :]).then_inc(b_out[hd % 2], 16)
            for o in b_out:
                act.wait_ge(o, 16 * HEADS // 2)
            skew = rel_d.rearrange("h p m -> h (p m)")[:, P - 1:P - 1 + (REVLEN - 1) * P] \
                .rearrange("h (q c) -> q h c", c=REVLEN - 1)[:, :, 0:NEAR]
            act.dma_start(bias, skew).then_inc(b_in, 16)
            pairs = [(dst, bank(4 + j % 4)[:, cols]) for j, (dst, cols) in enumerate(b_jobs())]
            for k in range(10):
                of_unit = NT if 6 <= k < 9 else 2
                stored(pairs[:of_unit])
                pairs = pairs[of_unit:]
                high(INB + k + RING)
            diff_attention()
            memory_attention(1)
            high(OUTB + 3)
            norm_squares(4, lambda t: act.wait_ge(o_ev, t + 1 + NT), lambda t: xs[:, t, :])
            routing(1)
            experts_act(1)
            overflow(1)
            act.dma_start(gfin, final_g.to_broadcast([P, D])).then_inc(fin_in, 16)
            norm_squares(5, lambda t: act.wait_ge(c_done, t + 1 + NT), lambda t: xs[:, t, :])

        @block.vector
        def _(dve):
            links = [0]

            def link(ins):
                links[0] += 1
                ins.then_inc(dve_link, 1)
                dve.wait_ge(dve_link, links[0])

            def low(n):
                dve.wait_ge(unit_hi, split_before(n) + 1)
                dve.tensor_tensor(part(ring_lo, n), part(ring, n), part(ring_hi, n).bitcast(F32), ALU.subtract).then_inc(unit_lo, 1)

            def low_rows(L, t):
                cols = slice(t * P, (t + 1) * P)
                dve.wait_ge(rows_hi, t + 1 + NT * L)
                dve.tensor_tensor(hn_lo[:, :, cols], hnT[:, :, cols], hn_hi[:, :, cols].bitcast(F32), ALU.subtract
                                  ).then_inc(rows_lo, 1)

            def low_cat(L, j):
                rows = RW if L == 0 and j < RB // 2 else P
                pair = slice(2 * j, 2 * j + 2)
                dve.wait_ge(cat_high, j + 1 + CAT_PAIRS[0] * L)
                dve.tensor_tensor(cat_lo[0:rows, pair, :], cat[0:rows, pair, :], cat_hi[0:rows, pair, :].bitcast(F32),
                                  ALU.subtract).then_inc(cat_lows, 1)

            def norm(n, src, turned, g):
                nt = NORM_TILES[n]
                for t in range(nt + 1):
                    if t < nt:
                        dve.wait_ge(n_sq, t + 1 + NORM_BASE[n])
                        dve.tensor_scalar(msq[:, t:t + 1], ssq[:, t:t + 1], 1.0 / D, EPS, ALU.mult, ALU.add
                                          ).then_inc(n_ms, 1)
                        dve.wait_ge(n_rs, t + 1 + NORM_BASE[n])
                        dve.tensor_scalar(xs[:, t, :], src[:, t, :], rstd[:, t:t + 1], None, ALU.mult
                                          ).then_inc(n_xs, 1)
                    if t >= 1:
                        b = 2 * ((t - 1) % 2)
                        dve.wait_ge(n_tr, t + NORM_BASE[n])
                        dve.tensor_tensor(turned[:, :, (t - 1) * P:t * P],
                                          ps[:, b:b + 2, :].rearrange("p b (k t) -> p (b k) t", k=KC // 2),
                                          v(g).unsqueeze(2).to_broadcast([P, KC, P]), ALU.mult).then_inc(n_ev, 1)
                    if t >= 2 and n in (1, 3):
                        low_rows(n // 2, t - 2)
                if n in (1, 3):
                    low_rows(n // 2, nt - 1)

            def absolute_lambda():
                lam, z = v("lam")[0:RW, :], hbx[0:RW, :]
                link(dve.tensor_scalar(z, lam, -1.0, None, ALU.mult))
                dve.tensor_tensor(spl[0:RW, :], lam, z, ALU.max).then_inc(a_vec, 1)

            def channel_vectors():
                lam, s, z, z2 = v("lam")[0:RW, :], hba[0:RW, :], hbx[0:RW, :], msp[0:RW, :]
                sp = spl[0:RW, :]
                dve.wait_ge(a_exp, 1)
                link(dve.tensor_scalar(z, sp, 2.0, None, ALU.add))
                link(dve.reciprocal(z, z))
                link(dve.tensor_tensor(z, z, sp, ALU.mult))
                link(dve.tensor_tensor(z2, z, z, ALU.mult))
                link(dve.tensor_scalar(s, z2, 1.0 / 19, None, ALU.mult))
                for k in range(17, 1, -2):
                    link(dve.scalar_tensor_tensor(s, s, 1.0 / k, z2, ALU.add, ALU.mult))
                link(dve.tensor_scalar(s, s, 1.0, 4.0, ALU.add, ALU.mult))
                link(dve.tensor_tensor(s, s, z, ALU.mult))
                link(dve.tensor_scalar(z, lam, -1.0, 0.0, ALU.mult, ALU.max))
                link(dve.scalar_tensor_tensor(sp, z, 2.0, s, ALU.mult, ALU.add))
                link(dve.tensor_scalar(sp, sp, 2.0, None, ALU.mult))
                dve.tensor_scalar(msp[0:RW, :], sp, -1.0, None, ALU.mult)
                link(dve.tensor_scalar(hba[0:RW, :], v("gate_a_b")[0:RW, :], 0.5, None, ALU.mult))
                dve.tensor_scalar(hbx[0:RW, :], v("gate_x_b")[0:RW, :], 0.5, None, ALU.mult).then_inc(a_vec, 1)

            def recurrence():
                def conv(c):
                    u, o = upad[:, c % 2, :], xc[c % 2]
                    w = v("conv_w", c * CONV, (c + 1) * CONV)[0:RW, :]
                    dve.wait_ge(a_uev, c + 1)
                    if c >= 2:
                        dve.wait_ge(a_gates, c - 1)
                        dve.wait_ge(a_cat, c - 1)
                    link(dve.tensor_scalar(o, u[:, 0:T], w[:, 0:1], v("conv_b", c, c + 1)[0:RW, :], ALU.mult, ALU.add))
                    for j in range(1, CONV):
                        ins = dve.scalar_tensor_tensor(o, u[:, j:j + T], w[:, j:j + 1], o, ALU.mult, ALU.add)
                        if j < CONV - 1:
                            link(ins)
                    ins.then_inc(a_xc, 1)

                def decay(c):
                    ug = gelu_bank(c)[0:RW, :]
                    dve.wait_ge(a_T, c + 1)
                    if c >= 1:
                        dve.wait_ge(a_sqrt, c)
                    link(dve.tensor_tensor(dd, ra[c % 2], ra[c % 2], ALU.mult))
                    dve.scalar_tensor_tensor(dd, dd, 1.0, ta, ALU.add, ALU.mult).then_inc(a_q, 1)
                    dve.wait_ge(a_gsq, c + 1)
                    link(dve.tensor_scalar(gq, gq, 0.044715, 1.0, ALU.mult, ALU.add))
                    dve.tensor_tensor(gq, gq, ug, ALU.mult).then_inc(a_g3, 1)
                    link(dve.scalar_tensor_tensor(tx[c % 2], tx[c % 2], 1.0, xc[c % 2], ALU.add, ALU.mult))

                def scan(c):
                    ug = gelu_bank(c)[0:RW, :]
                    b = tx[c % 2]
                    dve.wait_ge(a_tg, c + 1)
                    dve.scalar_tensor_tensor(gg, gg, 1.0, ug, ALU.add, ALU.mult)
                    dve.wait_ge(a_sqrt, c + 1)
                    link(dve.scalar_tensor_tensor(b, b, 0.5, sq, ALU.mult, ALU.mult))
                    link(dve.tensor_tensor_scan(sq, ra[c % 2], b, 0.0, ALU.mult, ALU.add))
                    dve.scalar_tensor_tensor(cat[0:RW, c, :], sq, 0.5, gg, ALU.mult, ALU.mult).then_inc(a_cat, 1)

                for c in range(RB + 2):
                    if c >= 2:
                        scan(c - 2)
                    if c < RB:
                        conv(c)
                    if 1 <= c <= RB:
                        decay(c - 1)

            def memory_attention(L):
                n = len(MSTEPS)
                done = CAT_PAIRS[L] - 1
                for i in range(n + 1):
                    if i < n:
                        s = i % 2
                        dve.wait_ge(m_s, i + 1 + MS * L)
                        link(dve.tensor_reduce(mx[:, s, :], ps[:, 2 * s:2 * s + 2, 0:MEM], AXX, ALU.max))
                        dve.tensor_scalar(nmx[:, s, :], mx[:, s, :], -DH ** -0.5, None, ALU.mult).then_inc(m_nmx, 1)
                    if i >= 1:
                        s = (i - 1) % 2
                        dve.wait_ge(m_exp, i + MS * L)
                        link(dve.reciprocal(rec[:, s, :], rsum[:, s, :]))
                        dve.tensor_tensor(E[s][:, :, 0:MEM], E[s][:, :, 0:MEM],
                                          rec[:, s, :].unsqueeze(2).to_broadcast([P, 2, MEM]), ALU.mult).then_inc(m_p, 1)
                    if i < done:
                        low_cat(L, i)
                low_cat(L, done)

            def output(L):
                for t in range(NT):
                    dve.wait_ge(o_mm, t + 1 + NT * L)
                    ht = h[:, t, :].rearrange("p (b n) -> p b n", b=2)
                    dve.tensor_tensor(ht, ps[:, 2 * t:2 * t + 2, :], ht, ALU.add).then_inc(o_ev, 1)

            def routing(L):
                def bc(a, axis, shape):
                    return a.unsqueeze(axis).to_broadcast(shape)

                def first_max(src, n_max, eq, ji, oh):
                    link(dve.tensor_reduce(n_max, src, AXX, ALU.max))
                    link(dve.tensor_tensor(eq, src, bc(n_max, 2, [P, NT, 4]), ALU.is_equal))
                    link(dve.tensor_tensor(eq, eq, bc(iota4, 1, [P, NT, 4]), ALU.mult))
                    link(dve.tensor_reduce(ji, eq, AXX, ALU.min))
                    link(dve.tensor_tensor(oh, bc(iota4, 1, [P, NT, 4]), bc(ji, 2, [P, NT, 4]), ALU.is_equal))

                dve.wait_ge(r_lgev, 1 + L)
                g, el = lg[:, :, 0:NG], lg[:, :, NG:NG + NE]
                first_max(g, r_gmax, r_eqg, r_gi, ohg)
                dve.tensor_tensor(rg_e, g, bc(r_gmax, 2, [P, NT, NG]), ALU.subtract).then_inc(r_exp, 1)
                for t in range(NT):
                    last = dve.tensor_tensor(r_prod[:, t, :, :], el[:, t, :].rearrange("p (g j) -> p g j", g=NG),
                                             bc(ohg[:, t, :], 2, [P, NG, EPG]), ALU.mult)
                link(last)
                link(dve.tensor_reduce(e_in, r_prod.rearrange("p t g j -> p t j g"), AXX, ALU.add))
                first_max(e_in, r_m1, r_eqe, r_ji, oh1)
                link(dve.scalar_tensor_tensor(e_in, oh1, NEG, e_in, ALU.mult, ALU.add))
                first_max(e_in, r_m2, r_eqe, r_ji, oh2)
                dve.tensor_tensor(rdiff, r_m2, r_m1, ALU.subtract).then_inc(r_exp, 1)
                for t in range(NT):
                    for o, oh in ((ohe1, oh1), (ohe2, oh2)):
                        last = dve.tensor_tensor(o[:, t, :].rearrange("p (g j) -> p g j", g=NG),
                                                 bc(ohg[:, t, :], 2, [P, NG, EPG]), bc(oh[:, t, :], 1, [P, NG, EPG]), ALU.mult)
                link(last)
                dve.tensor_tensor(sel, ohe1, ohe2, ALU.add).then_inc(r_sel, 1)
                dve.wait_ge(r_pexp, 1 + 2 * L)
                link(dve.tensor_reduce(r_gsum, rg_e, AXX, ALU.add))
                link(dve.reciprocal(r_gw, r_gsum))
                dve.wait_ge(r_pexp, 2 + 2 * L)
                link(dve.tensor_scalar(r_den, rdiff, 1.0, None, ALU.add))
                link(dve.reciprocal(r_den, r_den))
                link(dve.tensor_tensor(wv1, r_den, r_gw, ALU.mult))
                link(dve.tensor_tensor(wv2, rdiff, wv1, ALU.mult))
                dve.wait_ge(r_rank, 1 + L)
                link(dve.tensor_copy(r_cnt, bank(5)[:, 64:128].rearrange("p (t e) -> p t e", t=NT)))
                link(dve.tensor_scalar(r_off[:, 0, :], r_cnt[:, 0, :], 0.0, None, ALU.mult))
                for t in range(1, NT):
                    link(dve.tensor_tensor(r_off[:, t, :], r_off[:, t - 1, :], r_cnt[:, t - 1, :], ALU.add))
                link(dve.tensor_tensor(ntot, r_off[:, NT - 1, :], r_cnt[:, NT - 1, :], ALU.add))
                link(dve.tensor_tensor(r_rankv, bank(5)[:, 0:64].rearrange("p (t e) -> p t e", t=NT), r_off, ALU.add))
                link(dve.scalar_tensor_tensor(rk, r_rankv, 1.0, sel, ALU.add, ALU.mult))
                link(dve.tensor_scalar(rk, rk, -1.0, None, ALU.add))

                def hot(e):
                    if e >= 2:
                        dve.wait_ge(r_idx, e - 1 + NE * L)
                    dve.tensor_tensor(onesl[e % 2], bc(iota[:, :], 1, [P, NT, P]), bc(rk[:, :, e], 2, [P, NT, P]), ALU.is_equal
                                      ).then_inc(r_hot, 1)

                hot(0)
                hot(1)
                dve.wait_ge(r_idx, 2 + NE * L)
                dve.tensor_copy(idxi[:, 0:2], bank(3)[:, 0:2]).then_inc(r_idxi, 1)
                hot(2)
                hot(3)
                dve.wait_ge(r_idx, 4 + NE * L)
                dve.tensor_copy(idxi[:, 2:4], bank(3)[:, 2:4]).then_inc(r_idxi, 1)

            def hot_pair(L, e):
                for s in range(2):
                    dve.wait_ge(r_idx, e + s - 1 + NE * L)
                    dve.tensor_tensor(onesl[s], iota[:, :].unsqueeze(1).to_broadcast([P, NT, P]),
                                      rk[:, :, bass.ds(e + s, 1)].to_broadcast([P, NT, P]), ALU.is_equal).then_inc(r_hot, 1)
                dve.wait_ge(r_idx, e + 2 + NE * L)
                dve.tensor_copy(idxi[:, bass.ds(e, 2)], bank(3)[:, 0:2]).then_inc(r_idxi, 1)

            def slots(L):
                def bc(a, axis, shape):
                    return a.unsqueeze(axis).to_broadcast(shape)

                for j in range(1, NT):
                    last = dve.tensor_scalar(r_over[:, :, j - 1], ntot, float(j * P), None, ALU.is_gt)
                link(last)
                flat = r_over.rearrange("p e j -> p (e j)")
                cum = r_cum.rearrange("p e j -> p (e j)")
                link(dve.tensor_tensor_scan(cum, ones[:, 0:NE * 3], flat, 0.0, ALU.mult, ALU.add))
                link(dve.tensor_tensor(vidx, r_cum, r_over, ALU.mult))
                link(dve.memset(vc, 0.0))
                dve.tensor_copy(vcount, cum[:, NE * 3 - 1:NE * 3]).then_inc(v_over, 1)
                link(dve.tensor_tensor(r_base, r_cum[:, :, 0], r_over[:, :, 0], ALU.subtract))
                link(dve.tensor_scalar(r_base, r_base, float(P), float((NE - 1) * P), ALU.mult, ALU.add))
                link(dve.tensor_tensor(r_base, r_base, row16, ALU.subtract))
                link(dve.tensor_scalar(r_slot, r_rankv, float(P), None, ALU.is_ge))
                link(dve.tensor_tensor(r_slot, r_slot, bc(r_base, 1, [P, NT, NE]), ALU.mult))
                link(dve.tensor_tensor(r_slot, r_slot, r_rankv, ALU.add))
                link(dve.tensor_tensor(r_slot, r_slot, bc(row16, 1, [P, NT, NE]), ALU.add))
                link(dve.tensor_tensor(ohe1, ohe1, r_slot, ALU.mult))
                link(dve.tensor_tensor(ohe2, ohe2, r_slot, ALU.mult))
                link(dve.tensor_reduce(r_r1, ohe1, AXX, ALU.add))
                link(dve.tensor_reduce(r_r2, ohe2, AXX, ALU.add))
                link(dve.tensor_copy(r1i, r_r1))
                dve.tensor_copy(r2i, r_r2).then_inc(r_done, 1)

            def turned_rows(L, s):
                return dve.tensor_tensor(xgT[s], ps[:, 0:2, :].rearrange("p b (k t) -> p (b k) t", k=KC // 2),
                                         v(f"ffn{L}").unsqueeze(2).to_broadcast([P, KC, P]), ALU.mult)

            def gated(s):
                return dve.scalar_tensor_tensor(tnh[s], tnh[s], 1.0, bank(4 + s)[:, 0:DE], ALU.add, ALU.mult)

            def hidden(s):
                return dve.scalar_tensor_tensor(hid[s], tnh[s], 0.5, bank(4 + s)[:, DE:2 * DE], ALU.mult, ALU.mult)

            def experts_dve(L):
                def rows(e, s, reused=True):
                    dve.wait_ge(x_tr, e + 1 + NE * L)
                    if reused:
                        dve.wait_ge(e_up, e - 1 + NE * L)
                    turned_rows(L, s).then_inc(x_ev, 1)

                def hidden_of(e, s, reused=True):
                    dve.wait_ge(e_tanh, e + 1 + NE * L)
                    gated(s).then_inc(e_gate, 1)
                    if reused:
                        dve.wait_ge(e_ht, e - 1 + NE * L)
                    dve.wait_ge(e_gate, e + 1 + NE * L)
                    hidden(s).then_inc(e_hid, 1)

                rows(0, 0, False)
                hidden_of(0, 0, False)
                rows(1, 1, False)
                hidden_of(1, 1, False)
                rows(2, 0)
                slots(L)
                with dve.Fori(1, NE // 2 - 1) as i:
                    hot_pair(L, 2 * i + 2)
                    hidden_of(2 * i, 0)
                    rows(2 * i + 1, 1)
                    hidden_of(2 * i + 1, 1)
                    rows(2 * i + 2, 0)
                hidden_of(NE - 2, 0)
                rows(NE - 1, 1)
                hidden_of(NE - 1, 1)

            def overflow(L):
                dve.wait_ge(v_over, 1 + L)
                V = dve.value_load(vcount[0:1, 0:1], min_val=0, max_val=MORE)
                steps = 12
                with dve.If(V > 0):
                    with dve.Fori(0, V) as i:
                        at = [0]

                        def vlink(ins):
                            at[0] += 1
                            ins.then_inc(v_link[L], 1)
                            dve.wait_ge(v_link[L], i * steps + at[0])

                        dve.wait_ge(v_free[L], i + 1)
                        vlink(dve.tensor_scalar(vc, vc, 1.0, None, ALU.add))
                        vlink(dve.tensor_scalar(v_m, vidx, vc, None, ALU.is_equal))
                        vlink(dve.tensor_reduce(v_eoh, v_m, AXX, ALU.add))
                        vlink(dve.tensor_tensor(v_m, v_m, jcol, ALU.mult))
                        vlink(dve.tensor_reduce(v_jv, v_m.rearrange("p e j -> p (e j)"), AXX, ALU.add))
                        vlink(dve.tensor_tensor(v_rr, rk, v_eoh.unsqueeze(1).to_broadcast([P, NT, NE]), ALU.mult))
                        vlink(dve.tensor_reduce(v_rk, v_rr, AXX, ALU.add))
                        vlink(dve.tensor_scalar(v_rk, v_rk, v_jv, None, ALU.subtract))
                        vlink(dve.tensor_tensor(v_t16, v_eoh, iota16, ALU.mult))
                        vlink(dve.tensor_reduce(v_es, v_t16, AXX, ALU.add))
                        vlink(dve.tensor_copy(vsteer, v_es))
                        dve.tensor_tensor(onesl[0], iota[:, :].unsqueeze(1).to_broadcast([P, NT, P]),
                                          v_rk.unsqueeze(2).to_broadcast([P, NT, P]), ALU.is_equal).then_inc(v_hot[L], 1)
                        dve.wait_ge(v_idx[L], i + 1)
                        dve.tensor_copy(ovi, bank(3)[:, 0:1]).then_inc(v_idxi[L], 1)
                        dve.wait_ge(v_tr[L], i + 1)
                        turned_rows(L, 0).then_inc(v_ev[L], 1)
                        dve.wait_ge(v_tanh[L], i + 1)
                        vlink(gated(0))
                        assert at[0] == steps
                        hidden(0).then_inc(v_hid[L], 1)

            def combine(L):
                for t in range(NT):
                    dve.wait_ge(c_full[t % 2], 32 * (t // 2 + 1) + 32 * (NT // 2) * L)
                    link(dve.scalar_tensor_tensor(h[:, t, :], comb[t % 2][0], wv1[:, t:t + 1], h[:, t, :], ALU.mult, ALU.add))
                    dve.scalar_tensor_tensor(h[:, t, :], comb[t % 2][1], wv2[:, t:t + 1], h[:, t, :], ALU.mult, ALU.add
                                             ).then_inc(c_done, 1)

            def lambda_and_bias():
                dve.wait_ge(b_load, 48)
                lv = lall.rearrange("p (a b d) -> p a b d", a=2, b=2)
                link(dve.tensor_tensor(lprod, lv[:, :, 0, :], lv[:, :, 1, :], ALU.mult))
                dve.tensor_reduce(lsum, lprod, AXX, ALU.add).then_inc(l_sum, 1)
                dve.tensor_copy(relrep, relsb.unsqueeze(2).to_broadcast([REL, HEADS, P])).then_inc(b_rep, 1)
                dve.wait_ge(l_exp, 1)
                link(dve.tensor_tensor(neglam, lexp[:, 1:2], lexp[:, 0:1], ALU.subtract))
                link(dve.tensor_scalar(neglam, neglam, -LAMBDA_INIT, None, ALU.add))
                link(dve.tensor_scalar(gsub, v("subln"), 1.0 - LAMBDA_INIT, None, ALU.mult))

            def diff_attention():
                def scores(i):
                    b, hd = STEPS[i]
                    s, nk = i % 2, (b + 1) * P
                    near = min(nk, NEAR)
                    far = nk - near
                    S = ps[:, 2 * s:2 * s + 2, :]
                    dve.wait_ge(d_s, i + 1)
                    if i >= 2:
                        dve.wait_ge(d_pt, i - 1)
                    last = dve.scalar_tensor_tensor(E[s][:, :, far:nk], S[:, :, far:nk], DH ** -0.5,
                                                    bias[:, hd, NEAR - near:NEAR].unsqueeze(1).to_broadcast([P, 2, near]),
                                                    ALU.mult, ALU.add)
                    if far:
                        last = dve.tensor_scalar(E[s][:, :, 0:far], S[:, :, 0:far], DH ** -0.5, c31[:, hd:hd + 1],
                                                 ALU.mult, ALU.add)
                    link(last)
                    link(dve.tensor_reduce(mx[:, s, :], E[s][:, :, 0:nk], AXX, ALU.max))
                    dve.tensor_scalar(nmx[:, s, :], mx[:, s, :], -1.0, None, ALU.mult).then_inc(d_nmx, 1)

                def weights(i):
                    b, hd = STEPS[i]
                    s, nk = i % 2, (b + 1) * P
                    dve.wait_ge(d_exp, i + 1)
                    link(dve.reciprocal(rec[:, s, :], rsum[:, s, :]))
                    link(dve.tensor_tensor(rec[:, s, 1:2], rec[:, s, 1:2], neglam, ALU.mult))
                    link(dve.tensor_scalar(E[s][:, 0, 0:nk], E[s][:, 0, 0:nk], rec[:, s, 0:1], None, ALU.mult))
                    dve.scalar_tensor_tensor(E[s][:, 0, 0:nk], E[s][:, 1, 0:nk], rec[:, s, 1:2], E[s][:, 0, 0:nk],
                                             ALU.mult, ALU.add).then_inc(d_p, 1)

                def subnorm(b):
                    dve.wait_ge(d_oev, HEADS * (b + 1))
                    if b >= 1:
                        dve.wait_ge(d_ot, 2 * b)
                    link(dve.tensor_tensor(On, Osb, Osb, ALU.mult))
                    link(dve.tensor_reduce(ossq, On, AXX, ALU.add))
                    dve.tensor_scalar(ossq, ossq, 1.0 / P, EPS, ALU.mult, ALU.add).then_inc(d_ms, 1)
                    dve.wait_ge(d_rs, b + 1)
                    dve.tensor_tensor(On, Osb, orstd.unsqueeze(2).to_broadcast([P, HEADS, P]), ALU.mult).then_inc(d_on, 1)

                n = len(STEPS)
                dve.wait_ge(small_in, 32)
                dve.wait_ge(b_mask, 1)
                for i in range(n + 1):
                    if i < n:
                        scores(i)
                    if i >= 1:
                        weights(i - 1)
                    if i % HEADS == 2 and i > HEADS:
                        subnorm(i // HEADS - 1)
                subnorm(NT - 1)

            dve.wait_ge(vec_in, 16)
            dve.memset(upad[:, :, 0:3], 0.0).then_inc(dve_const, 1)
            absolute_lambda()
            norm(0, xs, memT, "mem")
            norm(1, h, hnT, "mix0")
            channel_vectors()
            recurrence()
            memory_attention(0)
            output(0)
            norm(2, h, hnT, "ffn0")
            routing(0)
            experts_dve(0)
            overflow(0)
            for n in range(RING):
                low(INB + n)
            combine(0)
            norm(3, h, hnT, "mix1")
            lambda_and_bias()
            diff_attention()
            memory_attention(1)
            output(1)
            norm(4, h, hnT, "ffn1")
            routing(1)
            experts_dve(1)
            overflow(1)
            combine(1)
            dve.wait_ge(fin_in, 16)
            for t in range(NT):
                dve.wait_ge(n_sq, t + 1 + NORM_BASE[5])
                dve.tensor_scalar(msq[:, t:t + 1], ssq[:, t:t + 1], 1.0 / D, EPS, ALU.mult, ALU.add).then_inc(n_ms, 1)
                dve.wait_ge(n_rs, t + 1 + NORM_BASE[5])
                dve.scalar_tensor_tensor(xs[:, t, :], h[:, t, :], rstd[:, t:t + 1], gfin, ALU.mult, ALU.mult
                                         ).then_inc(fin_row, 1)

        @block.tensor
        def _(pe):
            mm = nc.tensor.matmul
            ALL = slice(None)
            hn, cats = (hn_hi, hn_lo), (cat_hi, cat_lo)

            def whole_unit(n):
                pe.wait_ge(ring_full[n % RING], 16 * (n // RING + 1))
                return ring[:, n % RING, :]

            def unit(n, k=KC):
                pe.wait_ge(unit_lo, split_before(n) + 1)
                return [r[:, n % RING, :].rearrange("p (k n) -> p k n", k=k) for r in (ring_hi, ring_lo)]

            def both_of(parts, *at):
                return tuple(part[at] for part in parts)

            def passes(pairs):
                for (wh, wl), (mh, ml) in pairs:
                    yield wh, mh
                    yield wh, ml
                    yield wl, mh

            def chain(dst, pairs):
                pairs = list(pairs)
                for k, (lhsT, rhs) in enumerate(pairs):
                    ins = mm(dst, lhsT, rhs, start=(k == 0), stop=(k == len(pairs) - 1))
                return ins

            def turn_rows(n, L=None):
                for t in range(NORM_TILES[n]):
                    b = 2 * (t % 2)
                    pe.wait_ge(n_xs, t + 1 + NORM_BASE[n])
                    if t >= 2:
                        pe.wait_ge(n_ev, t - 1 + NORM_BASE[n])
                    elif t == 1 and L is not None:
                        pe.wait_ge(o_ev, 2 + NT * L)
                    for k in range(KC):
                        ins = nc.tensor.transpose(ps[:, b + k // 4, (k % 4) * P:(k % 4 + 1) * P],
                                                  xs[:, t, k * P:(k + 1) * P], ident[:, :])
                    ins.then_inc(n_tr, 1)

            jobs = [0]

            def job(dst, banks, pairs):
                n = jobs[0]
                if n >= banks:
                    pe.wait_ge(job_ev, n - banks + 1)
                jobs[0] += 1
                ins = chain(dst, pairs)
                ins.then_inc(job_mm, 1)

            def used(n):
                pe.wait_ge(job_mm, jobs[0])
                pe.sem_inc(unit_used, 1)

            def kv(n0):
                w = whole_unit(n0).rearrange("p (k n) -> p k n", k=KC)
                for c in range(2):
                    job(bank(6 + c)[:, 0:MEM], 2, ((w[:, k, c * P:(c + 1) * P], memT[:, k, :]) for k in range(KC)))
                w2 = whole_unit(n0 + 1).rearrange("p (k n) -> p k n", k=KC)
                for c in range(MT):
                    job(bank(6 + c)[:, 0:256], 2, ((memT[:, k, c * P:(c + 1) * P], w2[:, k, :]) for k in range(KC)))
                used(n0)
                used(n0 + 1)

            def recurrence():
                def project(c, j, dst):
                    w = unit(INA + c)
                    return chain(dst[0:RW, :], passes(
                        (both_of(w, ALL, k, slice(j * P, j * P + RW)), both_of(hn, ALL, k, ALL)) for k in range(KC)))

                def inputs(c):
                    if c >= 2:
                        pe.wait_ge(a_uev, c - 1)
                    project(c, 0, bank(c % 2)).then_inc(a_ux, 1)

                def gelu_inputs(c):
                    if c >= 3:
                        pe.wait_ge(a_cat, c - 2)
                    project(c, 1, gelu_bank(c)).then_inc(a_ug, 1)
                    pe.wait_ge(a_ug, c + 1)
                    pe.sem_inc(unit_used, 1)

                def gates(c):
                    pe.wait_ge(a_xc, c + 1)
                    if c >= 1:
                        pe.wait_ge(a_T, c)
                    else:
                        pe.wait_ge(gate_in, 16)
                    mm(bank(4)[0:RW, :], gw[:, 0, c, :], xc[c % 2], start=True, stop=True)
                    mm(bank(5)[0:RW, :], gw[:, 1, c, :], xc[c % 2], start=True, stop=True).then_inc(a_gates, 1)

                for c in range(RB):
                    inputs(c)
                    if c >= 1:
                        gates(c - 1)
                    gelu_inputs(c)
                gates(RB - 1)

            def q_memory(n):
                w = unit(n)
                pe.wait_ge(a_cat, RB - 2)
                for c in range(2):
                    job(bank(6 + c), 2, passes(
                        (both_of(w, ALL, k, slice(c * P, (c + 1) * P)), both_of(hn, ALL, k, ALL)) for k in range(KC)))
                used(n)

            def memory_attention(L):
                def scores(i):
                    t, hp = MSTEPS[i]
                    if i >= 2:
                        pe.wait_ge(m_exp, i - 1 + MS * L)
                    for n in range(2):
                        r = slice(n * DH, (n + 1) * DH)
                        ins = mm(bank(2 * (i % 2) + n)[:, 0:MEM], qmT[r, hp, t * P:(t + 1) * P], kTm[r, hp, :],
                                 start=True, stop=True)
                    ins.then_inc(m_s, 1)

                def turn(i):
                    s = i % 2
                    pe.wait_ge(m_p, i + 1 + MS * L)
                    if i >= 2:
                        pe.wait_ge(m_ptev, i - 1 + MS * L)
                    for n in range(2):
                        for c in range(MT):
                            j = n * MT + c
                            ins = nc.tensor.transpose(bank(4 + s)[:, j * P:(j + 1) * P], E[s][:, n, c * P:(c + 1) * P], ident[:, :])
                    ins.then_inc(m_pt, 1)

                def values(i):
                    t, hp = MSTEPS[i]
                    s = i % 2
                    pe.wait_ge(m_ptev, i + 1 + MS * L)
                    if i >= 2:
                        pe.wait_ge(m_oev, i - 1 + MS * L)
                    for n in range(2):
                        hd = 2 * hp + n
                        ins = chain(bank(6 + s)[n * DH:(n + 1) * DH, 0:P],
                                    ((vm[:, c, hd * DH:(hd + 1) * DH], PTs[s][:, n * MT + c, :]) for c in range(MT)))
                    ins.then_inc(m_o, 1)

                n = len(MSTEPS)
                pe.wait_ge(job_ev, jobs[0])
                if L == 0:
                    pe.wait_ge(a_cat, RB)
                else:
                    pe.wait_ge(d_otev, 2 * NT)
                scores(0)
                for i in range(n + 2):
                    if i + 1 < n:
                        scores(i + 1)
                    if 1 <= i <= n:
                        turn(i - 1)
                    if i >= 2:
                        values(i - 2)

            def output(L):
                pe.wait_ge(m_oev, MS + MS * L)
                n0, chunks = ((OUTA, [RW] * RB + [P] * 2), (OUTB, [P] * 8))[L]
                for j, rows in enumerate(chunks):
                    w = unit(n0 + j // 2, 2)
                    pe.wait_ge(cat_lows, j // 2 + 1 + CAT_PAIRS[0] * L)
                    last = j == len(chunks) - 1
                    for t in range(NT):
                        for b in range(2):
                            for k, (lhsT, rhs) in enumerate(passes(
                                    [(both_of(cats, slice(0, rows), j, slice(t * P, (t + 1) * P)),
                                      both_of(w, slice(0, rows), j % 2, slice(b * 512, (b + 1) * 512)))])):
                                ins = mm(bank(2 * t + b), lhsT, rhs, start=(j == 0 and k == 0), stop=(last and k == 2))
                        if last:
                            ins.then_inc(o_mm, 1)
                    if j % 2 == 1 and not last:
                        ins.then_inc(unit_used, 1)
                pe.wait_ge(o_mm, NT + NT * L)
                pe.sem_inc(unit_used, 1)

            def routing(L):
                if L == 0:
                    pe.wait_ge(small_in, 32)
                pe.wait_ge(n_ev, NT + NORM_BASE[2 + 2 * L])
                for t in range(NT):
                    ins = chain(bank(4)[:, t * (NG + NE):(t + 1) * (NG + NE)],
                                ((hnT[:, k, t * P:(t + 1) * P], wgr[:, L, k, :]) for k in range(KC)))
                ins.then_inc(r_lg, 1)
                if L == 0:
                    kv(KV1)
                pe.wait_ge(r_sel, 1 + L)
                mm(bank(5)[:, 0:64], before[:, :], sel.rearrange("p t e -> p (t e)"), start=True, stop=True)
                mm(bank(5)[:, 64:128], ones[:, :], sel.rearrange("p t e -> p (t e)"), start=True, stop=True).then_inc(r_rank, 1)
                for e in range(4):
                    slot_tokens(L, e, e % 2, e)

            def slot_tokens(L, e, s, column):
                pe.wait_ge(r_hot, e + 1 + NE * L)
                chain(bank(3)[:, column:column + 1], ((onesl[s][:, c, :], tokid[:, c:c + 1]) for c in range(NT))
                      ).then_inc(r_idx, 1)

            def turn_tile(s):
                for k in range(KC):
                    ins = nc.tensor.transpose(ps[:, k // 4, (k % 4) * P:(k % 4 + 1) * P], xg[s][:, k * P:(k + 1) * P], ident[:, :])
                return ins

            def up_tile(s):
                w = w_up[s].rearrange("p (k n) -> p k n", k=KC)
                return chain(bank(4 + s), ((xgT[s][:, k, :], w[:, k, :]) for k in range(KC)))

            def turn_hidden(s):
                for f in range(2):
                    ins = nc.tensor.transpose(bank(2)[:, f * P:(f + 1) * P], hid[s][:, f * P:(f + 1) * P], ident[:, :])
                return ins

            def down_tile(s):
                w = w_down[s].rearrange("p (f n) -> p f n", f=2)
                for b in range(2):
                    ins = chain(bank(6 + b), ((hidT[s][:, f, :], w[:, f, b * 512:(b + 1) * 512]) for f in range(2)))
                return ins

            def experts_pe(L):
                def turn(e, s, use, reused=True):
                    pe.wait_ge(x_full[s], 16 * use + 8 * NE * L)
                    if reused:
                        pe.wait_ge(x_ev, e + NE * L)
                    turn_tile(s).then_inc(x_tr, 1)

                def up(e, s, use, reused=True):
                    pe.wait_ge(up_full[s], 16 * use + 16 * (NE // 2) * L)
                    if reused:
                        pe.wait_ge(e_hid, e - 1 + NE * L)
                    pe.wait_ge(x_ev, e + 1 + NE * L)
                    up_tile(s).then_inc(e_up, 1)

                def down(e, s, use, reused=True):
                    pe.wait_ge(down_full[s], 16 * use + 16 * (NE // 2) * L)
                    if reused:
                        pe.wait_ge(e_yev, e + NE * L)
                    pe.wait_ge(e_htev, e + 1 + NE * L)
                    down_tile(s).then_inc(e_down, 1)

                def turn_h(e, s, reused=True):
                    if reused:
                        pe.wait_ge(e_htev, e + NE * L)
                    pe.wait_ge(e_hid, e + 1 + NE * L)
                    turn_hidden(s).then_inc(e_ht, 1)

                turn(0, 0, 1, False)
                up(0, 0, 1, False)
                turn(1, 1, 1)
                turn_h(0, 0, False)
                up(1, 1, 1, False)
                turn(2, 0, 2)
                down(0, 0, 1, False)
                turn_h(1, 1)
                with pe.Fori(1, NE // 2 - 1) as i:
                    up(2 * i, 0, i + 1)
                    pe.wait_ge(r_idxi, i + 1 + (NE // 2) * L)
                    slot_tokens(L, 2 * i + 2, 0, 0)
                    slot_tokens(L, 2 * i + 3, 1, 1)
                    turn(2 * i + 1, 1, i + 1)
                    down(2 * i - 1, 1, i)
                    turn_h(2 * i, 0)
                    up(2 * i + 1, 1, i + 1)
                    turn(2 * i + 2, 0, i + 2)
                    down(2 * i, 0, i + 1)
                    turn_h(2 * i + 1, 1)
                h8 = NE // 2
                up(NE - 2, 0, h8)
                turn(NE - 1, 1, h8)
                down(NE - 3, 1, h8 - 1)
                turn_h(NE - 2, 0)
                up(NE - 1, 1, h8)
                down(NE - 2, 0, h8)
                turn_h(NE - 1, 1)
                down(NE - 1, 1, h8)

            def overflow(L):
                pe.wait_ge(v_over, 1 + L)
                V = pe.value_load(vcount[0:1, 0:1], min_val=0, max_val=MORE)
                with pe.If(V > 0):
                    with pe.Fori(0, V) as i:
                        pe.wait_ge(v_hot[L], i + 1)
                        chain(bank(3)[:, 0:1], ((onesl[0][:, c, :], tokid[:, c:c + 1]) for c in range(NT))).then_inc(v_idx[L], 1)
                        pe.wait_ge(v_xfull[L], 16 * i + 16)
                        turn_tile(0).then_inc(v_tr[L], 1)
                        pe.wait_ge(v_wfull[L], 32 * i + 32)
                        pe.wait_ge(v_ev[L], i + 1)
                        up_tile(0).then_inc(v_up[L], 1)
                        pe.wait_ge(v_hid[L], i + 1)
                        turn_hidden(0).then_inc(v_ht[L], 1)
                        pe.wait_ge(v_htev[L], i + 1)
                        pe.wait_ge(e_yev, NE + NE * L)
                        down_tile(0).then_inc(v_down[L], 1)

            def relative_bias():
                pe.wait_ge(b_rep, 1)
                for hd in range(HEADS):
                    if hd >= 2:
                        pe.wait_ge(b_ev, hd - 1)
                    mm(bank(hd % 2)[:, 0:REVLEN], relrep[:, hd, :], hotsb, start=True, stop=True).then_inc(b_mm, 1)

            def project_b():
                j = [0]

                def columns(w, m):
                    return passes((both_of(w, ALL, k, slice(m * P, (m + 1) * P)), both_of(hn, ALL, k, ALL)) for k in range(KC))

                for c in range(HEADS // 2):
                    for o in range(2):
                        w = unit(INB + 2 * c + o)
                        for m in range(2):
                            job(bank(4 + j[0] % 4), 4, columns(w, m))
                            j[0] += 1
                        used(INB + 2 * c + o)
                for c in range(3):
                    w = unit(INB + 6 + c)
                    for t in range(NT):
                        job(bank(4 + j[0] % 4)[:, 0:256], 4, passes(
                            (both_of(hn, ALL, k, slice(t * P, (t + 1) * P)), both_of(w, ALL, k, ALL)) for k in range(KC)))
                        j[0] += 1
                    used(INB + 6 + c)
                w = unit(QMB)
                for c in range(2):
                    job(bank(4 + j[0] % 4), 4, columns(w, c))
                    j[0] += 1
                used(QMB)

            def diff_attention():
                def scores(i):
                    b, hd = STEPS[i]
                    s, nk = i % 2, (b + 1) * P
                    if i >= 2:
                        pe.wait_ge(d_nmx, i - 1)
                    for n in range(2):
                        r = slice(n * DH, (n + 1) * DH)
                        ins = mm(bank(2 * s + n)[:, 0:nk], qT[r, hd, b * P:(b + 1) * P], kT[r, hd, 0:nk], start=True, stop=True)
                    ins.then_inc(d_s, 1)

                def turn(i):
                    b, hd = STEPS[i]
                    s = i % 2
                    pe.wait_ge(d_p, i + 1)
                    if i >= 1:
                        pe.wait_ge(d_ptev, i)
                    for c in range(b + 1):
                        ins = nc.tensor.transpose(bank(4)[:, c * P:(c + 1) * P], E[s][:, 0, c * P:(c + 1) * P], ident[:, :])
                    ins.then_inc(d_pt, 1)

                def values(i):
                    b, hd = STEPS[i]
                    pe.wait_ge(d_ptev, i + 1)
                    if i >= 1:
                        pe.wait_ge(d_oev, i)
                    chain(bank(5)[:, 0:P], ((PTs[i % 2][:, c, :], vB[:, c, hd * P:(hd + 1) * P]) for c in range(b + 1))
                          ).then_inc(d_o, 1)

                def turn_out(b):
                    pe.wait_ge(d_on, b + 1)
                    if b >= 1:
                        pe.wait_ge(d_otev, 2 * b)
                    for j, (a, n) in enumerate(((0, 4), (4, 2))):
                        for c in range(n):
                            ins = nc.tensor.transpose(bank(6 + j)[:, c * P:(c + 1) * P], On[:, a + c, :], ident[:, :])
                        ins.then_inc(d_ot, 1)

                n = len(STEPS)
                pe.wait_ge(job_ev, jobs[0])
                scores(0)
                for i in range(n + 2):
                    if i + 1 < n:
                        scores(i + 1)
                    if 1 <= i <= n:
                        turn(i - 1)
                    if i >= 2:
                        values(i - 2)
                    if i % HEADS == 4 and i > HEADS:
                        turn_out(i // HEADS - 1)
                turn_out(NT - 1)

            pe.wait_ge(pool_const, 11)
            turn_rows(0)
            pe.wait_ge(n_ev, MT)
            kv(KV0)
            turn_rows(1)
            pe.wait_ge(rows_lo, NT)
            recurrence()
            q_memory(QMA)
            memory_attention(0)
            output(0)
            turn_rows(2, 0)
            routing(0)
            experts_pe(0)
            overflow(0)
            turn_rows(3)
            pe.wait_ge(rows_lo, 2 * NT)
            relative_bias()
            project_b()
            diff_attention()
            memory_attention(1)
            output(1)
            turn_rows(4, 1)
            routing(1)
            experts_pe(1)
            overflow(1)


def reversed_buckets(np):
    n = np.maximum(255 - np.arange(REVLEN), 0)
    large = 16 + (np.log(np.maximum(n, 1) / 16) / math.log(8) * 16 + 1e-9).astype(np.int64)
    bucket = np.where(n < 16, n, np.minimum(large, REL - 1))
    hot = np.zeros((REL, REVLEN), np.float32)
    hot[bucket, np.arange(REVLEN)] = 1.0
    return hot


def kernel(**inputs):
    import numpy as np
    import concourse.bacc as bacc
    from concourse.bass_utils import run_bass_kernel_spmd as run

    a = {k: np.asarray(w) for k, w in inputs.items()}

    def by_partition(w):
        return w.reshape(w.shape[0] // P, P, -1).transpose(1, 0, 2).reshape(P, -1)

    units = np.zeros((UNITS, P, UNIT), np.float32)

    def put(n, block):
        units[n, :block.shape[0], :block.shape[1]] = block

    for L, n in ((0, KV0), (1, KV1)):
        for j in range(2):
            put(n + j, by_partition(a["w_mem_kv"][L][:, j * 256:(j + 1) * 256]))
    wa, wb = a["w_in_a"][0], a["w_in_b"][0]
    tok = RB * RW
    for c in range(RB):
        block = units[INA + c].reshape(P, KC, 2, P)
        for j in range(2):
            block[:, :, j, :RW] = by_partition(wa[:, j * tok + c * RW:j * tok + (c + 1) * RW]).reshape(P, KC, RW)
    put(QMA, by_partition(wa[:, 2 * tok:2 * tok + 256]))
    for c in range(3):
        for o in range(2):
            put(INB + 2 * c + o, by_partition(wb[:, o * tok + c * 256:o * tok + (c + 1) * 256]))
        put(INB + 6 + c, by_partition(wb[:, 2 * tok + c * 256:2 * tok + (c + 1) * 256]))
    put(QMB, by_partition(wb[:, 3 * tok:3 * tok + 256]))
    oa, ob = a["w_out"]
    for c in range(RB):
        units[OUTA + c // 2, :RW, (c % 2) * D:(c % 2 + 1) * D] = oa[c * RW:(c + 1) * RW]
    put(OUTA + 4, by_partition(oa[tok:]))
    for c in range(4):
        put(OUTB + c, by_partition(ob[c * 256:(c + 1) * 256]))

    experts = np.empty((2, NE, P, EXPW), np.float32)
    up = np.concatenate([a["w_exp1"], a["w_exp3"]], axis=3).reshape(2, NE, KC, P, 2 * DE)
    experts[..., :UPW] = up.transpose(0, 1, 3, 2, 4).reshape(2, NE, P, UPW)
    experts[..., UPW:] = a["w_exp2"].reshape(2, NE, 2, P, D).transpose(0, 1, 3, 2, 4).reshape(2, NE, P, 2 * D)

    vecs = np.zeros((P, NVEC), np.float32)

    def vec(name, block):
        lo, hi = VEC[name]
        vecs[:block.shape[0], lo:hi] = block

    for name, g in (("mix0", a["norm_mix_g"][0]), ("mix1", a["norm_mix_g"][1]), ("ffn0", a["norm_ffn_g"][0]),
                    ("ffn1", a["norm_ffn_g"][1]), ("mem", a["mem_norm_g"])):
        vec(name, g.reshape(KC, P).T)
    vec("subln", a["diff_subln_g"][0].reshape(P, 1))
    vec("conv_w", a["conv_w"][0].reshape(CONV, RB, RW).transpose(2, 1, 0).reshape(RW, RB * CONV))
    for name, key in (("conv_b", "conv_b"), ("gate_a_b", "gate_a_b"), ("gate_x_b", "gate_x_b"), ("lam", "lru_lambda")):
        vec(name, a[key][0].reshape(RB, RW).T)

    router = np.concatenate([a["w_group"], a["w_router"]], axis=2).reshape(2, KC, P, NG + NE).transpose(2, 0, 1, 3).reshape(P, -1)
    gate_w = np.stack([a["gate_a_w"][0], a["gate_x_w"][0]]).transpose(2, 0, 1, 3).reshape(RW, 2 * RB * RW)
    diff_l = np.concatenate([a[k][0] for k in ("diff_lq1", "diff_lk1", "diff_lq2", "diff_lk2")]).reshape(1, -1)

    arrays = {
        "x": a["x"][0], "mem": a["mem"][0], "units": units, "experts": experts, "gate_w": gate_w, "vecs": vecs,
        "router": router, "diff_l": diff_l, "rel_bias": a["rel_bias"], "final_g": a["final_norm_g"].reshape(1, D),
        "onehot": reversed_buckets(np),
    }
    arrays = {f"in_{k}": np.ascontiguousarray(w) for k, w in arrays.items()}
    nc = bacc.Bacc("TRN2", target_bir_lowering=False, num_devices=1)
    args = [nc.dram_tensor(k, w.shape, mybir.dt.from_np(w.dtype), kind="ExternalInput").ap() for k, w in arrays.items()]
    args.append(nc.dram_tensor("out_0", (T, D), F32, kind="ExternalOutput").ap())
    build(nc, *args)
    r = run(nc, [arrays], core_ids=[0])
    return r.results[0]["out_0"].reshape(1, T, D)
```

```python
import math
from contextlib import ExitStack

import concourse.bass as bass
from concourse import mybir

F32 = mybir.dt.float32
F32R = mybir.dt.float32r
F16 = mybir.dt.float16
I32 = mybir.dt.int32
ALU = mybir.AluOpType
ACT = mybir.ActivationFunctionType
AXX = mybir.AxisListType.X

P = 128
D = 1024
T = 512
NT = T // P
KC = D // P
MEM = 256
MT = MEM // P
DH = 64
RB, RW = 8, 96
CONV = 4
HEADS = 6
NG, EPG = 4, 4
NE = NG * EPG
DE = 256
EPS = 1e-6
REL = 32
NEAR = 2 * P
REVLEN = 384
UNIT = KC * 256
RING = 3
MORE = 2 * T // P - 1
UPW = KC * 2 * DE
EXPW = UPW + 2 * D
LAMBDA_INIT = 0.8 - 0.6 * math.exp(-0.3)
GELU_C = math.sqrt(2.0 / math.pi)
NEG = -1.0e30

KV0, INA, QMA, OUTA = 0, 2, 10, 11
KV1 = OUTA + 4
INB = KV1 + 2
QMB = INB + 9
OUTB = QMB + 1
UNITS = OUTB + 4


def split_before(n):
    return n - 2 if n < KV1 else n - 4


def vec_columns():
    at, out = 0, {}
    for name, n in (("mix0", KC), ("mix1", KC), ("ffn0", KC), ("ffn1", KC), ("mem", KC),
                    ("subln", 1), ("conv_w", RB * CONV), ("conv_b", RB), ("gate_a_b", RB),
                    ("gate_x_b", RB), ("lam", RB)):
        out[name] = (at, at + n)
        at += n
    return out, at


VEC, NVEC = vec_columns()


def build(nc, x, mem, units, experts, gate_w, vecs, router, diff_l, rel_bias, final_g, onehot, out):
    ctx = ExitStack()
    with ctx:
        def sb(name, shape, dt=F32):
            return ctx.enter_context(nc.sbuf_tensor(name, shape, dt))

        def both(name, shape):
            with nc.sbuf_tensor(name, shape, F32) as whole:
                pass
            return whole, sb(f"{name}_low", shape, F32R)

        def sem(name):
            return ctx.enter_context(nc.semaphore(name))

        h = sb("h", [P, NT, D])
        xs_all, cat_low = both("xs_all", [P, 10 * T])
        xs = xs_all[:, 0:NT * D].rearrange("p (t d) -> p t d", t=NT)
        cat = xs_all[:, :].rearrange("p (c t) -> p c t", t=T)
        cat_lo = cat_low[:, :].rearrange("p (c t) -> p c t", t=T)
        hnT, hn_lo = both("hnT", [P, KC, T])
        memT = sb("memT", [P, KC, MEM])
        ring, ring_lo = both("ring", [P, RING, UNIT])
        ring_hi = sb("ring_high", [P, RING, UNIT], F32R)
        expw, expw_part = both("expw", [P, 2, EXPW])
        hn_hi = expw_part[:, 1, 0:KC * T].rearrange("p (k t) -> p k t", k=KC)
        cat_hi = expw_part[:, 1, 0:8 * T].rearrange("p (c t) -> p c t", t=T)
        w_up = [expw[:, s, 0:UPW] for s in range(2)]
        w_down = [expw[:, s, UPW:EXPW] for s in range(2)]
        wgr = sb("wgr", [P, 2, KC, NG + NE])
        arena = sb("arena", [P, 9 * D])
        kvq = sb("kvq", [P, 2 * D])
        kTm = kvq[:, 0:512].rearrange("p (c m) -> p c m", c=2)
        vm = kvq[:, 512:1024].rearrange("p (c m) -> p c m", c=MT)
        qmT = kvq[:, 1024:2048].rearrange("p (c t) -> p c t", c=2)
        ident = sb("ident", [P, P])
        iota = sb("iota", [P, P])
        before = sb("before", [P, P])
        ones = sb("ones", [P, P])
        vec = sb("vec", [P, NVEC])
        small = sb("small", [P, 828])

        def v(name, lo=0, hi=None):
            a, b = VEC[name]
            return vec[:, a + lo:(b if hi is None else a + hi)]

        taken = [0]

        def sm(*shape, dt=None):
            n = 1
            for s in shape:
                n *= s
            a = taken[0]
            taken[0] += n
            assert taken[0] <= 828
            t = small[:, a:a + n]
            if dt is not None:
                t = t.bitcast(dt)
            if len(shape) == 2:
                t = t.rearrange("p (a b) -> p a b", a=shape[0])
            if len(shape) == 3:
                t = t.rearrange("p (a b c) -> p a b c", a=shape[0], b=shape[1])
            return t

        ssq, msq, rstd, mhalf = sm(NT), sm(NT), sm(NT), sm(8)
        mx, nmx, rsum, rec, ratio = sm(2, 2), sm(2, 2), sm(2, 2), sm(4, 2), sm(1)
        lprod, lsum, lexp, neglam = sm(2, DH), sm(2), sm(2), sm(1)
        ossq, orstd, gsub = sm(HEADS), sm(HEADS), sm(1)
        c31 = sm(HEADS)
        iota4, iota16, row16, jcol = sm(4), sm(NE), sm(NE), sm(NE, 3)
        wv1, wv2 = sm(NT), sm(NT)
        r1i, r2i = sm(NT, dt=I32), sm(NT, dt=I32)
        idxi = sm(NE, dt=I32)
        vcount, vsteer = sm(1, dt=I32), sm(1, dt=I32)
        vidx, vc = sm(NE, 3), sm(1)
        rk = sm(NT, NE)
        ntot = sm(NE)
        ovi = sm(1, dt=I32)
        hba, hbx, spl, msp = sm(RB), sm(RB), sm(RB), sm(RB)
        tokid = sb("tokid", [P, NT], F16)

        upad = arena[0:RW, 0:2 * 515].rearrange("p (s n) -> p s n", s=2)
        def ab(i, n=1):
            a = 1040 + 512 * i
            return arena[0:RW, a:a + 512 * n]
        xc = [ab(0), ab(1)]
        ta, tx0, sq, dd, ra0, ra1, gg, gq = (ab(i) for i in range(2, 10))
        ra = [ra0, ra1]
        tx = [tx0, cat[0:RW, HEADS, :]]
        rec_out = [cat[0:RW, HEADS + 2 + s, :] for s in range(2)]
        gw = arena[0:RW, 1040 + 5120:1040 + 5120 + 2 * RB * RW].rearrange("p (s g j) -> p s g j", s=2, g=RB)
        qT = arena[:, 0:3072].rearrange("p (c t) -> p c t", c=HEADS)
        kT = arena[:, 3072:6144].rearrange("p (c t) -> p c t", c=HEADS)
        vB = arena[:, 6144:9216].rearrange("p (t c) -> p t c", t=NT)
        bias = memT[:, :, :].rearrange("p k m -> p (k m)")[:, 0:HEADS * NEAR].rearrange("p (h n) -> p h n", h=HEADS)
        hflat = hnT[:, :, :].rearrange("p k t -> p (k t)")
        E = [place.rearrange("p (n k) -> p n k", n=2)
             for place in (expw[:, 1, 4 * D:5 * D], expw[:, 1, 5 * D:6 * D], xs_all[:, 8 * T:10 * T])]
        PTs = [hflat[:, 2048 + s * 512:2560 + s * 512].rearrange("p (c q) -> p c q", c=4) for s in range(2)]
        Osb = hflat[:, 3072:3840].rearrange("p (h d) -> p h d", h=HEADS)
        gfin = hflat[:, 0:D]
        xg = [arena[:, s * D:(s + 1) * D] for s in range(2)]
        xgT = [arena[:, (2 + s) * D:(3 + s) * D].rearrange("p (k t) -> p k t", k=KC) for s in range(2)]
        ysb = [arena[:, (4 + s) * D:(5 + s) * D] for s in range(2)]
        hid = [arena[:, 6144 + s * 256:6400 + s * 256] for s in range(2)]
        tnh = [arena[:, 6656 + s * 256:6912 + s * 256] for s in range(2)]
        hidT = [arena[:, 7168 + s * 256:7424 + s * 256].rearrange("p (f t) -> p f t", f=2) for s in range(2)]
        onesl = [arena[:, 7680 + s * 256:7936 + s * 256].bitcast(F16).rearrange("p (c t) -> p c t", c=NT) for s in range(2)]
        rsc = arena[:, 8192:9216]
        lgT = arena[0:NG + NE, 4096:4096 + T]
        comb = [[arena[:, (2 * t + r) * D:(2 * t + r + 1) * D] for r in range(2)] for t in range(NT)]
        lall = hflat[:, 0:256]
        relsb = hflat[0:REL, 256:256 + HEADS]
        hotsb = hflat[0:REL, 264:264 + REVLEN]
        relrep = hflat[0:REL, 648:648 + HEADS * P].rearrange("p (h m) -> p h m", h=HEADS)
        relrows = hflat[:, 1536:1536 + HEADS * REVLEN].rearrange("p (h m) -> p h m", h=HEADS)
        On = hflat[:, 0:HEADS * P].rearrange("p (h d) -> p h d", h=HEADS)

        scr = [0]

        def rt(*shape):
            n = 1
            for k in shape:
                n *= k
            a = scr[0]
            scr[0] += n
            assert scr[0] <= D
            t = rsc[:, a:a + n]
            if len(shape) == 2:
                t = t.rearrange("p (a b) -> p a b", a=shape[0])
            if len(shape) == 3:
                t = t.rearrange("p (a b c) -> p a b c", a=shape[0], b=shape[1])
            return t

        lg = rt(NT, NG + NE)
        r_gmax, r_gi, r_gsum, r_gw, r_m1, r_m2, r_ji, r_den = (rt(NT) for _ in range(8))
        rdiff = rt(NT)
        r_eqg, ohg, rg_e, e_in, r_eqe, oh1, oh2 = (rt(NT, 4) for _ in range(7))
        r_prod = rt(NT, NG, EPG)
        ohe1, ohe2, sel, r_rankv, r_slot, r_cnt = (rt(NT, NE) for _ in range(6))
        r_off, r_base = rt(NT, NE), rt(NE)
        r_over, r_cum = rt(NE, 3), rt(NE, 3)
        r_r1, r_r2 = rt(NT), rt(NT)
        v_m, v_eoh, v_jv, v_rr, v_rk, v_t16, v_es = rt(NE, 3), rt(NE), rt(1), rt(NT, NE), rt(NT), rt(NE), rt(1)

        ps = ctx.enter_context(nc.psum_tensor("ps", [P, 8, 512], F32))

        def bank(i):
            return ps[:, i, :]

        def part(r, n):
            if INA <= n < QMA:
                return r[:, n % RING, :].rearrange("p (k n) -> p k n", n=P)[:, :, 0:RW]
            return r[:, n % RING, :]

        def value_bank(L):
            return (4, 6)[L]

        def gelu_bank(c):
            return bank((2, 3, 6)[c % 3])

        xs_d = nc.dram_tensor("xs_rows", [T, D], F32).ap()
        y_d = nc.dram_tensor("expert_rows", [(NE + MORE) * P, D], F32).ap()
        rel_d = nc.dram_tensor("bias_rows", [HEADS, P, REVLEN], F32).ap()

        h_in = [sem(f"h_in{t}") for t in range(NT)]
        mem_in, small_in, gate_in, fin_in = (sem(n) for n in ("mem_in", "small_in", "gate_in", "fin_in"))
        pool_const, dve_const = sem("pool_const"), sem("dve_const")
        dve_link, act_link = sem("dve_link"), sem("act_link")
        ring_full = [sem(f"ring_full{i}") for i in range(RING)]
        unit_used, unit_hi, unit_lo = sem("unit_used"), sem("unit_hi"), sem("unit_lo")
        rows_hi, rows_lo, cat_high, cat_lows = sem("rows_hi"), sem("rows_lo"), sem("cat_high"), sem("cat_lows")
        up_full = [sem("up_full0"), sem("up_full1")]
        down_full = [sem("down_full0"), sem("down_full1")]
        n_sq, n_ms, n_rs, n_xs, n_tr, n_ev = (
            sem(n) for n in ("norm_squared", "norm_mean", "norm_rstd", "norm_rows", "norm_turned", "norm_stored"))
        job_mm, job_ev = sem("job_mm"), sem("job_ev")
        a_ux, a_ug, a_gates = sem("a_ux"), sem("a_ug"), sem("a_gates")
        a_uev, a_gsq, a_T, a_sqrt, a_tg = (sem(n) for n in ("a_uev", "a_gsq", "a_T", "a_sqrt", "a_tg"))
        a_xc, a_q, a_g3, a_cat = (sem(n) for n in ("a_xc", "a_q", "a_g3", "a_cat"))
        a_vec, a_exp = sem("a_vec"), sem("a_exp")
        d_s, d_pt, d_o, d_ot = (sem(n) for n in ("d_s", "d_pt", "d_o", "d_ot"))
        d_nmx, d_p, d_ms, d_on = (sem(n) for n in ("d_nmx", "d_p", "d_ms", "d_on"))
        d_exp, d_ptev, d_oev, d_otev = (sem(n) for n in ("d_exp", "d_ptev", "d_oev", "d_otev"))
        rec_put = [sem("rec_put0"), sem("rec_put1")]
        last_rows_lo, d_far = sem("last_rows_lo"), sem("d_far")
        d_rs, b_mm, b_ev, b_in, b_mask = (sem(n) for n in ("d_rs", "b_mm", "b_ev", "b_in", "b_mask"))
        b_out = sem("b_out")
        l_sum, l_exp, b_rep, b_load = sem("l_sum"), sem("l_exp"), sem("b_rep"), sem("b_load")
        m_s, m_pt, m_o, m_nmx, m_p, m_exp, m_ptev, m_oev = (
            sem(n) for n in ("m_s", "m_pt", "m_o", "m_nmx", "m_p", "m_exp", "m_ptev", "m_oev"))
        o_mm, o_ev = sem("o_mm"), sem("o_ev")
        xs_out, r_lg, r_lgev, r_exp, r_pexp, r_sel, r_rank, r_hot, r_idx, r_idxi, r_done = (
            sem(n) for n in ("xs_out", "r_lg", "r_lgev", "r_exp", "r_pexp", "r_sel", "r_rank", "r_hot", "r_idx", "r_idxi", "r_done"))
        x_full, y_out = ([sem(f"{n}{s}") for s in range(2)] for n in ("x_full", "y_out"))
        c_full = [sem(f"c_full{t}") for t in range(NT)]
        x_tr, x_ev, e_up, e_tanh, e_hid, e_ht, e_htev, e_down, e_yev, e_gate = (
            sem(n) for n in ("x_tr", "x_ev", "e_up", "e_tanh", "e_hid", "e_ht", "e_htev", "e_down", "e_yev", "e_gate"))
        r_lt, r_ltev = sem("r_lt"), sem("r_ltev")
        turn_taken = sem("turn_taken")
        v_over, v_done, c_done = sem("v_over"), sem("v_done"), sem("c_done")
        (v_hot, v_idx, v_idxi, v_xfull, v_tr, v_ev, v_up, v_tanh, v_hid, v_ht, v_htev, v_down,
         v_yev, v_out, v_wfull, v_link, v_free) = (
            [sem(f"{n}{i}") for i in range(2)]
            for n in ("v_hot", "v_idx", "v_idxi", "v_xfull", "v_tr", "v_ev", "v_up", "v_tanh", "v_hid",
                      "v_ht", "v_htev", "v_down", "v_yev", "v_out", "v_wfull", "v_link", "v_free"))
        vec_in, zero_out = sem("vec_in"), sem("zero_out")
        fin_row, fin_out = sem("fin_row"), sem("fin_out")

        BLOCKS = range(NT - 1, -1, -1)
        STEPS = [(b, hd) for b in BLOCKS for hd in range(HEADS)]
        MSTEPS = [(t, hp) for t in range(NT) for hp in range(2)]
        MS = len(MSTEPS)
        CAT_PAIRS = (HEADS + 2) // 2

        def pieces(c):
            row, end = c * RW, (c + 1) * RW
            while row < end:
                n = min(end, (row // P + 1) * P) - row
                yield slice(row - c * RW, row - c * RW + n), row // P, slice(row % P, row % P + n)
                row += n

        def pieces_put(c):
            return sum(len(list(pieces(k))) for k in range(c % 2, c + 1, 2))
        NORM_TILES = [MT, NT, NT, NT, NT, NT]
        NORM_BASE = [sum(NORM_TILES[:n]) for n in range(6)]

        block = ctx.enter_context(nc.Block())

        @block.sync
        def _(sp):
            sp.dma_start(vec[:, :], vecs).then_inc(vec_in, 16)
            sp.dma_start(xs[:, 0:MT, :], mem.rearrange("(t p) d -> p t d", p=P)).then_inc(mem_in, 16)
            for t in range(NT):
                sp.dma_start(h[:, t, :], x[t * P:(t + 1) * P, :]).then_inc(h_in[t], 16)

            def load_unit(n):
                if n >= RING:
                    sp.wait_ge(unit_used, n - RING + 1)
                sp.dma_start(ring[:, n % RING, :], units[n, :, :]).then_inc(ring_full[n % RING], 16)

            def load_up(L, e, s, reused=True):
                if reused:
                    sp.wait_ge(e_up, e - 1 + NE * L)
                src = experts[L, e, :, 0:UPW] if isinstance(e, int) else \
                    experts[L, bass.ds(e, 1), :, 0:UPW].rearrange("o p n -> p (o n)")
                sp.dma_start(w_up[s], src).then_inc(up_full[s], 16)

            def load_down(L, e, s, reused=True):
                if reused:
                    sp.wait_ge(e_down, e - 1 + NE * L)
                src = experts[L, e, :, UPW:EXPW] if isinstance(e, int) else \
                    experts[L, bass.ds(e, 1), :, UPW:EXPW].rearrange("o p n -> p (o n)")
                sp.dma_start(w_down[s], src).then_inc(down_full[s], 16)

            def first_expert(L, e):
                load_up(L, e, e, False)
                load_down(L, e, e, False)

            for n in range(0, QMA):
                load_unit(n)
            first_expert(0, 0)
            for n in range(QMA, KV1 + 2):
                load_unit(n)

            for L in range(2):
                sp.wait_ge(o_mm, NT + NT * L)
                first_expert(L, 1)
                for t in range(NT):
                    sp.wait_ge(n_xs, t + 1 + NORM_BASE[2 + 2 * L])
                    sp.dma_start(xs_d[t * P:(t + 1) * P, :], xs[:, t, :]).then_inc(xs_out, 16)
                load_up(L, 2, 0)
                with sp.Fori(1, NE // 2 - 1) as i:
                    load_up(L, 2 * i + 1, 1)
                    load_down(L, 2 * i, 0)
                    load_up(L, 2 * i + 2, 0)
                    load_down(L, 2 * i + 1, 1)
                load_up(L, NE - 1, 1)
                load_down(L, NE - 2, 0)
                load_down(L, NE - 1, 1)
                if L == 0:
                    for n in range(INB, INB + RING):
                        load_unit(n)
                sp.wait_ge(v_over, 1 + L)
                V = sp.value_load(vcount[0:1, 0:1], min_val=0, max_val=MORE)
                with sp.If(V > 0):
                    sp.sem_inc(v_free[L], 1)
                    with sp.Fori(0, V) as i:
                        sp.wait_ge(v_hot[L], i + 1)
                        sp.sem_inc(turn_taken, 1)
                        ev = sp.value_load(vsteer[0:1, 0:1], min_val=0, max_val=NE - 1)
                        sp.wait_ge(e_down, NE + NE * L)
                        sp.dma_start(w_up[0], experts[L, bass.ds(ev, 1), :, 0:UPW]
                                     .rearrange("o p n -> p (o n)")).then_inc(v_wfull[L], 16)
                        sp.dma_start(w_down[0], experts[L, bass.ds(ev, 1), :, UPW:EXPW]
                                     .rearrange("o p n -> p (o n)")).then_inc(v_wfull[L], 16)
                        sp.wait_ge(v_yev[L], i + 1)
                        sp.dma_start(y_d[bass.ds(i * P + NE * P, P), :], ysb[0]).then_inc(v_out[L], 16)
                        sp.wait_ge(v_out[L], 16 * i + 16)
                        sp.sem_inc(v_free[L], 1)
                sp.sem_inc(v_done, 1)
                if L == 0:
                    sp.wait_ge(c_full[NT - 1], 32)
                    first_expert(1, 0)
                    for n in range(INB + RING, UNITS):
                        load_unit(n)
            for t in range(NT):
                sp.wait_ge(fin_row, t + 1)
                sp.dma_start(out[t * P:(t + 1) * P, :], xs[:, t, :]).then_inc(fin_out, 16)
            sp.wait_ge(fin_out, 16 * NT)

        @block.gpsimd
        def _(pool):
            pool.memset(ones[:, :], 1.0).then_inc(pool_const, 1)
            pool.memset(ident[:, :], 0.0).then_inc(pool_const, 1)
            pool.memset(mhalf, -0.5).then_inc(pool_const, 1)
            pool.wait_ge(pool_const, 3)
            pool.affine_select(out=ident[:, :], in_=ident[:, :], compare_op=ALU.not_equal, fill=1.0, base=0,
                               pattern=[[-1, P]], channel_multiplier=1).then_inc(pool_const, 1)
            pool.affine_select(out=before[:, :], in_=ones[:, :], compare_op=ALU.is_gt, fill=0.0, base=0,
                               pattern=[[1, P]], channel_multiplier=-1).then_inc(pool_const, 1)
            pool.iota(iota[:, :], pattern=[[1, P]], base=0, channel_multiplier=0,
                      allow_small_or_imprecise_dtypes=True).then_inc(pool_const, 1)
            pool.iota(tokid[:, :], pattern=[[P, NT]], base=0, channel_multiplier=1,
                      allow_small_or_imprecise_dtypes=True).then_inc(pool_const, 1)
            pool.iota(iota4, pattern=[[1, 4]], base=-16, channel_multiplier=0,
                      allow_small_or_imprecise_dtypes=True).then_inc(pool_const, 1)
            pool.iota(iota16, pattern=[[1, NE]], base=0, channel_multiplier=0,
                      allow_small_or_imprecise_dtypes=True).then_inc(pool_const, 1)
            pool.iota(row16, pattern=[[P, NE]], base=0, channel_multiplier=0,
                      allow_small_or_imprecise_dtypes=True).then_inc(pool_const, 1)
            pool.iota(jcol, pattern=[[0, NE], [P, 3]], base=P, channel_multiplier=0,
                      allow_small_or_imprecise_dtypes=True).then_inc(pool_const, 1)
            pool.dma_start(gw, gate_w.rearrange("p (s g j) -> p s g j", s=2, g=RB)).then_inc(gate_in, 16)
            pool.dma_start(wgr[:, :, :, :], router.rearrange("p (l k e) -> p l k e", l=2, k=KC)).then_inc(small_in, 16)
            pool.dma_start(c31, rel_bias[REL - 1:REL, :].to_broadcast([P, HEADS])).then_inc(small_in, 16)

            def low(n):
                pool.wait_ge(unit_hi, split_before(n) + 1)
                pool.tensor_tensor(part(ring_lo, n), part(ring, n), part(ring_hi, n).bitcast(F32), ALU.subtract).then_inc(unit_lo, 1)

            def low_cat(L, j):
                pair = slice(2 * j, 2 * j + 2)
                pool.wait_ge(cat_high, j + 1 + CAT_PAIRS * L)
                pool.tensor_tensor(cat_lo[:, pair, :], cat[:, pair, :], cat_hi[:, pair, :].bitcast(F32),
                                  ALU.subtract).then_inc(cat_lows, 1)

            def low_rows(L, t):
                cols = slice(t * P, (t + 1) * P)
                pool.wait_ge(rows_hi, t + 1 + NT * L)
                pool.tensor_tensor(hn_lo[:, :, cols], hnT[:, :, cols], hn_hi[:, :, cols].bitcast(F32), ALU.subtract
                                   ).then_inc(rows_lo, 1)

            def put_chunk(c):
                pool.wait_ge(a_cat, c + 1)
                for rows, chunk, there in pieces(c):
                    pool.dma_start(cat[there, chunk, :], rec_out[c % 2][rows, :]).then_inc(rec_put[c % 2], 16)

            def powers(n):
                for t in range(NORM_TILES[n]):
                    pool.wait_ge(n_ms, t + 1 + NORM_BASE[n])
                    pool.tensor_tensor(rstd[:, t:t + 1], msq[:, t:t + 1], mhalf[:, 0:1], ALU.pow).then_inc(n_rs, 1)
                    if n in (1, 3) and t >= 2:
                        low_rows(n // 2, t - 2)

            def gather_experts(L):
                pool.wait_ge(xs_out, 16 * NT + 16 * NT * L)
                for e in range(NE):
                    pool.wait_ge(r_idxi, e // 2 + 1 + NE // 2 * L)
                    if e >= 2:
                        pool.wait_ge(x_tr, e - 1 + NE * L)
                    pool.indirect_dma_start(xg[e % 2], None, xs_d, bass.IndirectOffsetOnAxis(ap=idxi[:, e:e + 1], axis=0)
                                            ).then_inc(x_full[e % 2], 16)

            def gather_overflow(L):
                pool.wait_ge(v_over, 1 + L)
                V = pool.value_load(vcount[0:1, 0:1], min_val=0, max_val=MORE)
                with pool.If(V > 0):
                    pool.wait_ge(x_tr, NE + NE * L)
                    with pool.Fori(0, V) as i:
                        pool.wait_ge(v_idxi[L], i + 1)
                        pool.sem_inc(turn_taken, 1)
                        pool.indirect_dma_start(xg[0], None, xs_d, bass.IndirectOffsetOnAxis(ap=ovi, axis=0)
                                                ).then_inc(v_xfull[L], 16)

            def gather_results(L):
                pool.wait_ge(y_out[0], 16 * NE // 2 + 8 * NE * L)
                pool.wait_ge(y_out[1], 16 * NE // 2 + 8 * NE * L)
                pool.wait_ge(r_done, 1 + L)
                pool.wait_ge(v_done, 1 + L)
                for t in range(NT):
                    for r, ri in enumerate((r1i, r2i)):
                        pool.indirect_dma_start(comb[t][r], None, y_d, bass.IndirectOffsetOnAxis(ap=ri[:, t:t + 1], axis=0)
                                                ).then_inc(c_full[t], 16)

            def zero_rows():
                pool.memset(rsc, 0.0).then_inc(pool_const, 1)
                pool.wait_ge(pool_const, 12)
                for j in range(MORE):
                    pool.dma_start(y_d[(NE + j) * P:(NE + j + 1) * P, :], rsc).then_inc(zero_out, 16)

            powers(0)
            powers(1)
            for n in range(INA, KV1):
                low(n)
                if n == INA + RING:
                    zero_rows()
                if INA + RING + 2 <= n < INA + RING + RB:
                    put_chunk(n - INA - RING - 2)
                if n == INA + RING + RB - 1:
                    put_chunk(RB - 2)
                    put_chunk(RB - 1)
                if n == OUTA + 2:
                    for j in range(CAT_PAIRS):
                        low_cat(0, j)
            powers(2)
            gather_experts(0)
            low(INB)
            gather_overflow(0)
            gather_results(0)
            powers(3)
            low(INB + 1)
            low(INB + 2)
            pool.wait_ge(b_in, 16)
            pool.affine_select(out=bias, in_=bias, compare_op=ALU.is_ge, fill=NEG, base=P,
                               pattern=[[0, HEADS], [-1, NEAR]], channel_multiplier=1).then_inc(b_mask, 1)
            for n in range(INB + RING, OUTB + 1):
                low(n)
            for b in range(NT):
                pool.wait_ge(d_ms, b + 1)
                pool.tensor_tensor(orstd, ossq, mhalf[:, 0:HEADS], ALU.pow).then_inc(d_rs, 1)
                if b in (1, 2):
                    low(OUTB + b)
            for j in range(CAT_PAIRS):
                low_cat(1, j)
            low(OUTB + 3)
            powers(4)
            gather_experts(1)
            gather_overflow(1)
            gather_results(1)
            powers(5)

        @block.scalar
        def _(act):
            links = [0]

            def link(ins):
                links[0] += 1
                ins.then_inc(act_link, 1)
                act.wait_ge(act_link, links[0])

            def squares(n, t, into):
                act.activation(into(t), (xs if n == 0 else h)[:, t, :], ACT.Square,
                               accum_out=ssq[:, t:t + 1]).then_inc(n_sq, 1)

            def norm(n, ready, into):
                nt = NORM_TILES[n]
                split = n in (1, 3)
                for t in range(nt + 3 if split else nt + 1):
                    if split and t == 3:
                        high_rows(n, 0)
                    if t < nt:
                        ready(t)
                        squares(n, t, into)
                    if 1 <= t <= nt:
                        act.wait_ge(n_rs, t + NORM_BASE[n])
                        if n == 1 and t == 1:
                            act.wait_ge(n_tr, MT)
                        act.activation(xs[:, t - 1, :], (xs if n == 0 else h)[:, t - 1, :], ACT.Copy, scale=rstd[:, t - 1:t]
                                       ).then_inc(n_xs, 1)
                    if split and t >= 4:
                        high_rows(n, t - 3)

            def high_rows(n, t):
                cols = slice(t * P, (t + 1) * P)
                act.wait_ge(n_ev, t + 1 + NORM_BASE[n])
                act.activation(hn_hi[:, :, cols], hnT[:, :, cols], ACT.Copy).then_inc(rows_hi, 1)

            jobs = [0]

            def stored(pairs):
                for dst, src in pairs:
                    n = jobs[0]
                    act.wait_ge(job_mm, n + 1)
                    act.activation(dst, src, ACT.Copy).then_inc(job_ev, 1)
                    jobs[0] += 1

            def high(n):
                act.wait_ge(ring_full[n % RING], 16 * (n // RING + 1))
                act.activation(part(ring_hi, n), part(ring, n), ACT.Copy).then_inc(unit_hi, 1)

            def high_cat(L, j):
                act.activation(cat_hi[:, 2 * j:2 * j + 2, :], cat[:, 2 * j:2 * j + 2, :], ACT.Copy).then_inc(cat_high, 1)

            def load_bias():
                act.wait_ge(r_lg, 1)
                act.dma_start(relsb, rel_bias).then_inc(b_load, 16)
                act.dma_start(hotsb, onehot).then_inc(b_load, 16)
                act.dma_start(lall, diff_l.to_broadcast([P, 4 * DH])).then_inc(b_load, 16)

            def relative_bias():
                act.wait_ge(l_sum, 1)
                act.activation(lexp, lsum, ACT.Exp).then_inc(l_exp, 1)
                for hd in range(HEADS):
                    act.wait_ge(b_mm, hd + 1)
                    act.activation(relrows[:, hd, :], bank(hd % 2)[:, 0:REVLEN], ACT.Copy).then_inc(b_ev, 1)
                    act.wait_ge(b_ev, hd + 1)
                    act.dma_start(rel_d[hd, :, :], relrows[:, hd, :]).then_inc(b_out, 16)

            def skewed_bias():
                act.wait_ge(b_out, 16 * HEADS)
                skew = rel_d.rearrange("h p m -> h (p m)")[:, P - 1:P - 1 + (REVLEN - 1) * P] \
                    .rearrange("h (q c) -> q h c", c=REVLEN - 1)[:, :, 0:NEAR]
                act.dma_start(bias, skew).then_inc(b_in, 16)

            def kv_jobs(L):
                stored([(kTm[:, c, :], bank(6 + c)[:, 0:MEM]) for c in range(2)]
                       + [(vm[:, c, :], bank(value_bank(L) + c)[:, 0:MEM]) for c in range(2)])

            def q_jobs():
                stored([(qmT[:, c, :], bank(6 + c)) for c in range(2)])

            def b_jobs():
                for c in range(HEADS // 2):
                    for dst in (qT, kT):
                        for j in range(2):
                            yield dst[:, 2 * c + j, :], slice(0, T)
                for c in range(3):
                    for t in range(NT):
                        yield vB[:, t, c * 256:(c + 1) * 256], slice(0, 256)
                for c in range(2):
                    yield qmT[:, c, :], slice(0, T)

            def recurrence():
                def first(c):
                    act.wait_ge(a_ux, c + 1)
                    if c >= 2:
                        act.wait_ge(a_xc, c - 1)
                    act.activation(upad[:, c % 2, 3:515], bank(c % 2)[0:RW, :], ACT.Copy).then_inc(a_uev, 1)

                def second(c):
                    act.wait_ge(a_gates, c + 1)
                    if c >= 1:
                        act.wait_ge(a_q, c)
                    if c >= 2:
                        act.wait_ge(a_cat, c - 1)
                    link(act.activation(ta, bank(4)[0:RW, :], ACT.Tanh, bias=hba[0:RW, c:c + 1], scale=0.5))
                    act.activation(tx[c % 2], bank(5)[0:RW, :], ACT.Tanh, bias=hbx[0:RW, c:c + 1], scale=0.5)
                    act.activation(ra[c % 2], ta, ACT.Exp, bias=msp[0:RW, c:c + 1], scale=msp[0:RW, c:c + 1])
                    act.activation(ta, ta, ACT.Tanh, bias=spl[0:RW, c:c + 1], scale=spl[0:RW, c:c + 1]).then_inc(a_T, 1)
                    act.wait_ge(a_ug, c + 1)
                    if c >= 1:
                        act.wait_ge(a_tg, c)
                    act.activation(gq, gelu_bank(c)[0:RW, :], ACT.Square).then_inc(a_gsq, 1)
                    act.wait_ge(a_g3, c + 1)
                    act.activation(gg, gq, ACT.Tanh, scale=GELU_C).then_inc(a_tg, 1)
                    act.wait_ge(a_q, c + 1)
                    act.activation(sq, dd, ACT.Sqrt).then_inc(a_sqrt, 1)

                act.wait_ge(a_vec, 2)
                for c in range(RB):
                    first(c)
                    if c >= 1:
                        second(c - 1)
                    high(INA + c + RING)
                second(RB - 1)

            def block_out(j):
                b = BLOCKS[j]
                for part, (a, n) in enumerate(((0, 4), (4, 2))):
                    act.wait_ge(d_ot, 2 * j + part + 1)
                    act.activation(cat[:, a:a + n, b * P:(b + 1) * P],
                                   bank(6 + part)[:, 0:n * P].rearrange("p (c q) -> p c q", c=n), ACT.Copy,
                                   scale=gsub[:, 0:1]).then_inc(d_otev, 1)

            def memory_attention(L):
                def softmax(i):
                    s = i % 2
                    act.wait_ge(m_nmx, i + 1 + MS * L)
                    if i >= 3:
                        act.wait_ge(m_pt, i - 2 + MS * L)
                    for n in range(2):
                        last = act.activation(E[i % 3][:, n, 0:MEM], bank(2 * s + n)[:, 0:MEM], ACT.Exp,
                                              bias=nmx[:, s, n:n + 1], scale=DH ** -0.5, accum_out=rsum[:, s, n:n + 1])
                    last.then_inc(m_exp, 1)

                def turned(i):
                    s = i % 2
                    act.wait_ge(m_pt, i + 1 + MS * L)
                    if i >= 2:
                        act.wait_ge(m_o, i - 1 + MS * L)
                    act.activation(PTs[s], bank(4 + s).rearrange("p (c q) -> p c q", c=4), ACT.Copy).then_inc(m_ptev, 1)

                def result(i):
                    t, hp = MSTEPS[i]
                    act.wait_ge(m_o, i + 1 + MS * L)
                    act.activation(cat[:, HEADS + hp, t * P:(t + 1) * P], bank(6 + i % 2)[:, 0:P], ACT.Copy
                                   ).then_inc(m_oev, 1)

                n = len(MSTEPS)
                done = CAT_PAIRS - 1
                for i in range(n + 2):
                    if i == 2 and L == 0:
                        for s in range(2):
                            act.wait_ge(rec_put[s], 16 * pieces_put(RB - 2 + s))
                    if i < n:
                        softmax(i)
                    if 1 <= i <= n:
                        turned(i - 1)
                    if i == 2 and L == 1:
                        block_out(NT - 1)
                        act.wait_ge(d_otev, 2 * NT)
                    if i >= 2:
                        result(i - 2)
                    if 2 <= i < 2 + done:
                        high_cat(L, i - 2)
                act.wait_ge(m_oev, MS + MS * L)
                high_cat(L, done)

            def diff_attention(queries):
                def far_scores(i):
                    b, hd = STEPS[i]
                    s, far = i % 2, (b + 1) * P - NEAR
                    if far > 0:
                        act.wait_ge(d_s, i + 1)
                        if i >= 3:
                            act.wait_ge(d_pt, i - 2)
                        act.activation(E[i % 3][:, :, 0:far], ps[:, 2 * s:2 * s + 2, 0:far], ACT.Identity,
                                       bias=c31[:, hd:hd + 1], scale=DH ** -0.5).then_inc(d_far, 1)

                def softmax(i):
                    b, hd = STEPS[i]
                    s, nk = i % 2, (b + 1) * P
                    act.wait_ge(d_nmx, i + 1)
                    for n in range(2):
                        last = act.activation(E[i % 3][:, n, 0:nk], E[i % 3][:, n, 0:nk], ACT.Exp, bias=nmx[:, s, n:n + 1],
                                              accum_out=rsum[:, s, n:n + 1])
                    last.then_inc(d_exp, 1)

                def turned(i):
                    b, hd = STEPS[i]
                    s = i % 2
                    act.wait_ge(d_pt, i + 1)
                    if i >= 2:
                        act.wait_ge(d_o, i - 1)
                    act.activation(PTs[s][:, 0:b + 1, :], bank(4).rearrange("p (c q) -> p c q", c=4)[:, 0:b + 1, :],
                                   ACT.Copy).then_inc(d_ptev, 1)

                def result(i):
                    hd = STEPS[i][1]
                    act.wait_ge(d_o, i + 1)
                    if hd == 0 and i > 0:
                        act.wait_ge(d_on, i // HEADS)
                    act.activation(Osb[:, hd, :], bank(5)[:, 0:P], ACT.Copy, scale=rec[:, i % 4, 0:1]).then_inc(d_oev, 1)

                n = len(STEPS)
                act.wait_ge(small_in, 32)
                far_scores(0)
                for i in range(n + 2):
                    if i + 1 < n and i != 1:
                        far_scores(i + 1)
                    if i < n:
                        softmax(i)
                    if i == 1:
                        queries()
                        far_scores(2)
                    if i == 2 * HEADS + 3:
                        high(OUTB + 1)
                    if i == 3 * HEADS + 3:
                        high(OUTB + 2)
                    if 1 <= i <= n:
                        turned(i - 1)
                    if i >= 2:
                        result(i - 2)
                        if (i - 2) % HEADS == 3 and i - 2 > HEADS:
                            block_out((i - 2) // HEADS - 1)

            def routing(L):
                for t in range(NT):
                    act.wait_ge(r_lt, t + 1 + NT * L)
                    act.activation(lgT[:, t * P:(t + 1) * P], bank(5 + t % 2)[0:NG + NE, 0:P], ACT.Copy).then_inc(r_ltev, 1)
                act.wait_ge(r_lg, 1 + L)
                act.wait_ge(zero_out, 16 * MORE)
                act.activation(lg, bank(4)[:, 0:NT * (NG + NE)].rearrange("p (t e) -> p t e", t=NT), ACT.Copy).then_inc(r_lgev, 1)
                act.wait_ge(r_exp, 1 + 2 * L)
                act.activation(rg_e, rg_e, ACT.Exp).then_inc(r_pexp, 1)
                act.wait_ge(r_exp, 2 + 2 * L)
                act.activation(rdiff, rdiff, ACT.Exp).then_inc(r_pexp, 1)

            def experts_act(L):
                def first(e, s):
                    act.wait_ge(e_up, e + 1 + NE * L)
                    act.activation(tnh[s], bank(4 + s)[:, 0:DE], ACT.Tanh, scale=0.5).then_inc(e_tanh, 1)

                def turned(e, s):
                    act.wait_ge(e_ht, e + 1 + NE * L)
                    act.activation(hidT[s], bank(2)[:, 0:2 * P].rearrange("p (f t) -> p f t", f=2), ACT.Copy
                                   ).then_inc(e_htev, 1)

                def result(e, s, uses):
                    act.wait_ge(e_down, e + 1 + NE * L)
                    if uses is not None:
                        act.wait_ge(y_out[s], uses + 8 * NE * L)
                    act.activation(ysb[s].rearrange("p (b n) -> p b n", b=2), ps[:, 6:8, :], ACT.Copy).then_inc(e_yev, 1)
                    act.wait_ge(e_yev, e + 1 + NE * L)
                    if isinstance(e, int):
                        act.dma_start(y_d[e * P:(e + 1) * P, :], ysb[s]).then_inc(y_out[s], 16)
                    else:
                        act.dma_start(y_d[bass.ds(e * P, P), :], ysb[s]).then_inc(y_out[s], 16)

                first(0, 0)
                turned(0, 0)
                first(1, 1)
                result(0, 0, None)
                turned(1, 1)
                first(2, 0)
                result(1, 1, None)
                turned(2, 0)
                with act.Fori(1, NE // 2 - 1) as i:
                    first(2 * i + 1, 1)
                    result(2 * i, 0, 16 * i)
                    turned(2 * i + 1, 1)
                    first(2 * i + 2, 0)
                    result(2 * i + 1, 1, 16 * i)
                    turned(2 * i + 2, 0)
                first(NE - 1, 1)
                result(NE - 2, 0, 16 * (NE // 2 - 1))
                turned(NE - 1, 1)
                if L == 0:
                    high(INB)
                result(NE - 1, 1, 16 * (NE // 2 - 1))

            def overflow(L):
                act.wait_ge(v_over, 1 + L)
                V = act.value_load(vcount[0:1, 0:1], min_val=0, max_val=MORE)
                with act.If(V > 0):
                    act.wait_ge(y_out[0], 16 * NE // 2 + 8 * NE * L)
                    with act.Fori(0, V) as i:
                        act.wait_ge(v_up[L], i + 1)
                        act.activation(tnh[0], bank(4)[:, 0:DE], ACT.Tanh, scale=0.5).then_inc(v_tanh[L], 1)
                        act.wait_ge(v_ht[L], i + 1)
                        act.activation(hidT[0], bank(2)[:, 0:2 * P].rearrange("p (f t) -> p f t", f=2), ACT.Copy
                                       ).then_inc(v_htev[L], 1)
                        act.wait_ge(v_down[L], i + 1)
                        act.activation(ysb[0].rearrange("p (b n) -> p b n", b=2), ps[:, 6:8, :], ACT.Copy
                                       ).then_inc(v_yev[L], 1)

            act.wait_ge(a_vec, 1)
            act.activation(spl[0:RW, :], spl[0:RW, :], ACT.Exp, scale=-1.0).then_inc(a_exp, 1)
            norm(0, lambda t: act.wait_ge(mem_in, 16), lambda t: xs[:, MT + t, :])
            act.wait_ge(n_ms, MT)
            norm(1, lambda t: act.wait_ge(h_in[t], 16), lambda t: arena[:, (2 + t) * D:(3 + t) * D])
            high(INA)
            kv_jobs(0)
            high(INA + 1)
            high(INA + 2)
            recurrence()
            q_jobs()
            high(OUTA + 2)
            memory_attention(0)
            high(OUTA + 3)
            norm(2, lambda t: act.wait_ge(o_ev, t + 1), lambda t: xs[:, t, :])
            routing(0)
            kv_jobs(1)
            load_bias()
            experts_act(0)
            relative_bias()
            overflow(0)
            for n in range(1, RING):
                high(INB + n)
            norm(3, lambda t: act.wait_ge(c_done, t + 1), lambda t: xs[:, t, :])
            skewed_bias()
            banks = [4 + j % 4 for j in range(24)] + [6, 7]
            pairs = [(dst, bank(b)[:, cols]) for b, (dst, cols) in zip(banks, b_jobs())]

            def store_unit(k):
                of_unit = NT if k >= 6 else 2
                stored(pairs[:of_unit])
                del pairs[:of_unit]

            for k in range(QMB - INB):
                store_unit(k)
                if INB + k + RING <= OUTB:
                    high(INB + k + RING)
            diff_attention(lambda: store_unit(QMB - INB))
            memory_attention(1)
            high(OUTB + 3)
            norm(4, lambda t: act.wait_ge(o_ev, t + 1 + NT), lambda t: xs[:, t, :])
            routing(1)
            act.dma_start(gfin, final_g.to_broadcast([P, D])).then_inc(fin_in, 16)
            experts_act(1)
            overflow(1)
            for t in range(NT):
                act.wait_ge(c_done, t + 1 + NT)
                squares(5, t, lambda t: xs[:, t, :])

        @block.vector
        def _(dve):
            links = [0]

            def link(ins):
                links[0] += 1
                ins.then_inc(dve_link, 1)
                dve.wait_ge(dve_link, links[0])

            def norm(n, turned, g, residual=None):
                nt = NORM_TILES[n]
                if residual:
                    residual(0)
                for t in range(nt + 1):
                    if residual and t + 1 < nt:
                        residual(t + 1)
                    if t < nt:
                        mean_square(n, t)
                    if t >= 1:
                        b = 2 * ((t - 1) % 2)
                        dve.wait_ge(n_tr, t + NORM_BASE[n])
                        dve.tensor_tensor(turned[:, :, (t - 1) * P:t * P],
                                          ps[:, b:b + 2, :].rearrange("p b (k t) -> p (b k) t", k=KC // 2),
                                          v(g).unsqueeze(2).to_broadcast([P, KC, P]), ALU.mult).then_inc(n_ev, 1)

                if n in (1, 3):
                    for t in range(2, NT):
                        cols = slice(t * P, (t + 1) * P)
                        dve.wait_ge(rows_hi, t + 1 + NT * (n // 2))
                        dve.tensor_tensor(hn_lo[:, :, cols], hnT[:, :, cols], hn_hi[:, :, cols].bitcast(F32), ALU.subtract
                                          ).then_inc(last_rows_lo, 1)

            def mean_square(n, t):
                dve.wait_ge(n_sq, t + 1 + NORM_BASE[n])
                dve.tensor_scalar(msq[:, t:t + 1], ssq[:, t:t + 1], 1.0 / D, EPS, ALU.mult, ALU.add).then_inc(n_ms, 1)

            def absolute_lambda():
                lam, z = v("lam")[0:RW, :], hbx[0:RW, :]
                link(dve.tensor_scalar(z, lam, -1.0, None, ALU.mult))
                dve.tensor_tensor(spl[0:RW, :], lam, z, ALU.max).then_inc(a_vec, 1)

            def channel_vectors():
                lam, s, z, z2 = v("lam")[0:RW, :], hba[0:RW, :], hbx[0:RW, :], msp[0:RW, :]
                sp = spl[0:RW, :]
                dve.wait_ge(a_exp, 1)
                link(dve.tensor_scalar(z, sp, 2.0, None, ALU.add))
                link(dve.reciprocal(z, z))
                link(dve.tensor_tensor(z, z, sp, ALU.mult))
                link(dve.tensor_tensor(z2, z, z, ALU.mult))
                link(dve.tensor_scalar(s, z2, 1.0 / 19, None, ALU.mult))
                for k in range(17, 1, -2):
                    link(dve.scalar_tensor_tensor(s, s, 1.0 / k, z2, ALU.add, ALU.mult))
                link(dve.tensor_scalar(s, s, 1.0, 4.0, ALU.add, ALU.mult))
                link(dve.tensor_tensor(s, s, z, ALU.mult))
                link(dve.tensor_scalar(z, lam, -1.0, 0.0, ALU.mult, ALU.max))
                link(dve.scalar_tensor_tensor(sp, z, 2.0, s, ALU.mult, ALU.add))
                link(dve.tensor_scalar(sp, sp, 2.0, None, ALU.mult))
                dve.tensor_scalar(msp[0:RW, :], sp, -1.0, None, ALU.mult)
                link(dve.tensor_scalar(hba[0:RW, :], v("gate_a_b")[0:RW, :], 0.5, None, ALU.mult))
                dve.tensor_scalar(hbx[0:RW, :], v("gate_x_b")[0:RW, :], 0.5, None, ALU.mult).then_inc(a_vec, 1)

            def recurrence():
                def conv(c):
                    u, o = upad[:, c % 2, :], xc[c % 2]
                    w = v("conv_w", c * CONV, (c + 1) * CONV)[0:RW, :]
                    dve.wait_ge(a_uev, c + 1)
                    if c >= 2:
                        dve.wait_ge(a_gates, c - 1)
                        dve.wait_ge(a_cat, c - 1)
                    link(dve.tensor_scalar(o, u[:, 0:T], w[:, 0:1], v("conv_b", c, c + 1)[0:RW, :], ALU.mult, ALU.add))
                    for j in range(1, CONV):
                        ins = dve.scalar_tensor_tensor(o, u[:, j:j + T], w[:, j:j + 1], o, ALU.mult, ALU.add)
                        if j < CONV - 1:
                            link(ins)
                    ins.then_inc(a_xc, 1)

                def decay(c):
                    ug = gelu_bank(c)[0:RW, :]
                    dve.wait_ge(a_T, c + 1)
                    if c >= 1:
                        dve.wait_ge(a_sqrt, c)
                    link(dve.tensor_tensor(dd, ra[c % 2], ra[c % 2], ALU.mult))
                    dve.scalar_tensor_tensor(dd, dd, 1.0, ta, ALU.add, ALU.mult).then_inc(a_q, 1)
                    dve.wait_ge(a_gsq, c + 1)
                    link(dve.tensor_scalar(gq, gq, 0.044715, 1.0, ALU.mult, ALU.add))
                    dve.tensor_tensor(gq, gq, ug, ALU.mult).then_inc(a_g3, 1)
                    link(dve.scalar_tensor_tensor(tx[c % 2], tx[c % 2], 1.0, xc[c % 2], ALU.add, ALU.mult))

                def scan(c):
                    ug = gelu_bank(c)[0:RW, :]
                    b = tx[c % 2]
                    dve.wait_ge(a_tg, c + 1)
                    dve.scalar_tensor_tensor(gg, gg, 1.0, ug, ALU.add, ALU.mult)
                    dve.wait_ge(a_sqrt, c + 1)
                    if c >= 2:
                        dve.wait_ge(rec_put[c % 2], 16 * pieces_put(c - 2))
                    link(dve.scalar_tensor_tensor(b, b, 0.5, sq, ALU.mult, ALU.mult))
                    link(dve.tensor_tensor_scan(sq, ra[c % 2], b, 0.0, ALU.mult, ALU.add))
                    dve.scalar_tensor_tensor(rec_out[c % 2], sq, 0.5, gg, ALU.mult, ALU.mult).then_inc(a_cat, 1)

                for c in range(RB + 2):
                    if c >= 2:
                        scan(c - 2)
                    if c < RB:
                        conv(c)
                    if 1 <= c <= RB:
                        decay(c - 1)

            def subnorm(b):
                dve.wait_ge(d_oev, HEADS * (b + 1))
                if b >= 1:
                    dve.wait_ge(d_ot, 2 * b)
                link(dve.tensor_tensor(On, Osb, Osb, ALU.mult))
                link(dve.tensor_reduce(ossq, On, AXX, ALU.add))
                dve.tensor_scalar(ossq, ossq, 1.0 / P, EPS, ALU.mult, ALU.add).then_inc(d_ms, 1)
                dve.wait_ge(d_rs, b + 1)
                dve.tensor_tensor(On, Osb, orstd.unsqueeze(2).to_broadcast([P, HEADS, P]), ALU.mult).then_inc(d_on, 1)

            def memory_attention(L):
                n = len(MSTEPS)
                for i in range(n + 1):
                    if i < n:
                        s = i % 2
                        dve.wait_ge(m_s, i + 1 + MS * L)
                        link(dve.tensor_reduce(mx[:, s, :], ps[:, 2 * s:2 * s + 2, 0:MEM], AXX, ALU.max))
                        dve.tensor_scalar(nmx[:, s, :], mx[:, s, :], -DH ** -0.5, None, ALU.mult).then_inc(m_nmx, 1)
                    if i >= 1:
                        s = (i - 1) % 2
                        dve.wait_ge(m_exp, i + MS * L)
                        if i == 1 and L == 1:
                            dve.wait_ge(d_oev, len(STEPS))
                        link(dve.reciprocal(rec[:, s, :], rsum[:, s, :]))
                        e = E[(i - 1) % 3][:, :, 0:MEM]
                        dve.tensor_tensor(e, e,
                                          rec[:, s, :].unsqueeze(2).to_broadcast([P, 2, MEM]), ALU.mult).then_inc(m_p, 1)
                    if i == 1 and L == 1:
                        subnorm(NT - 1)

            def output(L, t):
                dve.wait_ge(o_mm, t + 1 + NT * L)
                ht = h[:, t, :].rearrange("p (b n) -> p b n", b=2)
                dve.tensor_tensor(ht, ps[:, 2 * t:2 * t + 2, :], ht, ALU.add).then_inc(o_ev, 1)

            def routing(L):
                def bc(a, axis, shape):
                    return a.unsqueeze(axis).to_broadcast(shape)

                def first_max(src, n_max, eq, ji, oh):
                    link(dve.tensor_reduce(n_max, src, AXX, ALU.max))
                    link(dve.tensor_tensor(eq, src, bc(n_max, 2, [P, NT, 4]), ALU.is_equal))
                    link(dve.tensor_tensor(eq, eq, bc(iota4, 1, [P, NT, 4]), ALU.mult))
                    link(dve.tensor_reduce(ji, eq, AXX, ALU.min))
                    link(dve.tensor_tensor(oh, bc(iota4, 1, [P, NT, 4]), bc(ji, 2, [P, NT, 4]), ALU.is_equal))

                dve.wait_ge(r_lgev, 1 + L)
                g, el = lg[:, :, 0:NG], lg[:, :, NG:NG + NE]
                first_max(g, r_gmax, r_eqg, r_gi, ohg)
                dve.tensor_tensor(rg_e, g, bc(r_gmax, 2, [P, NT, NG]), ALU.subtract).then_inc(r_exp, 1)
                for t in range(NT):
                    last = dve.tensor_tensor(r_prod[:, t, :, :], el[:, t, :].rearrange("p (g j) -> p g j", g=NG),
                                             bc(ohg[:, t, :], 2, [P, NG, EPG]), ALU.mult)
                link(last)
                link(dve.tensor_reduce(e_in, r_prod.rearrange("p t g j -> p t j g"), AXX, ALU.add))
                first_max(e_in, r_m1, r_eqe, r_ji, oh1)
                link(dve.scalar_tensor_tensor(e_in, oh1, NEG, e_in, ALU.mult, ALU.add))
                first_max(e_in, r_m2, r_eqe, r_ji, oh2)
                dve.tensor_tensor(rdiff, r_m2, r_m1, ALU.subtract).then_inc(r_exp, 1)
                for t in range(NT):
                    for o, oh in ((ohe1, oh1), (ohe2, oh2)):
                        last = dve.tensor_tensor(o[:, t, :].rearrange("p (g j) -> p g j", g=NG),
                                                 bc(ohg[:, t, :], 2, [P, NG, EPG]), bc(oh[:, t, :], 1, [P, NG, EPG]), ALU.mult)
                link(last)
                dve.tensor_tensor(sel, ohe1, ohe2, ALU.add).then_inc(r_sel, 1)
                dve.wait_ge(r_pexp, 1 + 2 * L)
                link(dve.tensor_reduce(r_gsum, rg_e, AXX, ALU.add))
                link(dve.reciprocal(r_gw, r_gsum))
                dve.wait_ge(r_pexp, 2 + 2 * L)
                link(dve.tensor_scalar(r_den, rdiff, 1.0, None, ALU.add))
                link(dve.reciprocal(r_den, r_den))
                link(dve.tensor_tensor(wv1, r_den, r_gw, ALU.mult))
                link(dve.tensor_tensor(wv2, rdiff, wv1, ALU.mult))
                dve.wait_ge(r_rank, 1 + L)
                link(dve.tensor_copy(r_cnt, bank(5)[:, 64:128].rearrange("p (t e) -> p t e", t=NT)))
                link(dve.tensor_scalar(r_off[:, 0, :], r_cnt[:, 0, :], 0.0, None, ALU.mult))
                for t in range(1, NT):
                    link(dve.tensor_tensor(r_off[:, t, :], r_off[:, t - 1, :], r_cnt[:, t - 1, :], ALU.add))
                link(dve.tensor_tensor(ntot, r_off[:, NT - 1, :], r_cnt[:, NT - 1, :], ALU.add))
                link(dve.tensor_tensor(r_rankv, bank(5)[:, 0:64].rearrange("p (t e) -> p t e", t=NT), r_off, ALU.add))
                link(dve.scalar_tensor_tensor(rk, r_rankv, 1.0, sel, ALU.add, ALU.mult))
                link(dve.tensor_scalar(rk, rk, -1.0, None, ALU.add))

                def hot(e):
                    if e >= 2:
                        dve.wait_ge(r_idx, e - 1 + NE * L)
                    dve.tensor_tensor(onesl[e % 2], bc(iota[:, :], 1, [P, NT, P]), bc(rk[:, :, e], 2, [P, NT, P]), ALU.is_equal
                                      ).then_inc(r_hot, 1)

                hot(0)
                hot(1)
                dve.wait_ge(r_idx, 2 + NE * L)
                dve.tensor_copy(idxi[:, 0:2], bank(3)[:, 0:2]).then_inc(r_idxi, 1)
                hot(2)
                hot(3)
                dve.wait_ge(r_idx, 4 + NE * L)
                dve.tensor_copy(idxi[:, 2:4], bank(3)[:, 2:4]).then_inc(r_idxi, 1)

            def hot_pair(L, e):
                for s in range(2):
                    dve.wait_ge(r_idx, e + s - 1 + NE * L)
                    dve.tensor_tensor(onesl[s], iota[:, :].unsqueeze(1).to_broadcast([P, NT, P]),
                                      rk[:, :, bass.ds(e + s, 1)].to_broadcast([P, NT, P]), ALU.is_equal).then_inc(r_hot, 1)
                dve.wait_ge(r_idx, e + 2 + NE * L)
                dve.tensor_copy(idxi[:, bass.ds(e, 2)], bank(3)[:, 0:2]).then_inc(r_idxi, 1)

            def slots(L):
                def bc(a, axis, shape):
                    return a.unsqueeze(axis).to_broadcast(shape)

                for j in range(1, NT):
                    last = dve.tensor_scalar(r_over[:, :, j - 1], ntot, float(j * P), None, ALU.is_gt)
                link(last)
                flat = r_over.rearrange("p e j -> p (e j)")
                cum = r_cum.rearrange("p e j -> p (e j)")
                link(dve.tensor_tensor_scan(cum, ones[:, 0:NE * 3], flat, 0.0, ALU.mult, ALU.add))
                link(dve.tensor_tensor(vidx, r_cum, r_over, ALU.mult))
                link(dve.memset(vc, 0.0))
                dve.tensor_copy(vcount, cum[:, NE * 3 - 1:NE * 3]).then_inc(v_over, 1)
                link(dve.tensor_tensor(r_base, r_cum[:, :, 0], r_over[:, :, 0], ALU.subtract))
                link(dve.tensor_scalar(r_base, r_base, float(P), float((NE - 1) * P), ALU.mult, ALU.add))
                link(dve.tensor_tensor(r_base, r_base, row16, ALU.subtract))
                link(dve.tensor_scalar(r_slot, r_rankv, float(P), None, ALU.is_ge))
                link(dve.tensor_tensor(r_slot, r_slot, bc(r_base, 1, [P, NT, NE]), ALU.mult))
                link(dve.tensor_tensor(r_slot, r_slot, r_rankv, ALU.add))
                link(dve.tensor_tensor(r_slot, r_slot, bc(row16, 1, [P, NT, NE]), ALU.add))
                link(dve.tensor_tensor(ohe1, ohe1, r_slot, ALU.mult))
                link(dve.tensor_tensor(ohe2, ohe2, r_slot, ALU.mult))
                link(dve.tensor_reduce(r_r1, ohe1, AXX, ALU.add))
                link(dve.tensor_reduce(r_r2, ohe2, AXX, ALU.add))
                link(dve.tensor_copy(r1i, r_r1))
                dve.tensor_copy(r2i, r_r2).then_inc(r_done, 1)

            def turned_rows(L, s):
                return dve.tensor_tensor(xgT[s], ps[:, 0:2, :].rearrange("p b (k t) -> p (b k) t", k=KC // 2),
                                         v(f"ffn{L}").unsqueeze(2).to_broadcast([P, KC, P]), ALU.mult)

            def gated(s):
                return dve.scalar_tensor_tensor(tnh[s], tnh[s], 1.0, bank(4 + s)[:, 0:DE], ALU.add, ALU.mult)

            def hidden(s):
                return dve.scalar_tensor_tensor(hid[s], tnh[s], 0.5, bank(4 + s)[:, DE:2 * DE], ALU.mult, ALU.mult)

            def experts_dve(L):
                def rows(e, s, reused=True):
                    dve.wait_ge(x_tr, e + 1 + NE * L)
                    if reused:
                        dve.wait_ge(e_up, e - 1 + NE * L)
                    turned_rows(L, s).then_inc(x_ev, 1)

                def hidden_of(e, s, reused=True):
                    dve.wait_ge(e_tanh, e + 1 + NE * L)
                    gated(s).then_inc(e_gate, 1)
                    if reused:
                        dve.wait_ge(e_ht, e - 1 + NE * L)
                    dve.wait_ge(e_gate, e + 1 + NE * L)
                    hidden(s).then_inc(e_hid, 1)

                rows(0, 0, False)
                hidden_of(0, 0, False)
                rows(1, 1, False)
                hidden_of(1, 1, False)
                rows(2, 0)
                slots(L)
                with dve.Fori(1, NE // 2 - 1) as i:
                    hot_pair(L, 2 * i + 2)
                    hidden_of(2 * i, 0)
                    rows(2 * i + 1, 1)
                    hidden_of(2 * i + 1, 1)
                    rows(2 * i + 2, 0)
                hidden_of(NE - 2, 0)
                rows(NE - 1, 1)
                hidden_of(NE - 1, 1)

            def overflow(L):
                dve.wait_ge(v_over, 1 + L)
                V = dve.value_load(vcount[0:1, 0:1], min_val=0, max_val=MORE)
                steps = 12
                with dve.If(V > 0):
                    with dve.Fori(0, V) as i:
                        at = [0]

                        def vlink(ins):
                            at[0] += 1
                            ins.then_inc(v_link[L], 1)
                            dve.wait_ge(v_link[L], i * steps + at[0])

                        dve.wait_ge(v_free[L], i + 1)
                        vlink(dve.tensor_scalar(vc, vc, 1.0, None, ALU.add))
                        vlink(dve.tensor_scalar(v_m, vidx, vc, None, ALU.is_equal))
                        vlink(dve.tensor_reduce(v_eoh, v_m, AXX, ALU.add))
                        vlink(dve.tensor_tensor(v_m, v_m, jcol, ALU.mult))
                        vlink(dve.tensor_reduce(v_jv, v_m.rearrange("p e j -> p (e j)"), AXX, ALU.add))
                        vlink(dve.tensor_tensor(v_rr, rk, v_eoh.unsqueeze(1).to_broadcast([P, NT, NE]), ALU.mult))
                        vlink(dve.tensor_reduce(v_rk, v_rr, AXX, ALU.add))
                        vlink(dve.tensor_scalar(v_rk, v_rk, v_jv, None, ALU.subtract))
                        vlink(dve.tensor_tensor(v_t16, v_eoh, iota16, ALU.mult))
                        vlink(dve.tensor_reduce(v_es, v_t16, AXX, ALU.add))
                        vlink(dve.tensor_copy(vsteer, v_es))
                        dve.tensor_tensor(onesl[0], iota[:, :].unsqueeze(1).to_broadcast([P, NT, P]),
                                          v_rk.unsqueeze(2).to_broadcast([P, NT, P]), ALU.is_equal).then_inc(v_hot[L], 1)
                        dve.wait_ge(v_idx[L], i + 1)
                        dve.tensor_copy(ovi, bank(3)[:, 0:1]).then_inc(v_idxi[L], 1)
                        dve.wait_ge(v_tr[L], i + 1)
                        turned_rows(L, 0).then_inc(v_ev[L], 1)
                        dve.wait_ge(v_tanh[L], i + 1)
                        vlink(gated(0))
                        assert at[0] == steps
                        hidden(0).then_inc(v_hid[L], 1)

            def combine(L, t):
                if L == 0 and t == 1:
                    dve.wait_ge(b_out, 16 * HEADS)
                dve.wait_ge(c_full[t], 32 + 32 * L)
                link(dve.scalar_tensor_tensor(h[:, t, :], comb[t][0], wv1[:, t:t + 1], h[:, t, :], ALU.mult, ALU.add))
                dve.scalar_tensor_tensor(h[:, t, :], comb[t][1], wv2[:, t:t + 1], h[:, t, :], ALU.mult, ALU.add
                                         ).then_inc(c_done, 1)

            def lambda_and_bias():
                dve.wait_ge(b_load, 48)
                lv = lall.rearrange("p (a b d) -> p a b d", a=2, b=2)
                link(dve.tensor_tensor(lprod, lv[:, :, 0, :], lv[:, :, 1, :], ALU.mult))
                dve.tensor_reduce(lsum, lprod, AXX, ALU.add).then_inc(l_sum, 1)
                dve.tensor_copy(relrep, relsb.unsqueeze(2).to_broadcast([REL, HEADS, P])).then_inc(b_rep, 1)
                dve.wait_ge(l_exp, 1)
                link(dve.tensor_tensor(neglam, lexp[:, 1:2], lexp[:, 0:1], ALU.subtract))
                link(dve.tensor_scalar(neglam, neglam, -LAMBDA_INIT, None, ALU.add))
                link(dve.tensor_scalar(gsub, v("subln"), 1.0 - LAMBDA_INIT, None, ALU.mult))

            def diff_attention():
                def scores(i):
                    b, hd = STEPS[i]
                    s, nk = i % 2, (b + 1) * P
                    near = min(nk, NEAR)
                    far = nk - near
                    S = ps[:, 2 * s:2 * s + 2, :]
                    dve.wait_ge(d_s, i + 1)
                    if i >= 3:
                        dve.wait_ge(d_pt, i - 2)
                    if far:
                        dve.wait_ge(d_far, i + 1)
                    last = dve.scalar_tensor_tensor(E[i % 3][:, :, far:nk], S[:, :, far:nk], DH ** -0.5,
                                                    bias[:, hd, NEAR - near:NEAR].unsqueeze(1).to_broadcast([P, 2, near]),
                                                    ALU.mult, ALU.add)
                    link(last)
                    link(dve.tensor_reduce(mx[:, s, :], E[i % 3][:, :, 0:nk], AXX, ALU.max))
                    dve.tensor_scalar(nmx[:, s, :], mx[:, s, :], -1.0, None, ALU.mult).then_inc(d_nmx, 1)

                def weights(i):
                    b, hd = STEPS[i]
                    s, nk, e = i % 2, (b + 1) * P, E[i % 3]
                    dve.wait_ge(d_exp, i + 1)
                    if i >= 4:
                        dve.wait_ge(d_oev, i - 3)
                    link(dve.reciprocal(rec[:, i % 4, :], rsum[:, s, :]))
                    link(dve.scalar_tensor_tensor(ratio, rec[:, i % 4, 1:2], neglam, rsum[:, s, 0:1], ALU.mult, ALU.mult))
                    dve.scalar_tensor_tensor(e[:, 0, 0:nk], e[:, 1, 0:nk], ratio, e[:, 0, 0:nk],
                                             ALU.mult, ALU.add).then_inc(d_p, 1)

                n = len(STEPS)
                dve.wait_ge(b_mask, 1)
                for i in range(n + 1):
                    if i < n:
                        scores(i)
                    if i >= 1:
                        weights(i - 1)
                    if i % HEADS == 2 and i > HEADS:
                        subnorm(i // HEADS - 1)

            dve.wait_ge(vec_in, 16)
            dve.memset(upad[:, :, 0:3], 0.0).then_inc(dve_const, 1)
            absolute_lambda()
            norm(0, memT, "mem")
            norm(1, hnT, "mix0")
            channel_vectors()
            recurrence()
            memory_attention(0)
            norm(2, hnT, "ffn0", lambda t: output(0, t))
            routing(0)
            experts_dve(0)
            lambda_and_bias()
            overflow(0)
            norm(3, hnT, "mix1", lambda t: combine(0, t))
            diff_attention()
            memory_attention(1)
            norm(4, hnT, "ffn1", lambda t: output(1, t))
            routing(1)
            experts_dve(1)
            overflow(1)
            for t in range(NT + 2):
                if t < NT:
                    combine(1, t)
                if 1 <= t <= NT:
                    mean_square(5, t - 1)
                if t == 2:
                    dve.wait_ge(fin_in, 16)
                if t >= 2:
                    dve.wait_ge(n_rs, t - 1 + NORM_BASE[5])
                    dve.scalar_tensor_tensor(xs[:, t - 2, :], h[:, t - 2, :], rstd[:, t - 2:t - 1], gfin, ALU.mult, ALU.mult
                                             ).then_inc(fin_row, 1)

        @block.tensor
        def _(pe):
            mm = nc.tensor.matmul
            ALL = slice(None)
            hn, cats = (hn_hi, hn_lo), (cat_hi, cat_lo)

            def whole_unit(n):
                pe.wait_ge(ring_full[n % RING], 16 * (n // RING + 1))
                return ring[:, n % RING, :]

            def unit(n, k=KC):
                pe.wait_ge(unit_lo, split_before(n) + 1)
                return [r[:, n % RING, :].rearrange("p (k n) -> p k n", k=k) for r in (ring_hi, ring_lo)]

            def both_of(parts, *at):
                return tuple(part[at] for part in parts)

            def passes(pairs):
                for (wh, wl), (mh, ml) in pairs:
                    yield wh, mh
                    yield wh, ml
                    yield wl, mh

            def chain(dst, pairs):
                pairs = list(pairs)
                for k, (lhsT, rhs) in enumerate(pairs):
                    ins = mm(dst, lhsT, rhs, start=(k == 0), stop=(k == len(pairs) - 1))
                return ins

            def turn_rows(n, L=None):
                for t in range(NORM_TILES[n]):
                    b = 2 * (t % 2)
                    pe.wait_ge(n_xs, t + 1 + NORM_BASE[n])
                    if t >= 2 or n == 1:
                        pe.wait_ge(n_ev, t - 1 + NORM_BASE[n])
                    elif t == 1 and L is not None:
                        pe.wait_ge(o_ev, 2 + NT * L)
                    for k in range(KC):
                        ins = nc.tensor.transpose(ps[:, b + k // 4, (k % 4) * P:(k % 4 + 1) * P],
                                                  xs[:, t, k * P:(k + 1) * P], ident[:, :])
                    ins.then_inc(n_tr, 1)
                    if L is not None and t >= 1:
                        logits(L, t - 1)
                if L is not None:
                    logits(L, NT - 1)

            def logits(L, t):
                if t == 0:
                    pe.wait_ge(o_ev, NT + NT * L)
                    if L == 0:
                        pe.wait_ge(small_in, 32)
                pe.wait_ge(n_ev, t + 1 + NORM_BASE[2 + 2 * L])
                if t >= 2:
                    pe.wait_ge(r_ltev, t - 1 + NT * L)
                chain(bank(5 + t % 2)[0:NG + NE, 0:P],
                      ((wgr[:, L, k, :], hnT[:, k, t * P:(t + 1) * P]) for k in range(KC))).then_inc(r_lt, 1)

            jobs = [0]

            def job(dst, banks, pairs):
                n = jobs[0]
                if n >= banks:
                    pe.wait_ge(job_ev, n - banks + 1)
                jobs[0] += 1
                ins = chain(dst, pairs)
                ins.then_inc(job_mm, 1)

            def used(n):
                pe.wait_ge(job_mm, jobs[0])
                pe.sem_inc(unit_used, 1)

            def kv_keys(n0):
                w = whole_unit(n0).rearrange("p (k n) -> p k n", k=KC)
                for c in range(2):
                    job(bank(6 + c)[:, 0:MEM], 2, ((w[:, k, c * P:(c + 1) * P], memT[:, k, :]) for k in range(KC)))
                used(n0)

            def kv_values(n0, c):
                first = value_bank(0 if n0 == KV0 else 1)
                w = whole_unit(n0 + 1).rearrange("p (k n) -> p k n", k=KC)
                job(bank(first + c)[:, 0:256], 8 - first, ((memT[:, k, c * P:(c + 1) * P], w[:, k, :]) for k in range(KC)))
                if c == MT - 1:
                    used(n0 + 1)

            def recurrence():
                def project(c, j, dst):
                    w = unit(INA + c)
                    return chain(dst[0:RW, :], passes(
                        (both_of(w, ALL, k, slice(j * P, j * P + RW)), both_of(hn, ALL, k, ALL)) for k in range(KC)))

                def inputs(c):
                    if c >= 2:
                        pe.wait_ge(a_uev, c - 1)
                    project(c, 0, bank(c % 2)).then_inc(a_ux, 1)

                def gelu_inputs(c):
                    if c >= 3:
                        pe.wait_ge(a_cat, c - 2)
                    project(c, 1, gelu_bank(c)).then_inc(a_ug, 1)
                    pe.wait_ge(a_ug, c + 1)
                    pe.sem_inc(unit_used, 1)

                def gates(c):
                    pe.wait_ge(a_xc, c + 1)
                    if c >= 1:
                        pe.wait_ge(a_T, c)
                    else:
                        pe.wait_ge(job_ev, jobs[0])
                        pe.wait_ge(gate_in, 16)
                    mm(bank(4)[0:RW, :], gw[:, 0, c, :], xc[c % 2], start=True, stop=True)
                    mm(bank(5)[0:RW, :], gw[:, 1, c, :], xc[c % 2], start=True, stop=True).then_inc(a_gates, 1)

                for c in range(RB):
                    inputs(c)
                    if c >= 1:
                        gates(c - 1)
                    gelu_inputs(c)
                gates(RB - 1)

            def q_memory(n):
                w = unit(n)
                pe.wait_ge(a_cat, RB - 2)
                for c in range(2):
                    job(bank(6 + c), 2, passes(
                        (both_of(w, ALL, k, slice(c * P, (c + 1) * P)), both_of(hn, ALL, k, ALL)) for k in range(KC)))
                used(n)

            def turn_out(b):
                pe.wait_ge(d_on, b + 1)
                if b == 0:
                    pe.wait_ge(job_ev, jobs[0])
                if b >= 1:
                    pe.wait_ge(d_otev, 2 * b)
                for j, (a, n) in enumerate(((0, 4), (4, 2))):
                    for c in range(n):
                        ins = nc.tensor.transpose(bank(6 + j)[:, c * P:(c + 1) * P], On[:, a + c, :], ident[:, :])
                    ins.then_inc(d_ot, 1)

            def memory_attention(L):
                def scores(i):
                    t, hp = MSTEPS[i]
                    if i >= 2:
                        pe.wait_ge(m_exp, i - 1 + MS * L)
                    for n in range(2):
                        r = slice(n * DH, (n + 1) * DH)
                        ins = mm(bank(2 * (i % 2) + n)[:, 0:MEM], qmT[r, hp, t * P:(t + 1) * P], kTm[r, hp, :],
                                 start=True, stop=True)
                    ins.then_inc(m_s, 1)

                def turn(i):
                    s = i % 2
                    pe.wait_ge(m_p, i + 1 + MS * L)
                    if i >= 2:
                        pe.wait_ge(m_ptev, i - 1 + MS * L)
                    for n in range(2):
                        for c in range(MT):
                            j = n * MT + c
                            ins = nc.tensor.transpose(bank(4 + s)[:, j * P:(j + 1) * P], E[i % 3][:, n, c * P:(c + 1) * P], ident[:, :])
                    ins.then_inc(m_pt, 1)

                def values(i):
                    t, hp = MSTEPS[i]
                    s = i % 2
                    pe.wait_ge(m_ptev, i + 1 + MS * L)
                    if i >= 2:
                        pe.wait_ge(m_oev, i - 1 + MS * L)
                    for n in range(2):
                        hd = 2 * hp + n
                        ins = chain(bank(6 + s)[n * DH:(n + 1) * DH, 0:P],
                                    ((vm[:, c, hd * DH:(hd + 1) * DH], PTs[s][:, n * MT + c, :]) for c in range(MT)))
                    ins.then_inc(m_o, 1)

                n = len(MSTEPS)
                pe.wait_ge(job_ev, jobs[0])
                if L == 0:
                    pe.wait_ge(a_cat, RB)
                else:
                    pe.wait_ge(d_nmx, len(STEPS))
                scores(0)
                for i in range(n + 2):
                    if i + 1 < n:
                        scores(i + 1)
                    if i == 1 and L == 1:
                        pe.wait_ge(d_ptev, len(STEPS))
                        pe.wait_ge(d_oev, len(STEPS))
                    if 1 <= i <= n:
                        turn(i - 1)
                    if i == 2 and L == 1:
                        turn_out(NT - 1)
                        pe.wait_ge(d_otev, 2 * NT)
                    if i >= 2:
                        values(i - 2)

            def output(L):
                pe.wait_ge(m_oev, MS + MS * L)
                n0, chunks = (OUTA, OUTB)[L], 2 * CAT_PAIRS
                for j in range(chunks):
                    w = unit(n0 + j // 2, 2)
                    pe.wait_ge(cat_lows, j // 2 + 1 + CAT_PAIRS * L)
                    last = j == chunks - 1
                    for t in range(NT):
                        for b in range(2):
                            for k, (lhsT, rhs) in enumerate(passes(
                                    [(both_of(cats, ALL, j, slice(t * P, (t + 1) * P)),
                                      both_of(w, ALL, j % 2, slice(b * 512, (b + 1) * 512)))])):
                                ins = mm(bank(2 * t + b), lhsT, rhs, start=(j == 0 and k == 0), stop=(last and k == 2))
                        if last:
                            ins.then_inc(o_mm, 1)
                    if j % 2 == 1 and not last:
                        ins.then_inc(unit_used, 1)
                pe.wait_ge(o_mm, NT + NT * L)
                pe.sem_inc(unit_used, 1)

            def routing(L):
                pe.wait_ge(r_ltev, NT + NT * L)
                for t in range(NT):
                    ins = nc.tensor.transpose(bank(4)[:, t * (NG + NE):(t + 1) * (NG + NE)], lgT[:, t * P:(t + 1) * P],
                                              ident[0:NG + NE, 0:NG + NE])
                ins.then_inc(r_lg, 1)
                if L == 0:
                    kv_keys(KV1)
                pe.wait_ge(r_sel, 1 + L)
                mm(bank(5)[:, 0:64], before[:, :], sel.rearrange("p t e -> p (t e)"), start=True, stop=True)
                mm(bank(5)[:, 64:128], ones[:, :], sel.rearrange("p t e -> p (t e)"), start=True, stop=True).then_inc(r_rank, 1)
                if L == 0:
                    kv_values(KV1, 0)
                for e in range(4):
                    slot_tokens(L, e, e % 2, e)
                if L == 0:
                    kv_values(KV1, 1)

            def slot_tokens(L, e, s, column):
                pe.wait_ge(r_hot, e + 1 + NE * L)
                chain(bank(3)[:, column:column + 1], ((onesl[s][:, c, :], tokid[:, c:c + 1]) for c in range(NT))
                      ).then_inc(r_idx, 1)

            def turn_tile(s):
                for k in range(KC):
                    ins = nc.tensor.transpose(ps[:, k // 4, (k % 4) * P:(k % 4 + 1) * P], xg[s][:, k * P:(k + 1) * P], ident[:, :])
                return ins

            def up_tile(s):
                w = w_up[s].rearrange("p (k n) -> p k n", k=KC)
                return chain(bank(4 + s), ((xgT[s][:, k, :], w[:, k, :]) for k in range(KC)))

            def turn_hidden(s):
                for f in range(2):
                    ins = nc.tensor.transpose(bank(2)[:, f * P:(f + 1) * P], hid[s][:, f * P:(f + 1) * P], ident[:, :])
                return ins

            def down_tile(s):
                w = w_down[s].rearrange("p (f n) -> p f n", f=2)
                for b in range(2):
                    ins = chain(bank(6 + b), ((hidT[s][:, f, :], w[:, f, b * 512:(b + 1) * 512]) for f in range(2)))
                return ins

            def experts_pe(L):
                def turn(e, s, use, reused=True):
                    pe.wait_ge(x_full[s], 16 * use + 8 * NE * L)
                    if reused:
                        pe.wait_ge(x_ev, e + NE * L)
                    turn_tile(s).then_inc(x_tr, 1)

                def up(e, s, use, reused=True):
                    pe.wait_ge(up_full[s], 16 * use + 16 * (NE // 2) * L)
                    if reused:
                        pe.wait_ge(e_hid, e - 1 + NE * L)
                    pe.wait_ge(x_ev, e + 1 + NE * L)
                    up_tile(s).then_inc(e_up, 1)

                def down(e, s, use, reused=True):
                    pe.wait_ge(down_full[s], 16 * use + 16 * (NE // 2) * L)
                    if reused:
                        pe.wait_ge(e_yev, e + NE * L)
                    pe.wait_ge(e_htev, e + 1 + NE * L)
                    down_tile(s).then_inc(e_down, 1)

                def turn_h(e, s, reused=True):
                    if reused:
                        pe.wait_ge(e_htev, e + NE * L)
                    pe.wait_ge(e_hid, e + 1 + NE * L)
                    turn_hidden(s).then_inc(e_ht, 1)

                turn(0, 0, 1, False)
                up(0, 0, 1, False)
                turn(1, 1, 1)
                turn_h(0, 0, False)
                up(1, 1, 1, False)
                turn(2, 0, 2)
                down(0, 0, 1, False)
                turn_h(1, 1)
                with pe.Fori(1, NE // 2 - 1) as i:
                    up(2 * i, 0, i + 1)
                    pe.wait_ge(r_idxi, i + 1 + (NE // 2) * L)
                    slot_tokens(L, 2 * i + 2, 0, 0)
                    slot_tokens(L, 2 * i + 3, 1, 1)
                    turn(2 * i + 1, 1, i + 1)
                    down(2 * i - 1, 1, i)
                    turn_h(2 * i, 0)
                    up(2 * i + 1, 1, i + 1)
                    turn(2 * i + 2, 0, i + 2)
                    down(2 * i, 0, i + 1)
                    turn_h(2 * i + 1, 1)
                h8 = NE // 2
                up(NE - 2, 0, h8)
                turn(NE - 1, 1, h8)
                down(NE - 3, 1, h8 - 1)
                turn_h(NE - 2, 0)
                up(NE - 1, 1, h8)
                down(NE - 2, 0, h8)
                turn_h(NE - 1, 1)
                down(NE - 1, 1, h8)

            def overflow(L):
                pe.wait_ge(v_over, 1 + L)
                V = pe.value_load(vcount[0:1, 0:1], min_val=0, max_val=MORE)
                with pe.If(V > 0):
                    with pe.Fori(0, V) as i:
                        pe.wait_ge(v_hot[L], i + 1)
                        chain(bank(3)[:, 0:1], ((onesl[0][:, c, :], tokid[:, c:c + 1]) for c in range(NT))).then_inc(v_idx[L], 1)
                        pe.wait_ge(v_xfull[L], 16 * i + 16)
                        turn_tile(0).then_inc(v_tr[L], 1)
                        pe.wait_ge(v_wfull[L], 32 * i + 32)
                        pe.wait_ge(v_ev[L], i + 1)
                        up_tile(0).then_inc(v_up[L], 1)
                        pe.wait_ge(v_hid[L], i + 1)
                        turn_hidden(0).then_inc(v_ht[L], 1)
                        pe.wait_ge(v_htev[L], i + 1)
                        pe.wait_ge(e_yev, NE + NE * L)
                        down_tile(0).then_inc(v_down[L], 1)

            def relative_bias():
                pe.wait_ge(b_rep, 1)
                pe.wait_ge(x_ev, NE)
                for hd in range(HEADS):
                    if hd >= 2:
                        pe.wait_ge(b_ev, hd - 1)
                    mm(bank(hd % 2)[:, 0:REVLEN], relrep[:, hd, :], hotsb, start=True, stop=True).then_inc(b_mm, 1)

            def project_b():
                j = [0]

                def columns(w, m):
                    return passes((both_of(w, ALL, k, slice(m * P, (m + 1) * P)), both_of(hn, ALL, k, ALL)) for k in range(KC))

                for c in range(HEADS // 2):
                    for o in range(2):
                        w = unit(INB + 2 * c + o)
                        for m in range(2):
                            job(bank(4 + j[0] % 4), 4, columns(w, m))
                            j[0] += 1
                        used(INB + 2 * c + o)
                for c in range(3):
                    w = unit(INB + 6 + c)
                    for t in range(NT):
                        job(bank(4 + j[0] % 4)[:, 0:256], 4, passes(
                            (both_of(hn, ALL, k, slice(t * P, (t + 1) * P)), both_of(w, ALL, k, ALL)) for k in range(KC)))
                        j[0] += 1
                    used(INB + 6 + c)

                def queries():
                    w = unit(QMB)
                    for c in range(2):
                        job(bank(6 + c), 4, columns(w, c))
                    used(QMB)

                return queries

            def diff_attention(queries):
                def scores(i):
                    b, hd = STEPS[i]
                    s, nk = i % 2, (b + 1) * P
                    if i >= 2:
                        pe.wait_ge(d_nmx, i - 1)
                    for n in range(2):
                        r = slice(n * DH, (n + 1) * DH)
                        ins = mm(bank(2 * s + n)[:, 0:nk], qT[r, hd, b * P:(b + 1) * P], kT[r, hd, 0:nk], start=True, stop=True)
                    ins.then_inc(d_s, 1)

                def turn(i):
                    b, hd = STEPS[i]
                    s = i % 2
                    pe.wait_ge(d_p, i + 1)
                    if i >= 1:
                        pe.wait_ge(d_ptev, i)
                    for c in range(b + 1):
                        ins = nc.tensor.transpose(bank(4)[:, c * P:(c + 1) * P], E[i % 3][:, 0, c * P:(c + 1) * P], ident[:, :])
                    ins.then_inc(d_pt, 1)

                def values(i):
                    b, hd = STEPS[i]
                    pe.wait_ge(d_ptev, i + 1)
                    if i >= 1:
                        pe.wait_ge(d_oev, i)
                    chain(bank(5)[:, 0:P], ((PTs[i % 2][:, c, :], vB[:, c, hd * P:(hd + 1) * P]) for c in range(b + 1))
                          ).then_inc(d_o, 1)

                n = len(STEPS)
                pe.wait_ge(job_ev, jobs[0])
                scores(0)
                for i in range(n + 2):
                    if i + 1 < n:
                        scores(i + 1)
                    if i == 0:
                        queries()
                    if i >= 2:
                        values(i - 2)
                    if 1 <= i <= n:
                        turn(i - 1)
                    if i % HEADS == 4 and i > HEADS:
                        turn_out(i // HEADS - 1)

            pe.wait_ge(pool_const, 11)
            turn_rows(0)
            pe.wait_ge(n_ev, MT)
            kv_keys(KV0)
            turn_rows(1)
            for c in range(MT):
                kv_values(KV0, c)
            pe.wait_ge(rows_lo, 2)
            pe.wait_ge(last_rows_lo, 2)
            recurrence()
            q_memory(QMA)
            memory_attention(0)
            output(0)
            turn_rows(2, 0)
            routing(0)
            experts_pe(0)
            relative_bias()
            pe.wait_ge(b_ev, HEADS)
            overflow(0)
            turn_rows(3)
            pe.wait_ge(rows_lo, 4)
            pe.wait_ge(last_rows_lo, 4)
            diff_attention(project_b())
            memory_attention(1)
            output(1)
            turn_rows(4, 1)
            routing(1)
            experts_pe(1)
            overflow(1)


def reversed_buckets(np):
    n = np.maximum(255 - np.arange(REVLEN), 0)
    large = 16 + (np.log(np.maximum(n, 1) / 16) / math.log(8) * 16 + 1e-9).astype(np.int64)
    bucket = np.where(n < 16, n, np.minimum(large, REL - 1))
    hot = np.zeros((REL, REVLEN), np.float32)
    hot[bucket, np.arange(REVLEN)] = 1.0
    return hot


def kernel(**inputs):
    import numpy as np
    import concourse.bacc as bacc
    from concourse.bass_utils import run_bass_kernel_spmd as run

    a = {k: np.asarray(w) for k, w in inputs.items()}

    def by_partition(w):
        return w.reshape(w.shape[0] // P, P, -1).transpose(1, 0, 2).reshape(P, -1)

    units = np.zeros((UNITS, P, UNIT), np.float32)

    def put(n, block):
        units[n, :block.shape[0], :block.shape[1]] = block

    for L, n in ((0, KV0), (1, KV1)):
        for j in range(2):
            put(n + j, by_partition(a["w_mem_kv"][L][:, j * 256:(j + 1) * 256]))
    wa, wb = a["w_in_a"][0], a["w_in_b"][0]
    tok = RB * RW
    for c in range(RB):
        block = units[INA + c].reshape(P, KC, 2, P)
        for j in range(2):
            block[:, :, j, :RW] = by_partition(wa[:, j * tok + c * RW:j * tok + (c + 1) * RW]).reshape(P, KC, RW)
    put(QMA, by_partition(wa[:, 2 * tok:2 * tok + 256]))
    for c in range(3):
        for o in range(2):
            put(INB + 2 * c + o, by_partition(wb[:, o * tok + c * 256:o * tok + (c + 1) * 256]))
        put(INB + 6 + c, by_partition(wb[:, 2 * tok + c * 256:2 * tok + (c + 1) * 256]))
    put(QMB, by_partition(wb[:, 3 * tok:3 * tok + 256]))
    oa, ob = a["w_out"]
    for c in range(4):
        put(OUTA + c, by_partition(oa[c * 256:(c + 1) * 256]))
        put(OUTB + c, by_partition(ob[c * 256:(c + 1) * 256]))

    experts = np.empty((2, NE, P, EXPW), np.float32)
    up = np.concatenate([a["w_exp1"], a["w_exp3"]], axis=3).reshape(2, NE, KC, P, 2 * DE)
    experts[..., :UPW] = up.transpose(0, 1, 3, 2, 4).reshape(2, NE, P, UPW)
    experts[..., UPW:] = a["w_exp2"].reshape(2, NE, 2, P, D).transpose(0, 1, 3, 2, 4).reshape(2, NE, P, 2 * D)

    vecs = np.zeros((P, NVEC), np.float32)

    def vec(name, block):
        lo, hi = VEC[name]
        vecs[:block.shape[0], lo:hi] = block

    for name, g in (("mix0", a["norm_mix_g"][0]), ("mix1", a["norm_mix_g"][1]), ("ffn0", a["norm_ffn_g"][0]),
                    ("ffn1", a["norm_ffn_g"][1]), ("mem", a["mem_norm_g"])):
        vec(name, g.reshape(KC, P).T)
    vec("subln", a["diff_subln_g"][0].reshape(P, 1))
    vec("conv_w", a["conv_w"][0].reshape(CONV, RB, RW).transpose(2, 1, 0).reshape(RW, RB * CONV))
    for name, key in (("conv_b", "conv_b"), ("gate_a_b", "gate_a_b"), ("gate_x_b", "gate_x_b"), ("lam", "lru_lambda")):
        vec(name, a[key][0].reshape(RB, RW).T)

    router = np.concatenate([a["w_group"], a["w_router"]], axis=2).reshape(2, KC, P, NG + NE).transpose(2, 0, 1, 3).reshape(P, -1)
    gate_w = np.stack([a["gate_a_w"][0], a["gate_x_w"][0]]).transpose(2, 0, 1, 3).reshape(RW, 2 * RB * RW)
    diff_l = np.concatenate([a[k][0] for k in ("diff_lq1", "diff_lk1", "diff_lq2", "diff_lk2")]).reshape(1, -1)

    arrays = {
        "x": a["x"][0], "mem": a["mem"][0], "units": units, "experts": experts, "gate_w": gate_w, "vecs": vecs,
        "router": router, "diff_l": diff_l, "rel_bias": a["rel_bias"], "final_g": a["final_norm_g"].reshape(1, D),
        "onehot": reversed_buckets(np),
    }
    arrays = {f"in_{k}": np.ascontiguousarray(w) for k, w in arrays.items()}
    nc = bacc.Bacc("TRN2", target_bir_lowering=False, num_devices=1)
    args = [nc.dram_tensor(k, w.shape, mybir.dt.from_np(w.dtype), kind="ExternalInput").ap() for k, w in arrays.items()]
    args.append(nc.dram_tensor("out_0", (T, D), F32, kind="ExternalOutput").ap())
    build(nc, *args)
    r = run(nc, [arrays], core_ids=[0])
    return r.results[0]["out_0"].reshape(1, T, D)
```
